# Optimizing a Trainium2 kernel written in Bass

```python
import jax, jax.numpy as jnp
from jax import lax
import numpy as np
import math

D_MODEL = 2048
BATCH = 1
SEQ = 256
DEPTH = 2

EXPAND = 2
D_INNER = EXPAND * D_MODEL
CONV_K = 4
EPS = 1e-6
LRU_WIDTH = D_INNER // 2
LRU_BLOCKS = 16
LRU_BLOCK = LRU_WIDTH // LRU_BLOCKS
LRU_C = 8.0
MLSTM_WIDTH = D_INNER - LRU_WIDTH
MLSTM_HEADS = 4
MLSTM_DV = MLSTM_WIDTH // MLSTM_HEADS
MLSTM_DQK = MLSTM_DV // 2
MLSTM_CHUNK = 64
MLSTM_GATE_IN = MLSTM_HEADS * (2 * MLSTM_DQK + MLSTM_DV)
EVEN_IN = LRU_WIDTH + MLSTM_WIDTH + D_INNER
SSD_HEADDIM = 64
SSD_HEADS = D_INNER // SSD_HEADDIM
SSD_GROUPS = 8
SSD_HPG = SSD_HEADS // SSD_GROUPS
SSD_STATE = 128
SSD_CHUNK = 128
SSD_CONV_DIM = D_INNER + 2 * SSD_GROUPS * SSD_STATE
SSD_IN = D_INNER + SSD_CONV_DIM + SSD_HEADS
N_EVEN = (DEPTH + 1) // 2
N_ODD = DEPTH // 2


def rmsnorm(x, w):
    xf = x.astype(jnp.float32)
    y = xf * lax.rsqrt(jnp.mean(xf * xf, axis=-1, keepdims=True) + EPS)
    return (y * w.astype(jnp.float32)).astype(x.dtype)

def causal_conv(x, w, b):
    s = x.shape[1]
    xp = jnp.pad(x, ((0, 0), (CONV_K - 1, 0), (0, 0)))
    y = b + w[0] * xp[:, 0:s]
    for tap in range(1, CONV_K):
        y = y + w[tap] * xp[:, tap:tap + s]
    return y

def rglru(x, w_a, b_a, w_x, b_x, lam):
    bn, s, _ = x.shape
    xb = x.reshape(bn, s, LRU_BLOCKS, LRU_BLOCK)
    r = jax.nn.sigmoid((jnp.einsum('bsni,nij->bsnj', xb, w_a).reshape(bn, s, LRU_WIDTH) + b_a).astype(jnp.float32))
    i = jax.nn.sigmoid((jnp.einsum('bsni,nij->bsnj', xb, w_x).reshape(bn, s, LRU_WIDTH) + b_x).astype(jnp.float32))
    log_a = -LRU_C * r * jax.nn.softplus(-lam.astype(jnp.float32))
    a = jnp.exp(log_a)
    u = jnp.sqrt(-jnp.expm1(2.0 * log_a)) * (i * x.astype(jnp.float32))

    def combine(left, right):
        a1, b1 = left
        a2, b2 = right
        return a1 * a2, a2 * b1 + b2

    _, h = lax.associative_scan(combine, (a, u), axis=1)
    return h

def mlstm_chunkwise(q, k, v, ig, lf):
    bn, nh, s, _ = q.shape
    nc = s // MLSTM_CHUNK

    def chunks(t):
        return jnp.moveaxis(t.reshape(bn, nh, nc, MLSTM_CHUNK, *t.shape[3:]), 2, 0)

    causal = jnp.tril(jnp.ones((MLSTM_CHUNK, MLSTM_CHUNK), dtype=bool))

    def step(carry, inp):
        c_mat, n_vec, m = carry
        qc, kc, vc, ic, fc = inp
        g = jnp.cumsum(fc, axis=-1)
        dmat = jnp.where(causal, g[..., :, None] - g[..., None, :] + ic[..., None, :], -jnp.inf)
        m_inter = g + m[..., None]
        m_j = jnp.maximum(m_inter, jnp.max(dmat, axis=-1))
        sc = jnp.einsum('bhld,bhsd->bhls', qc, kc) * jnp.exp(dmat - m_j[..., None])
        inter = jnp.exp(m_inter - m_j)
        num = jnp.einsum('bhls,bhsv->bhlv', sc, vc) + inter[..., None] * jnp.einsum('bhvd,bhld->bhlv', c_mat, qc)
        den = jnp.sum(sc, axis=-1) + inter * jnp.einsum('bhd,bhld->bhl', n_vec, qc)
        h = num / jnp.maximum(jnp.abs(den), jnp.exp(-m_j))[..., None]
        g_tot = g[..., -1]
        w = g_tot[..., None] - g + ic
        m_new = jnp.maximum(g_tot + m, jnp.max(w, axis=-1))
        decay = jnp.exp(g_tot + m - m_new)
        ws = jnp.exp(w - m_new[..., None])
        c_mat = decay[..., None, None] * c_mat + jnp.einsum('bhs,bhsv,bhsd->bhvd', ws, vc, kc)
        n_vec = decay[..., None] * n_vec + jnp.einsum('bhs,bhsd->bhd', ws, kc)
        return (c_mat, n_vec, m_new), h

    init = (jnp.zeros((bn, nh, MLSTM_DV, MLSTM_DQK), jnp.float32),
            jnp.zeros((bn, nh, MLSTM_DQK), jnp.float32),
            jnp.zeros((bn, nh), jnp.float32))
    _, hs = lax.scan(step, init, (chunks(q), chunks(k), chunks(v), chunks(ig), chunks(lf)))
    return jnp.moveaxis(hs, 0, 2).reshape(bn, nh, s, MLSTM_DV)

def lru_mlstm_layer(x, w_in, conv_l_w, conv_l_b, lru_wa, lru_ba, lru_wx, lru_bx, lru_lam,
                    conv_m_w, conv_m_b, w_q, w_k, w_v, w_o, w_if, b_if, m_norm, w_out):
    bn, s, _ = x.shape
    u = x @ w_in
    x_l, x_m, z = jnp.split(u, [LRU_WIDTH, LRU_WIDTH + MLSTM_WIDTH], axis=-1)
    y_l = rglru(causal_conv(x_l, conv_l_w, conv_l_b), lru_wa, lru_ba, lru_wx, lru_bx, lru_lam)
    x_mc = jax.nn.silu(causal_conv(x_m, conv_m_w, conv_m_b))
    xm_h = x_m.reshape(bn, s, MLSTM_HEADS, MLSTM_DV)
    xmc_h = x_mc.reshape(bn, s, MLSTM_HEADS, MLSTM_DV)
    q = jnp.einsum('bshi,hij->bshj', xmc_h, w_q)
    k = jnp.einsum('bshi,hij->bshj', xmc_h, w_k) * (MLSTM_DQK ** -0.5)
    v = jnp.einsum('bshi,hij->bshj', xm_h, w_v)
    o = jax.nn.sigmoid(jnp.einsum('bshi,hij->bshj', xm_h, w_o).astype(jnp.float32))
    gin = jnp.concatenate([q.reshape(bn, s, -1), k.reshape(bn, s, -1), v.reshape(bn, s, -1)], axis=-1)
    gates = (gin @ w_if + b_if).astype(jnp.float32)
    ig = jnp.transpose(gates[..., :MLSTM_HEADS], (0, 2, 1))
    lf = jnp.transpose(jax.nn.log_sigmoid(gates[..., MLSTM_HEADS:]), (0, 2, 1))
    to_bhs = lambda t: jnp.transpose(t, (0, 2, 1, 3)).astype(jnp.float32)
    h = mlstm_chunkwise(to_bhs(q), to_bhs(k), to_bhs(v), ig, lf)
    h = rmsnorm(jnp.transpose(h, (0, 2, 1, 3)), m_norm)
    y_m = (o * h).reshape(bn, s, MLSTM_WIDTH)
    y = jnp.concatenate([y_l, y_m], axis=-1).astype(x.dtype) * jax.nn.silu(z)
    return y @ w_out

def ssd_scan(xh, dt, a, bm, cm):
    bn, s = xh.shape[:2]
    nc = s // SSD_CHUNK
    ch = lambda t: t.reshape(bn, nc, SSD_CHUNK, *t.shape[2:])
    xdt = ch(xh * dt[..., None])
    da_cs = jnp.cumsum(ch(dt * a), axis=2)
    bm, cm = ch(bm), ch(cm)
    causal = jnp.tril(jnp.ones((SSD_CHUNK, SSD_CHUNK), dtype=bool))
    da_t = jnp.moveaxis(da_cs, 2, -1)
    decay = jnp.exp(jnp.where(causal, da_t[..., :, None] - da_t[..., None, :], -jnp.inf))
    cb = jnp.einsum('bclgn,bcsgn->bcgls', cm, bm)
    y_diag = jnp.einsum('bcgls,bcgels,bcsgep->bclgep', cb, decay, xdt)
    decay_states = jnp.exp(da_cs[:, :, -1:] - da_cs)
    states = jnp.einsum('bclgn,bclge,bclgep->bcgepn', bm, decay_states, xdt)
    chunk_decay = jnp.exp(da_cs[:, :, -1])

    def step(st, inp):
        new_st, dc = inp
        return dc[..., None, None] * st + new_st, st

    init = jnp.zeros((bn, SSD_GROUPS, SSD_HPG, SSD_HEADDIM, SSD_STATE), jnp.float32)
    _, s_in = lax.scan(step, init, (jnp.moveaxis(states, 1, 0), jnp.moveaxis(chunk_decay, 1, 0)))
    s_in = jnp.moveaxis(s_in, 0, 1)
    y_off = jnp.einsum('bclgn,bcgepn,bclge->bclgep', cm, s_in, jnp.exp(da_cs))
    return (y_diag + y_off).reshape(bn, s, SSD_GROUPS, SSD_HPG, SSD_HEADDIM)

def ssd_layer(x, w_in, conv_w, conv_b, dt_bias, a_log, d_skip, gnorm, w_out):
    bn, s, _ = x.shape
    u = x @ w_in
    z, xbc, dt = jnp.split(u, [D_INNER, D_INNER + SSD_CONV_DIM], axis=-1)
    xbc = jax.nn.silu(causal_conv(xbc, conv_w, conv_b))
    xs, bm, cm = jnp.split(xbc, [D_INNER, D_INNER + SSD_GROUPS * SSD_STATE], axis=-1)
    dt = jax.nn.softplus(dt.astype(jnp.float32) + dt_bias.astype(jnp.float32))
    a = -jnp.exp(a_log.astype(jnp.float32)).reshape(SSD_GROUPS, SSD_HPG)
    xh = xs.astype(jnp.float32).reshape(bn, s, SSD_GROUPS, SSD_HPG, SSD_HEADDIM)
    y = ssd_scan(xh, dt.reshape(bn, s, SSD_GROUPS, SSD_HPG), a,
                 bm.astype(jnp.float32).reshape(bn, s, SSD_GROUPS, SSD_STATE),
                 cm.astype(jnp.float32).reshape(bn, s, SSD_GROUPS, SSD_STATE))
    y = y + d_skip.astype(jnp.float32).reshape(SSD_GROUPS, SSD_HPG, 1) * xh
    y = y.reshape(bn, s, D_INNER).astype(x.dtype) * jax.nn.silu(z)
    y = rmsnorm(y.reshape(bn, s, SSD_GROUPS, D_INNER // SSD_GROUPS),
                gnorm.reshape(SSD_GROUPS, D_INNER // SSD_GROUPS)).reshape(bn, s, D_INNER)
    return y @ w_out

def first_inputs(seed: int = 0) -> dict:
    key = jax.random.key(seed)
    ks = iter(jax.random.split(key, 40))
    nrm = lambda shape, scale: jax.random.normal(next(ks), shape, jnp.float32) * scale
    uni = lambda shape, lo, hi: jax.random.uniform(next(ks), shape, jnp.float32, lo, hi)
    ne, no, h = N_EVEN, N_ODD, MLSTM_HEADS
    x = jax.random.normal(next(ks), (BATCH, SEQ, D_MODEL), jnp.float32)
    a0 = uni((ne, LRU_WIDTH), 0.9, 0.999) ** (1.0 / LRU_C)
    dt0 = jnp.exp(uni((no, SSD_HEADS), float(np.log(1e-3)), float(np.log(1e-1))))
    return {
        "x": x,
        "e_norm": 1.0 + nrm((ne, D_MODEL), 0.05),
        "e_w_in": nrm((ne, D_MODEL, EVEN_IN), D_MODEL ** -0.5),
        "e_conv_l_w": nrm((ne, CONV_K, LRU_WIDTH), 0.5),
        "e_conv_l_b": nrm((ne, LRU_WIDTH), 0.02),
        "e_lru_wa": nrm((ne, LRU_BLOCKS, LRU_BLOCK, LRU_BLOCK), LRU_BLOCK ** -0.5),
        "e_lru_ba": nrm((ne, LRU_WIDTH), 0.02),
        "e_lru_wx": nrm((ne, LRU_BLOCKS, LRU_BLOCK, LRU_BLOCK), LRU_BLOCK ** -0.5),
        "e_lru_bx": nrm((ne, LRU_WIDTH), 0.02),
        "e_lru_lam": jnp.log(a0) - jnp.log1p(-a0),
        "e_conv_m_w": nrm((ne, CONV_K, MLSTM_WIDTH), 0.5),
        "e_conv_m_b": nrm((ne, MLSTM_WIDTH), 0.02),
        "e_w_q": nrm((ne, h, MLSTM_DV, MLSTM_DQK), MLSTM_DV ** -0.5),
        "e_w_k": nrm((ne, h, MLSTM_DV, MLSTM_DQK), MLSTM_DV ** -0.5),
        "e_w_v": nrm((ne, h, MLSTM_DV, MLSTM_DV), MLSTM_DV ** -0.5),
        "e_w_o": nrm((ne, h, MLSTM_DV, MLSTM_DV), MLSTM_DV ** -0.5),
        "e_w_if": nrm((ne, MLSTM_GATE_IN, 2 * h), MLSTM_GATE_IN ** -0.5),
        "e_b_if": jnp.concatenate([nrm((ne, h), 0.1), uni((ne, h), 3.0, 6.0)], axis=-1),
        "e_m_norm": 1.0 + nrm((ne, h, MLSTM_DV), 0.05),
        "e_w_out": nrm((ne, D_INNER, D_MODEL), D_INNER ** -0.5),
        "o_norm": 1.0 + nrm((no, D_MODEL), 0.05),
        "o_w_in": nrm((no, D_MODEL, SSD_IN), D_MODEL ** -0.5),
        "o_conv_w": nrm((no, CONV_K, SSD_CONV_DIM), 0.5),
        "o_conv_b": nrm((no, SSD_CONV_DIM), 0.02),
        "o_dt_bias": dt0 + jnp.log(-jnp.expm1(-dt0)),
        "o_a_log": jnp.log(uni((no, SSD_HEADS), 1.0, 16.0)),
        "o_d_skip": 1.0 + nrm((no, SSD_HEADS), 0.1),
        "o_gnorm": 1.0 + nrm((no, D_INNER), 0.05),
        "o_w_out": nrm((no, D_INNER, D_MODEL), D_INNER ** -0.5),
        "final_norm": 1.0 + nrm((D_MODEL,), 0.05),
    }

def first_block(x, e_norm, e_w_in, e_conv_l_w, e_conv_l_b, e_lru_wa, e_lru_ba, e_lru_wx, e_lru_bx,
              e_lru_lam, e_conv_m_w, e_conv_m_b, e_w_q, e_w_k, e_w_v, e_w_o, e_w_if, e_b_if,
              e_m_norm, e_w_out, o_norm, o_w_in, o_conv_w, o_conv_b, o_dt_bias, o_a_log,
              o_d_skip, o_gnorm, o_w_out, final_norm):
    for layer in range(DEPTH):
        j = layer // 2
        if layer % 2 == 0:
            x = x + lru_mlstm_layer(
                rmsnorm(x, e_norm[j]), e_w_in[j], e_conv_l_w[j], e_conv_l_b[j], e_lru_wa[j],
                e_lru_ba[j], e_lru_wx[j], e_lru_bx[j], e_lru_lam[j], e_conv_m_w[j], e_conv_m_b[j],
                e_w_q[j], e_w_k[j], e_w_v[j], e_w_o[j], e_w_if[j], e_b_if[j], e_m_norm[j],
                e_w_out[j]).astype(x.dtype)
        else:
            x = x + ssd_layer(
                rmsnorm(x, o_norm[j]), o_w_in[j], o_conv_w[j], o_conv_b[j], o_dt_bias[j],
                o_a_log[j], o_d_skip[j], o_gnorm[j], o_w_out[j]).astype(x.dtype)
    return rmsnorm(x, final_norm)


DEPTH_2 = 1

D_SSM = 1024
SSM_GROUP = 16
N_SSM_GROUPS = D_SSM // SSM_GROUP
SSM_STATE = 64
SSM_DT_MIN = 1e-3
SSM_DT_MAX = 1e-1
GLA_HEADS = 4
GLA_DK = 128
GLA_DV = 256
GLA_GATE_RANK = 16
GLA_GATE_NORM = 16.0
GLA_CHUNK = 32
DIFF_HEADS = 4
DIFF_DK = 128
DIFF_DV = 256
Q_BLOCK = 128
N_BRANCH = 3
D_FF = 5504
CONV_W = 3
IN_SPLITS = (D_SSM, GLA_HEADS * GLA_DK, GLA_HEADS * GLA_DK, GLA_HEADS * GLA_DV, GLA_HEADS * GLA_DV, GLA_GATE_RANK, DIFF_HEADS * 2 * DIFF_DK, DIFF_HEADS * 2 * DIFF_DK, DIFF_HEADS * DIFF_DV, N_BRANCH * D_MODEL)
D_IN = sum(IN_SPLITS)
ALIBI_SLOPES = tuple(2.0 ** (-8.0 * (h + 1) / DIFF_HEADS) for h in range(DIFF_HEADS))


def _rms_f32(x, w):
    xf = x.astype(jnp.float32)
    return xf * lax.rsqrt(jnp.mean(xf * xf, axis=-1, keepdims=True) + EPS) * w.astype(jnp.float32)

def rmsnorm_2(x, w):
    return _rms_f32(x, w).astype(x.dtype)

def _split_points():
    return tuple(int(c) for c in np.cumsum(IN_SPLITS)[:-1])

def _complex_affine_combine(e1, e2):
    a1r, a1i, b1r, b1i = e1
    a2r, a2i, b2r, b2i = e2
    return (a2r * a1r - a2i * a1i,
            a2r * a1i + a2i * a1r,
            a2r * b1r - a2i * b1i + b2r,
            a2r * b1i + a2i * b1r + b2i)

def s5_branch(u, a_re, a_im, log_dt, b_re, b_im, c_re, c_im, d_skip, w_glu):
    f32 = jnp.float32
    bsz, seq, _ = u.shape
    ug = u.astype(f32).reshape(bsz, seq, N_SSM_GROUPS, SSM_GROUP)
    lam_r = jnp.minimum(a_re.astype(f32), -1e-4)
    lam_i = a_im.astype(f32)
    dt = jnp.exp(log_dt.astype(f32))[:, None]
    mag = jnp.exp(dt * lam_r)
    ab_r = mag * jnp.cos(dt * lam_i)
    ab_i = mag * jnp.sin(dt * lam_i)
    den = lam_r * lam_r + lam_i * lam_i
    f_r = ((ab_r - 1.0) * lam_r + ab_i * lam_i) / den
    f_i = (ab_i * lam_r - (ab_r - 1.0) * lam_i) / den
    br = b_re.astype(f32)
    bi = b_im.astype(f32)
    bb_r = f_r[..., None] * br - f_i[..., None] * bi
    bb_i = f_r[..., None] * bi + f_i[..., None] * br
    x_r = jnp.einsum('bsgc,gpc->bsgp', ug, bb_r)
    x_i = jnp.einsum('bsgc,gpc->bsgp', ug, bb_i)
    shape_a = (1, seq, N_SSM_GROUPS, SSM_STATE)
    a_seq_r = jnp.broadcast_to(ab_r, shape_a)
    a_seq_i = jnp.broadcast_to(ab_i, shape_a)
    _, _, h_r, h_i = lax.associative_scan(_complex_affine_combine, (a_seq_r, a_seq_i, x_r, x_i), axis=1)
    y = (jnp.einsum('bsgp,gcp->bsgc', h_r, c_re.astype(f32))
         - jnp.einsum('bsgp,gcp->bsgc', h_i, c_im.astype(f32)))
    y = y + d_skip.astype(f32).reshape(N_SSM_GROUPS, SSM_GROUP) * ug
    z = jax.nn.gelu(y.reshape(bsz, seq, D_SSM)).astype(u.dtype) @ w_glu
    val, gate = jnp.split(z, 2, axis=-1)
    return (val * jax.nn.sigmoid(gate)).astype(u.dtype)

def gla_branch(q, k, v, r, gate_lr, w_gate, b_gate, norm_w, w_br):
    f32 = jnp.float32
    bsz, seq, _ = q.shape
    n = seq // GLA_CHUNK
    cshape_k = (bsz, n, GLA_CHUNK, GLA_HEADS, GLA_DK)
    qf = q.astype(f32).reshape(cshape_k) * (GLA_DK ** -0.5)
    kf = k.astype(f32).reshape(cshape_k)
    vf = v.astype(f32).reshape(bsz, n, GLA_CHUNK, GLA_HEADS, GLA_DV)
    log_a = jax.nn.log_sigmoid(gate_lr.astype(f32) @ w_gate.astype(f32) + b_gate.astype(f32)) / GLA_GATE_NORM
    cum = jnp.cumsum(log_a.reshape(cshape_k), axis=2)
    last = cum[:, :, -1:]
    q_dec = qf * jnp.exp(cum)
    k_inv = kf * jnp.exp(-cum)
    k_tail = kf * jnp.exp(last - cum)
    tri = jnp.tril(jnp.ones((GLA_CHUNK, GLA_CHUNK), dtype=bool))
    scores = jnp.where(tri, jnp.einsum('bnchd,bnshd->bnhcs', q_dec, k_inv), 0.0)
    o_intra = jnp.einsum('bnhcs,bnshv->bnchv', scores, vf)

    def step(state, inp):
        qd, kt, vv, dl = inp
        o = jnp.einsum('bchd,bhdv->bchv', qd, state)
        state = dl[..., None] * state + jnp.einsum('bchd,bchv->bhdv', kt, vv)
        return state, o

    xs = (jnp.moveaxis(q_dec, 1, 0), jnp.moveaxis(k_tail, 1, 0), jnp.moveaxis(vf, 1, 0),
          jnp.moveaxis(jnp.exp(last[:, :, 0]), 1, 0))
    init = jnp.zeros((bsz, GLA_HEADS, GLA_DK, GLA_DV), f32)
    _, o_inter = lax.scan(step, init, xs)
    o = (o_intra + jnp.moveaxis(o_inter, 0, 1)).reshape(bsz, seq, GLA_HEADS, GLA_DV)
    o = _rms_f32(o, norm_w).reshape(bsz, seq, GLA_HEADS * GLA_DV) * jax.nn.silu(r.astype(f32))
    return o.astype(q.dtype) @ w_br

def diff_attn_branch(q, k, v, lam_q1, lam_k1, lam_q2, lam_k2, norm_w, w_br, lambda_init):
    f32 = jnp.float32
    bsz, seq, _ = q.shape
    q = q.reshape(bsz, seq, DIFF_HEADS, 2, DIFF_DK)
    k = k.reshape(bsz, seq, DIFF_HEADS, 2, DIFF_DK)
    v = v.reshape(bsz, seq, DIFF_HEADS, DIFF_DV)
    lam = (jnp.exp(jnp.sum(lam_q1.astype(f32) * lam_k1.astype(f32)))
           - jnp.exp(jnp.sum(lam_q2.astype(f32) * lam_k2.astype(f32))) + lambda_init)
    slopes = jnp.array(ALIBI_SLOPES, dtype=f32)[None, :, None, None, None]
    scale = DIFF_DK ** -0.5
    pos = jnp.arange(seq, dtype=jnp.int32)
    outs = []
    for blk in range(seq // Q_BLOCK):
        start = blk * Q_BLOCK
        end = start + Q_BLOCK
        qb = q[:, start:end]
        kb = k[:, :end]
        vb = v[:, :end]
        s = jnp.einsum('bqhmd,bkhmd->bhmqk', qb, kb).astype(f32) * scale
        rel = (pos[start:end, None] - pos[None, :end]).astype(f32)
        s = s - slopes * rel
        s = jnp.where(rel >= 0.0, s, -jnp.inf)
        p = jax.nn.softmax(s, axis=-1)
        w = p[:, :, 0] - lam * p[:, :, 1]
        outs.append(jnp.einsum('bhqk,bkhv->bqhv', w.astype(v.dtype), vb))
    o = jnp.concatenate(outs, axis=1)
    o = _rms_f32(o, norm_w) * (1.0 - lambda_init)
    return o.reshape(bsz, seq, DIFF_HEADS * DIFF_DV).astype(q.dtype) @ w_br

def conv_gated_mlp(h, w_up, conv_w, conv_b, w_down):
    seq = h.shape[1]
    u = h @ w_up
    pad = jnp.pad(u, ((0, 0), (CONV_W - 1, 0), (0, 0)))
    acc = conv_b
    for i in range(CONV_W):
        acc = acc + pad[:, i:i + seq] * conv_w[i]
    val, gate = jnp.split(acc, 2, axis=-1)
    return (jax.nn.silu(gate) * val) @ w_down

def second_inputs(seed: int = 0) -> dict:
    key = jax.random.key(seed)
    ks = jax.random.split(key, 32)
    f32 = jnp.float32
    L = DEPTH_2
    G = N_SSM_GROUPS
    P = SSM_STATE

    def nrm(k, shape, scale):
        return jax.random.normal(k, shape, f32) * scale

    def gain(k, n):
        return 1.0 + nrm(k, (L, n), 0.02)

    return {
        'x': nrm(ks[0], (BATCH, SEQ, D_MODEL), 1.0),
        'norm_mix_w': gain(ks[1], D_MODEL),
        'w_in': nrm(ks[2], (L, D_MODEL, D_IN), D_MODEL ** -0.5),
        'ssm_a_re': -0.5 + nrm(ks[3], (L, G, P), 0.01),
        'ssm_a_im': jnp.pi * jnp.arange(P, dtype=f32) + nrm(ks[4], (L, G, P), 0.01),
        'ssm_log_dt': jax.random.uniform(ks[5], (L, G), f32, math.log(SSM_DT_MIN), math.log(SSM_DT_MAX)),
        'ssm_b_re': nrm(ks[6], (L, G, P, SSM_GROUP), (2 * SSM_GROUP) ** -0.5),
        'ssm_b_im': nrm(ks[7], (L, G, P, SSM_GROUP), (2 * SSM_GROUP) ** -0.5),
        'ssm_c_re': nrm(ks[8], (L, G, SSM_GROUP, P), (2 * P) ** -0.5),
        'ssm_c_im': nrm(ks[9], (L, G, SSM_GROUP, P), (2 * P) ** -0.5),
        'ssm_d': nrm(ks[10], (L, D_SSM), 1.0),
        'ssm_w_glu': nrm(ks[11], (L, D_SSM, 2 * D_MODEL), D_SSM ** -0.5),
        'gla_w_gate': nrm(ks[12], (L, GLA_GATE_RANK, GLA_HEADS * GLA_DK), GLA_GATE_RANK ** -0.5),
        'gla_b_gate': nrm(ks[13], (L, GLA_HEADS * GLA_DK), 0.1),
        'gla_norm_w': gain(ks[14], GLA_DV),
        'gla_w_br': nrm(ks[15], (L, GLA_HEADS * GLA_DV, D_MODEL), (GLA_HEADS * GLA_DV) ** -0.5),
        'diff_lam_q1': nrm(ks[16], (L, DIFF_DK), 0.1),
        'diff_lam_k1': nrm(ks[17], (L, DIFF_DK), 0.1),
        'diff_lam_q2': nrm(ks[18], (L, DIFF_DK), 0.1),
        'diff_lam_k2': nrm(ks[19], (L, DIFF_DK), 0.1),
        'diff_norm_w': gain(ks[20], DIFF_DV),
        'diff_w_br': nrm(ks[21], (L, DIFF_HEADS * DIFF_DV, D_MODEL), (DIFF_HEADS * DIFF_DV) ** -0.5),
        'w_out': nrm(ks[22], (L, D_MODEL, D_MODEL), D_MODEL ** -0.5),
        'norm_ffn_w': gain(ks[23], D_MODEL),
        'ffn_w_up': nrm(ks[24], (L, D_MODEL, 2 * D_FF), D_MODEL ** -0.5),
        'ffn_conv_w': nrm(ks[25], (L, CONV_W, 2 * D_FF), 0.5),
        'ffn_conv_b': nrm(ks[26], (L, 2 * D_FF), 0.01),
        'ffn_w_down': nrm(ks[27], (L, D_FF, D_MODEL), D_FF ** -0.5),
        'norm_final_w': 1.0 + nrm(ks[28], (D_MODEL,), 0.02),
    }

def second_block(x, norm_mix_w, w_in, ssm_a_re, ssm_a_im, ssm_log_dt, ssm_b_re, ssm_b_im, ssm_c_re, ssm_c_im,
              ssm_d, ssm_w_glu, gla_w_gate, gla_b_gate, gla_norm_w, gla_w_br, diff_lam_q1, diff_lam_k1,
              diff_lam_q2, diff_lam_k2, diff_norm_w, diff_w_br, w_out, norm_ffn_w, ffn_w_up, ffn_conv_w,
              ffn_conv_b, ffn_w_down, norm_final_w):
    bsz, seq, _ = x.shape
    split_points = _split_points()
    h = x
    for l in range(DEPTH_2):
        lambda_init = 0.8 - 0.6 * math.exp(-0.3 * l)
        hn = rmsnorm_2(h, norm_mix_w[l])
        proj = hn @ w_in[l]
        (u_ssm, q_gla, k_gla, v_gla, r_gla, a_lr,
         q_diff, k_diff, v_diff, gates) = jnp.split(proj, split_points, axis=-1)
        y_a = s5_branch(u_ssm, ssm_a_re[l], ssm_a_im[l], ssm_log_dt[l], ssm_b_re[l], ssm_b_im[l],
                        ssm_c_re[l], ssm_c_im[l], ssm_d[l], ssm_w_glu[l])
        y_b = gla_branch(q_gla, k_gla, v_gla, r_gla, a_lr, gla_w_gate[l], gla_b_gate[l],
                         gla_norm_w[l], gla_w_br[l])
        y_c = diff_attn_branch(q_diff, k_diff, v_diff, diff_lam_q1[l], diff_lam_k1[l], diff_lam_q2[l],
                               diff_lam_k2[l], diff_norm_w[l], diff_w_br[l], lambda_init)
        g = jax.nn.sigmoid(gates.astype(jnp.float32)).reshape(bsz, seq, N_BRANCH, D_MODEL)
        merged = (g[:, :, 0] * y_a.astype(jnp.float32) + g[:, :, 1] * y_b.astype(jnp.float32)
                  + g[:, :, 2] * y_c.astype(jnp.float32))
        h = h + merged.astype(h.dtype) @ w_out[l]
        h = h + conv_gated_mlp(rmsnorm_2(h, norm_ffn_w[l]), ffn_w_up[l], ffn_conv_w[l],
                               ffn_conv_b[l], ffn_w_down[l])
    return rmsnorm_2(h, norm_final_w)


_first_inputs = second_inputs


def second_inputs(seed=0):
    import zlib

    import numpy as np

    out = dict(_first_inputs(seed))
    spreads = {}
    factors = {'norm_mix_w': 2.915,
     'ssm_a_re': 64.0,
     'ssm_a_im': 41.288,
     'ssm_log_dt': 42.768,
     'ssm_b_re': 57.584,
     'ssm_b_im': 58.56,
     'ssm_c_re': 57.928,
     'ssm_c_im': 57.912,
     'gla_b_gate': 4.475,
     'gla_norm_w': 8.0,
     'diff_lam_k2': 8.0,
     'diff_norm_w': 46.738,
     'norm_ffn_w': 5.6,
     'ffn_conv_b': 22.827,
     'norm_final_w': 7.457}
    for name, (base, spread) in spreads.items():
        noise = np.random.default_rng([zlib.crc32(name.encode()), seed]).standard_normal(out[name].shape)
        drawn = base * np.exp(spread * noise) if base else spread * noise
        out[name] = __import__('jax').numpy.asarray(drawn.astype(out[name].dtype))
    for name, factor in factors.items():
        out[name] = (out[name] * factor).astype(out[name].dtype)
    return out


_narrow_inputs = second_inputs


def second_inputs(seed=0):
    out = dict(_narrow_inputs(seed))
    wider = {'gla_norm_w': 7.31, 'diff_norm_w': 3.13, 'norm_ffn_w': 4.2, 'norm_final_w': 3.07}
    for name, times in wider.items():
        mean = out[name].mean()
        out[name] = (mean + times * (out[name] - mean)).astype(out[name].dtype)
    return out


def setup_inputs(seed=0):
    out = dict(first_inputs(seed))
    for name, value in second_inputs(seed + 1).items():
        if name != "x":
            out[name + "_2"] = value
    return out


def reference(
    x, e_norm, e_w_in, e_conv_l_w, e_conv_l_b, e_lru_wa, e_lru_ba, e_lru_wx, e_lru_bx,
    e_lru_lam, e_conv_m_w, e_conv_m_b, e_w_q, e_w_k, e_w_v, e_w_o, e_w_if, e_b_if, e_m_norm,
    e_w_out, o_norm, o_w_in, o_conv_w, o_conv_b, o_dt_bias, o_a_log, o_d_skip, o_gnorm, o_w_out,
    final_norm, norm_mix_w_2, w_in_2, ssm_a_re_2, ssm_a_im_2, ssm_log_dt_2, ssm_b_re_2,
    ssm_b_im_2, ssm_c_re_2, ssm_c_im_2, ssm_d_2, ssm_w_glu_2, gla_w_gate_2, gla_b_gate_2,
    gla_norm_w_2, gla_w_br_2, diff_lam_q1_2, diff_lam_k1_2, diff_lam_q2_2, diff_lam_k2_2,
    diff_norm_w_2, diff_w_br_2, w_out_2, norm_ffn_w_2, ffn_w_up_2, ffn_conv_w_2, ffn_conv_b_2,
    ffn_w_down_2, norm_final_w_2,
):
    x = first_block(
        x, e_norm, e_w_in, e_conv_l_w, e_conv_l_b, e_lru_wa, e_lru_ba, e_lru_wx, e_lru_bx,
        e_lru_lam, e_conv_m_w, e_conv_m_b, e_w_q, e_w_k, e_w_v, e_w_o, e_w_if, e_b_if, e_m_norm,
        e_w_out, o_norm, o_w_in, o_conv_w, o_conv_b, o_dt_bias, o_a_log, o_d_skip, o_gnorm,
        o_w_out, final_norm,
    )
    return second_block(
        x, norm_mix_w_2, w_in_2, ssm_a_re_2, ssm_a_im_2, ssm_log_dt_2, ssm_b_re_2, ssm_b_im_2,
        ssm_c_re_2, ssm_c_im_2, ssm_d_2, ssm_w_glu_2, gla_w_gate_2, gla_b_gate_2, gla_norm_w_2,
        gla_w_br_2, diff_lam_q1_2, diff_lam_k1_2, diff_lam_q2_2, diff_lam_k2_2, diff_norm_w_2,
        diff_w_br_2, w_out_2, norm_ffn_w_2, ffn_w_up_2, ffn_conv_w_2, ffn_conv_b_2,
        ffn_w_down_2, norm_final_w_2,
    )


_drawn_inputs = setup_inputs


def setup_inputs(seed=0):
    import zlib

    import numpy as np

    out = dict(_drawn_inputs(seed))
    spreads = {}
    factors = {'e_lru_ba': 8.0, 'e_lru_bx': 6.327, 'diff_lam_q1_2': 3.238}
    for name, (base, spread) in spreads.items():
        noise = np.random.default_rng([zlib.crc32(name.encode()), seed]).standard_normal(out[name].shape)
        drawn = base * np.exp(spread * noise) if base else spread * noise
        out[name] = __import__('jax').numpy.asarray(drawn.astype(out[name].dtype))
    for name, factor in factors.items():
        out[name] = (out[name] * factor).astype(out[name].dtype)
    return out
```

```python
from contextlib import ExitStack

import numpy as np

from concourse import mybir

F32 = mybir.dt.float32
F32R = mybir.dt.float32r
ACT = mybir.ActivationFunctionType
ALU = mybir.AluOpType
AX = mybir.AxisListType.X

UB = 8
NRAW = 5
NW = 4
TICK = 16
NEG = -1.0e30
TWO_PI = 6.283185307179586


VEC = [
    ("e_norm", 16), ("conv_l_w", 64), ("conv_l_b", 16), ("lru_ba", 16), ("lru_bx", 16),
    ("lru_lam", 16), ("conv_m_w", 64), ("conv_m_b", 16), ("b_if", 1), ("m_norm", 16),
    ("o_norm", 16), ("o_conv_w", 192), ("o_conv_b", 48), ("dt_bias", 1), ("a_log", 1),
    ("d_skip", 32), ("gnorm", 32), ("final_norm", 16), ("norm_mix", 16), ("a_re", 32),
    ("a_im", 32), ("log_dt", 32), ("ssm_d", 8), ("gla_b", 4), ("gla_norm", 2),
    ("diff_lam", 4), ("diff_norm", 2), ("norm_ffn", 16), ("ffn_w", 258), ("ffn_b", 86),
    ("norm_final", 16),
]
VOFF = {}
_at = 0
for _n, _c in VEC:
    VOFF[_n] = _at
    _at += _c
NVEC = _at
SHP = [("ident", 128), ("ones", 128), ("mask", 384), ("gmask", 128), ("creset", 256), ("cmask", 8)]
SOFF = {}
_at = 0
for _n, _c in SHP:
    SOFF[_n] = _at
    _at += _c
NSHP = _at

NBLOCKS = 16 * 64 + 4 * (8 + 8 + 16 + 16) + 16 * 2 + 32 * 16 + 81 * 16 + 32 * 16 + \
    16 * (8 + 4 + 4 + 8 + 8 + 1 + 8 + 8 + 8 + 48) + 32 * 8 + 16 * 8 * 2 + 16 * 16 + 86 * 16 + 43 * 16
NUNITS = -(-NBLOCKS // UB)


class Eng:

    def __init__(self, name, sem):
        self.name, self.sem, self.n, self.q, self.seen = name, sem, 0, [], {}

    def wait(self, *tokens):
        for t in tokens:
            if t is None:
                continue
            sem, v = t
            if self.seen.get(id(sem), 0) < v:
                self.seen[id(sem)] = v
                self.q.append(lambda e, sem=sem, v=v: e.wait_ge(sem, v))

    def op(self, fn, *waits, inc=True, chain=True):
        self.wait(*waits)
        if chain and self.n:
            self.wait((self.sem, self.n))
        if inc:
            self.n += 1
            self.q.append(lambda e: fn(e).then_inc(self.sem, 1))
            return (self.sem, self.n)
        self.q.append(fn)
        return None

    @property
    def last(self):
        return (self.sem, self.n) if self.n else None

    def run(self, e):
        for f in self.q:
            f(e)


class Ring:

    def __init__(self, items):
        self.items, self.toks, self.held, self.i = items, [()] * len(items), [False] * len(items), 0

    def get(self):
        n = len(self.items)
        k = next(j % n for j in range(self.i, self.i + n) if not self.held[j % n])
        self.i = k + 1
        self.held[k] = True
        return k, self.items[k], self.toks[k]

    def free(self, k, *tokens):
        assert self.held[k]
        self.toks[k], self.held[k] = tokens, False


class Map:

    def __init__(self, nc, base, end):
        self.nc, self.at, self.end = nc, base, end

    def __call__(self, name, cols, dt=F32, rows=128):
        t = self.nc.alloc_sbuf_tensor_at(name, [rows, cols], dt, offset=self.at)
        self.at += (cols * 4 + 31) // 32 * 32
        assert self.at <= self.end, (name, self.at, self.end)
        return t[:, :]


def v3(ap, a):
    return ap.rearrange("p (a b) -> p a b", a=a)


def build(nc, args, out, scratch):
    order = []
    ctx = ExitStack()
    with ctx:
        def sem(name):
            return ctx.enter_context(nc.semaphore(name))

        base = (nc.sbuf_base + 31) // 32 * 32
        end = nc.sbuf_usable_end
        fx = Map(nc, base, end)
        RAW = v3(fx("RAW", NRAW * UB * 128), NRAW)
        WH = v3(fx("WH", NW * UB * 128, F32R), NW)
        WL = v3(fx("WL", NW * UB * 128, F32R), NW)
        XN = v3(fx("XN", 16 * 512, F32R), 16)
        CV = fx("CV", NVEC)
        CS = fx("CS", NSHP)
        RSB = fx("RSB", 256)
        SQF = fx("SQ", 1024)
        SQ, SQ4 = v3(SQF, 2), v3(SQF, 4)
        RS1 = fx("RS1", 256)
        RST = fx("RST", 2)
        identr = fx("identr", 128, F32R)
        maskr = fx("maskr", 384, F32R)
        EPSC = fx("epsc", 1)
        R0 = fx.at

        PS = [ctx.enter_context(nc.psum_tensor(f"ps{i}", [128, 512], F32))[:, :] for i in range(8)]

        T = Eng("T", sem("s_t"))
        V = Eng("V", sem("s_v"))
        A = Eng("A", sem("s_a"))
        G = Eng("G", sem("s_g"))
        S = Eng("S", sem("s_s"))
        raw_sem = [sem(f"s_raw{i}") for i in range(NRAW)]
        in_sems = [sem(f"s_in{i}") for i in range(20)]
        st_sem = sem("s_store")
        out_sem = sem("s_out")

        def cv(name, c, n=1, rows=slice(0, 128)):
            return CV[rows, VOFF[name] + c:VOFF[name] + c + n]

        def cs(name, n=None, c=0, rows=slice(0, 128)):
            w = dict(SHP)[name]
            return CS[rows, SOFF[name] + c:SOFF[name] + c + (n or w)]

        ident, ones = cs("ident"), cs("ones")

        n_in = [0]

        def load(dst, src, *waits):
            s = in_sems[n_in[0]]
            n_in[0] += 1
            S.op(lambda e: e.dma_start(dst, src).then_inc(s, 16), *waits, inc=False, chain=False)
            return (s, 16)

        t_cv = load(CV, args["vec"])
        t_cs = load(CS, args["shp"])

        raw_free = [None] * NRAW
        w_free = [None] * NW
        loaded, split_at = [0], [0]
        split_tok = {}

        def load_unit():
            u = loaded[0]
            loaded[0] += 1
            k = u % NRAW
            S.op(lambda e: e.dma_start(RAW[:, k, :], args["w"][u]).then_inc(raw_sem[k], 16),
                 *(raw_free[k] or ()), inc=False, chain=False)

        def split_unit():
            u = split_at[0]
            split_at[0] += 1
            k, w = u % NRAW, u % NW
            got = (raw_sem[k], 16 * (u // NRAW + 1))
            ta = A.op(lambda e: e.activation(WH[:, w, :], RAW[:, k, :], ACT.Copy),
                      got, w_free[w], chain=False)
            tv = V.op(lambda e: e.tensor_tensor(WL[:, w, :], RAW[:, k, :], WH[:, w, :].bitcast(F32),
                                                ALU.subtract), got, ta, w_free[w], chain=False)
            split_tok[u] = tv
            raw_free[k] = (tv,)
            if loaded[0] < NUNITS:
                load_unit()

        for _ in range(NRAW):
            load_unit()

        blk = [0]
        since = [0]

        def unit_ready():
            u = blk[0] // UB
            if blk[0] % UB == 0:
                while split_at[0] < min(u + NW, NUNITS) and split_at[0] - NW < u:
                    split_unit()
            return u, blk[0] % UB

        def unit_done(u, b):
            if b == UB - 1:
                w_free[u % NW] = T.last

        tasks = []

        def step(g):
            try:
                next(g)
                return True
            except StopIteration:
                return False

        def tick():
            for g in list(tasks):
                if not step(g):
                    tasks.remove(g)

        def start(g):
            tasks.append(g)
            return g

        def finish(*gs):
            while any(g in tasks for g in gs):
                tick()

        gring = Ring(PS[0:4])
        sring = Ring(PS[4:8])
        pend = []

        def flush():
            while pend:
                pend.pop(0)()

        def gemm(name, c0, kt, rhs, epi, *waits, k0=0, width=128):
            i, bank, fr = gring.get()
            T.wait(*fr, *waits)
            for k in range(kt):
                order.append((name, k0 + k, c0, width))
                u, b = unit_ready()
                T.wait(split_tok[u])
                h, l = WH[:, u % NW, b * 128:b * 128 + 128], WL[:, u % NW, b * 128:b * 128 + 128]
                x = rhs(k)
                if rhs is xn:
                    T.wait(xn_tok[k])
                last = k == kt - 1
                for j, (p, q) in enumerate(((h, x[:, 0:256]), (h, x[:, 256:512]), (l, x[:, 0:256]))):
                    tt = T.op(lambda e, p=p, q=q, s=(k == 0 and j == 0), f=(last and j == 2): e.matmul(
                        bank[:, 0:256], p, q, start=s, stop=f, skip_group_check=True),
                        inc=(j == 2 and (last or b == UB - 1)), chain=False)
                unit_done(u, b)
                blk[0] += 1
                since[0] += 1
            flush()
            pend.append(lambda: gring.free(i, *epi(bank, tt)))
            if since[0] >= TICK:
                since[0] = 0
                tick()

        def gemm_t(name, c0, kt, lhs, epi, *waits):
            i0, b0, f0 = gring.get()
            i1, b1, f1 = gring.get()
            T.wait(*f0, *f1, *waits)
            for k in range(kt):
                for j in range(4):
                    order.append((name, k, c0 + 128 * j, 128))
                u, b = unit_ready()
                assert b % 4 == 0
                T.wait(split_tok[u])
                h, l = WH[:, u % NW, b * 128:b * 128 + 512], WL[:, u % NW, b * 128:b * 128 + 512]
                x = lhs(k)
                if lhs is xn:
                    T.wait(xn_tok[k])
                for t, bank in ((0, b0), (1, b1)):
                    xh, xl = x[:, 128 * t:128 * t + 128], x[:, 256 + 128 * t:384 + 128 * t]
                    for m, (p, q) in enumerate(((xh, h), (xh, l), (xl, h))):
                        fin = t == 1 and m == 2 and (k == kt - 1 or b == UB - 4)
                        tt = T.op(lambda e, p=p, q=q, bank=bank, s=(k == 0 and m == 0), f=(k == kt - 1 and m == 2):
                                  e.matmul(bank, p, q, start=s, stop=f, skip_group_check=True),
                                  inc=fin, chain=False)
                blk[0] += 4
                unit_done(u, b + 3)
                since[0] += 4
            flush()

            def go():
                t = epi(b0, b1, tt)
                gring.free(i0, t)
                gring.free(i1, t)
            pend.append(go)
            if since[0] >= TICK:
                since[0] = 0
                tick()

        def evac(dst, bank, *waits, rows=slice(0, 128)):
            return copy_(dst, bank[rows, 0:256], *waits)

        def evac_rs(dst, bank, *waits, rows=slice(0, 128)):
            return tt_(dst, bank[rows, 0:256], RSB[rows, :], ALU.mult, *waits)

        def xn(k):
            return XN[:, k, :]

        def copy_(dst, src, *waits):
            return V.op(lambda e: e.tensor_copy(dst, src), *waits)

        def memset_(dst, v, E=V):
            return E.op(lambda e: e.memset(dst, v))

        def rmax_(dst, src):
            return V.op(lambda e: e.tensor_reduce(dst, src, AX, MAX))

        def recip_(dst, src, *waits):
            return V.op(lambda e: e.reciprocal(dst, src), *waits)

        def scan_(dst, a, b, init, o0, o1, *waits):
            return V.op(lambda e: e.tensor_tensor_scan(dst, a, b, init, o0, o1), *waits)

        def act(dst, src, f, *waits, bias=0.0, scale=1.0, accum=None):
            if accum is None:
                return A.op(lambda e: e.activation(dst, src, f, bias=bias, scale=scale), *waits)
            return A.op(lambda e: e.activation(dst, src, f, bias=bias, scale=scale, accum_out=accum), *waits)

        def tt_(dst, a, b, op, *waits, E=None):
            return (E or V).op(lambda e: e.tensor_tensor(dst, a, b, op), *waits)

        def ts_(dst, a, s1, s2, o0, o1, *waits, E=None):
            if s2 is None:
                return (E or V).op(lambda e: e.tensor_scalar(dst, a, s1, None, o0), *waits)
            return (E or V).op(lambda e: e.tensor_scalar(dst, a, s1, s2, o0, o1), *waits)

        def stt(dst, a, s, b, o0, o1, *waits, E=None):
            return (E or V).op(lambda e: e.scalar_tensor_tensor(out=dst, in0=a, scalar=s, in1=b, op0=o0, op1=o1), *waits)

        MUL, ADD, SUB, MAX, MIN = ALU.mult, ALU.add, ALU.subtract, ALU.max, ALU.min

        def mm(dst, l, r, *waits, start=True, stop=True, inc=True):
            return T.op(lambda e: e.matmul(dst, l, r, start=start, stop=stop, skip_group_check=True),
                        *waits, inc=inc, chain=False)

        def transpose(dst, src, idn, *waits, inc=True):
            return T.op(lambda e: e.transpose(dst, src, idn), *waits, inc=inc, chain=False)

        def split(dst, src, t_src, *waits):
            n = len(src.shape)
            hi = dst[:, :, 0:256] if n == 3 else dst[:, 0:256]
            lo = dst[:, :, 256:512] if n == 3 else dst[:, 256:512]
            ta = act(hi, src, ACT.Copy, t_src, *waits)
            return tt_(lo, src, hi.bitcast(F32), SUB, ta, *waits)

        def barrier(*engines):
            toks = [x.last for x in (T, V, A, G)]
            for x in engines:
                x.wait(*toks)

        def softplus(dst, x, t1, t2, t_x, positive_only=False):
            act(t1, x, ACT.Abs, t_x)
            ta = act(t1, t1, ACT.Exp, scale=-1.0)
            tv = ts_(t2, t1, 1.0, None, ADD, None, ta)
            ta = act(dst, t2, ACT.Ln, tv)
            ts_(t2, t2, -1.0, 1e-30, ADD, ADD, ta)
            recip_(t2, t2)
            stt(dst, dst, 1e-30, t2, ADD, MUL)
            tt_(dst, dst, t1, MUL)
            return stt(dst, x, 0.0, dst, MAX, ADD)

        def rs_from(dst, bank_ap, n, t_ps, *waits):
            act(dst, bank_ap, ACT.Ln, t_ps, *waits, bias=EPSC, scale=1.0 / n)
            return act(dst, dst, ACT.Exp, scale=-0.5)

        def sumsq(src, nt, t_src, bank, *waits):
            tt = None
            for k in range(0, nt, 2):
                w = (k // 2) % 2
                ta = act(SQ[:, w, :], src(k), ACT.Square, t_src, sq_free[w])
                mm(bank[:, 0:256], ones, SQ[:, w, 0:256], ta, *waits, start=(k == 0), stop=False, inc=False)
                tt = mm(bank[:, 0:256], ones, SQ[:, w, 256:512], start=False, stop=(k == nt - 2))
                sq_free[w] = tt
            return tt

        sq_free = [None, None]

        class Norm:

            def __init__(self, X, wname, tmp, first=None):
                self.X, self.w, self.tmp, self.first = X, wname, tmp, first
                self.i, self.bank, self.fr = sring.get()
                if first:
                    self.j, self.bank2, self.fr2 = sring.get()
                self.later, self.n = [], 0
                self.tmp_free = [None, None]

            def run_later(self):
                q, self.later = self.later, []
                for f in q:
                    f()

            def tile(self, t_x):
                k, self.n = self.n, self.n + 1
                X, tmp = self.X[:, k, :], self.tmp[:, k % 2, :]
                last = k == 15
                t = t_x
                if self.first:
                    t = ts_(tmp, X, cv(self.first, k), None, MUL, None, t_x, self.tmp_free[k % 2])
                    ta2 = act(SQ4[:, 2 + k % 2, :], tmp, ACT.Square, t, sq4_free[2 + k % 2])
                    t = ts_(tmp, tmp, cv(self.w, k), None, MUL, None, ta2)
                else:
                    t = ts_(tmp, X, cv(self.w, k), None, MUL, None, t_x, self.tmp_free[k % 2])
                self.run_later()
                hi, lo = XN[:, k, 0:256], XN[:, k, 256:512]
                ta = act(hi, tmp, ACT.Copy, t)
                tq = act(SQ4[:, k % 2, :], X, ACT.Square, t_x, sq4_free[k % 2])

                def rest():
                    xn_tok[k] = self.tmp_free[k % 2] = tt_(lo, tmp, hi.bitcast(F32), SUB, ta)
                    sq4_free[k % 2] = self.tt = mm(self.bank[:, 0:256], ones, SQ4[:, k % 2, :], tq, *self.fr,
                                                   start=(k == 0), stop=last)
                    if self.first:
                        sq4_free[2 + k % 2] = self.tt = mm(self.bank2[:, 0:256], ones, SQ4[:, 2 + k % 2, :],
                                                           *self.fr2, start=(k == 0), stop=last)
                self.later.append(rest)
                if last:
                    self.run_later()

            def end(self, rst=None):
                ta = rs_from(RSB, self.bank[:, 0:256], 2048, self.tt, V.last)
                sring.free(self.i, ta)
                if self.first:
                    V.op(lambda e: e.tensor_copy(RS1, RSB), ta)
                    t = V.last
                    t = tt_(RSB, RSB, RSB, MUL)
                    t = tt_(RSB, RSB, self.bank2[:, 0:256], MUL, self.tt)
                    sring.free(self.j, t)
                    ta = rs_from(RSB, RSB, 2048, t)
                    ta = tt_(RSB, RSB, RS1, MUL, ta)
                if rst is not None:
                    i, b, fr = sring.get()
                    mm(b[:, 0:1], RSB[0:1, 0:128], ones[0:1, 0:1], ta, *fr, inc=False)
                    tt = mm(b[:, 1:2], RSB[0:1, 128:256], ones[0:1, 0:1])
                    t = copy_(rst, b[:, 0:2], tt)
                    sring.free(i, t)
                    A.wait(t)
                V.wait(ta)
                return ta

        sq4_free = [None] * 4
        xn_tok = [None] * 16

        memset_(EPSC, 1e-6, E=V)
        copy_(identr, ident, t_cs)
        t0 = copy_(maskr, cs("mask"))
        A.wait(t0, t_cv, t_cs)
        V.wait(t_cv, t_cs)
        T.wait(t_cv, t_cs, t0)
        G.wait(t_cv, t_cs, t0)

        m = Map(nc, R0, end)
        YS = v3(m("YS1", 32 * 512, F32R), 32)
        ys0 = R0
        OZ = v3(m("OZ", 16 * 256), 16)
        w1 = m.at
        mm_ = Map(nc, ys0, end)
        XMS = [v3(mm_(f"XMS{i}", 4 * 512, F32R), 4) for i in range(2)]
        XCS = [v3(mm_(f"XCS{i}", 4 * 512, F32R), 4) for i in range(2)]
        QKV = [(v3(mm_(f"Q{i}", 512), 2), v3(mm_(f"K{i}", 512), 2), v3(mm_(f"VT{i}", 1024), 2)) for i in range(4)]
        m = Map(nc, w1, end)
        WIF = m("WIF", 32 * 36).rearrange("p (a b) -> p a b", a=32)
        XMP = [v3(m(f"XMP{i}", 4 * 259), 4) for i in range(2)]
        XMC = v3(m("XMC", 1024), 4)
        VF = v3(m("VF", 1024), 4)
        t_wif = load(WIF, args["w_if"])
        mt = Map(nc, w1 + 5120, end)
        X0 = v3(mt("X0", 16 * 256), 16)
        TMP0 = v3(mt("TMP0", 512), 2)
        nm = Norm(X0, "e_norm", TMP0)
        for q in range(4):
            t_x = load(X0[:, 4 * q:4 * q + 4, :], args["x"][:, 4 * q:4 * q + 4, :])
            for k in range(4):
                nm.tile(t_x)
        nm.end()
        barrier(V, A)
        for i in range(2):
            memset_(XMP[i][:, :, 0:3], 0.0, E=V)

        def conv(dst, src, w, b, taps, t_src, *waits):
            ta = act(dst, src[:, taps - 1:taps + 255], ACT.Identity, t_src, *waits, bias=b, scale=w(taps - 1))
            tv = ta
            for t in range(taps - 2, -1, -1):
                tv = stt(dst, src[:, t:t + 256], w(t), dst, MUL, ADD, tv)
            return tv

        t_xm = {}
        xms_free, xcs_free, xmp_free = [(), ()], [(), ()], [None, None]
        t_q, t_k, t_vt = {}, {}, {}
        gi, GB, gfr = sring.get()
        gate_n = [0]
        qk_toks = {}
        conv_toks = {}

        def xm_epi(h, j):
            def f(bank, tt):
                p = h % 2
                tv = evac_rs(XMP[p][:, j, 3:259], bank, tt, xmp_free[p])
                if j == 3:
                    finish_xm(h, tv)
                return (tv,)
            return f

        def finish_xm(h, tv):
            p = h % 2
            for j in range(4):
                k = 4 * h + j
                t = conv(XMC[:, j, :], XMP[p][:, j, :], lambda t, k=k: cv("conv_m_w", 16 * t + k),
                         cv("conv_m_b", k), 4, tv)
            t = act(XMC, XMC, ACT.Silu, t)
            t_xc = split(XCS[p], XMC, t, *xcs_free[p])
            t_x_ = split(XMS[p], XMP[p][:, :, 3:259], tv, *xms_free[p])
            xmp_free[p] = t_x_
            conv_toks[h] = (t_xc, t_x_)

        def gate_mm(kt, src, tok, last=False):
            tt = mm(GB[0:36, 0:256], WIF[:, kt, :], src, tok, t_wif, start=(gate_n[0] == 0),
                    stop=(gate_n[0] == 31))
            gate_n[0] += 1
            return tt

        vf_i = [0]
        vf_free = [None] * 4
        side_q = []

        def qk_epi(h, j, isk):
            def f(bank, tt):
                dst = QKV[h][1 if isk else 0][:, j, :]
                tv = evac(dst, bank, tt)
                t = tv
                if isk:
                    t = act(dst, dst, ACT.Copy, tv, scale=0.0625)
                qk_toks.setdefault(h, []).append(t)
                side_q.append(lambda: gate_mm((8 if isk else 0) + 2 * h + j, dst, t))
                return (tv,)
            return f

        def v_epi(h, j):
            def f(bank, tt):
                s = vf_i[0] % 4
                vf_i[0] += 1
                tv = evac(VF[:, s, :], bank, tt, vf_free[s])

                def side():
                    gate_mm(16 + 4 * h + j, VF[:, s, :], tv)
                    i, sbk, fr = sring.get()
                    transpose(sbk[:, 0:128], VF[:, s, 0:128], ident, *fr, inc=False)
                    t2 = transpose(sbk[:, 128:256], VF[:, s, 128:256], ident)
                    vf_free[s] = t2
                    t3 = act(QKV[h][2][:, :, 128 * j:128 * j + 128], v3(sbk[:, 0:256], 2), ACT.Copy, t2)
                    sring.free(i, t3)
                    qk_toks.setdefault(h, []).append(t3)
                side_q.append(side)
                return (tv,)
            return f

        def o_epi(h, j):
            def f(bank, tt):
                tv = evac(OZ[:, 4 * h + j, :], bank, tt)
                if j == 3:
                    oz_t[h] = act(OZ[:, 4 * h:4 * h + 4, :], OZ[:, 4 * h:4 * h + 4, :], ACT.Sigmoid, tv)
                return (tv,)
            return f
        oz_t = {}

        def drain_side():
            while True:
                q, side_q[:] = list(side_q), []
                for f in q:
                    f()
                yield

        dr = start(drain_side())
        for h in range(5):
            if h < 4:
                for j in range(4):
                    gemm("e_w_in", 2048 + 512 * h + 128 * j, 16, xn, xm_epi(h, j))
            if h > 0:
                g = h - 1
                p = g % 2
                if h == 4:
                    flush()
                t_xc, t_x_ = conv_toks[g]
                for j in range(2):
                    gemm("e_w_q", (g, 128 * j), 4, lambda k: XCS[p][:, k, :], qk_epi(g, j, False), t_xc)
                for j in range(2):
                    gemm("e_w_k", (g, 128 * j), 4, lambda k: XCS[p][:, k, :], qk_epi(g, j, True))
                xcs_free[p] = (T.last,)
                for j in range(4):
                    gemm("e_w_v", (g, 128 * j), 4, lambda k: XMS[p][:, k, :], v_epi(g, j), t_x_)
                for j in range(4):
                    gemm("e_w_o", (g, 128 * j), 4, lambda k: XMS[p][:, k, :], o_epi(g, j))
                xms_free[p] = (T.last,)

        flush()
        tick()
        tick()
        tasks.remove(dr)
        barrier(V, A, G)
        m = Map(nc, w1, end)
        ZQ = v3(m("ZQ", 1024), 4)
        ROWS = [m(f"ROW{i}", 256, rows=4) for i in range(6)]
        ONER = m("ONER", 256, rows=4)
        top = Map(nc, (end - 2304) // 32 * 32, end)
        top_at = top.at
        RC = top("RC", 512, rows=4)
        AT = top("AT", 8)
        bank_g = GB
        zq_free = [None]

        def gates():
            GI, FX, L1, L2, L3, GC = ROWS
            memset_(ONER, 1.0, E=V)
            act(GI, bank_g[0:4, 0:256], ACT.Identity, T.last, bias=cv("b_if", 0, rows=slice(0, 4)))
            ta = act(FX, bank_g[32:36, 0:256], ACT.Identity, bias=cv("b_if", 0, rows=slice(32, 36)))
            sring.free(gi, ta)
            tv = ts_(FX, FX, -1.0, None, MUL, None, ta)
            yield
            tv = softplus(L3, FX, L1, L2, tv)
            yield
            ts_(L3, L3, -1.0, None, MUL, None)
            scan_(GC, ONER, L3, 0.0, MUL, ADD)
            tt_(L1, GI, GC, SUB)
            ts_(L2, L1, 0.0, None, MUL, None)
            scan_(FX, L1, L2, 0.0, MAX, MAX)
            tv = tt_(L2, FX, GC, ADD)
            ts_(RC[:, 0:256], FX, -1.0, None, MUL, None)
            ta = act(RC[:, 256:512], L2, ACT.Exp, tv, scale=-1.0)
            yield
            i, bk, fr = sring.get()
            mm(bk[:, 0:4], L1[:, 0:128], ident[0:4, 0:4], *fr, tv, inc=False)
            tt = mm(bk[:, 4:8], L1[:, 128:256], ident[0:4, 0:4])
            t = copy_(AT, bk[:, 0:8], tt)
            sring.free(i, t)
            rc_tok.append((ta, t, V.last))

        rc_tok = []
        gt = start(gates())

        def z_epi(j):
            def f(bank, tt):
                tv = evac_rs(ZQ[:, j % 4, :], bank, tt)
                if j % 4 == 3:
                    q = slice(j - 3, j + 1)
                    ta = act(ZQ, ZQ, ACT.Silu, tv)
                    t = tt_(OZ[:, q, :], OZ[:, q, :], ZQ, MUL, ta, oz_t[j // 4])
                return (tv,)
            return f

        for j in range(16):
            gemm("e_w_in", 4096 + 2048 + 128 * j, 16, xn, z_epi(j))
        flush()
        finish(gt)
        barrier(V, A, G)

        m = Map(nc, w1, end)
        XL = v3(m("XL", 2 * 259), 2)
        XC = v3(m("XC", 512), 2)
        RB = v3(m("RB", 512), 2)
        IB = v3(m("IB", 512), 2)
        ZB = v3(m("ZB", 512), 2)
        m2 = Map(nc, m.at, top_at)
        EB = m2("EB", 384)
        EM = m2("EM", 256)
        DN = m2("DN", 256)
        HB = v3(m2("HB", 1024), 4)
        RS2 = m2("RS2", 256)
        SP8 = m2("SP8", 16)
        SPt = [m2(f"SPt{i}", 16) for i in range(3)]
        memset_(XL[:, :, 0:3], 0.0, E=V)
        tv = ts_(SPt[2], cv("lru_lam", 0, 16), -1.0, None, MUL, None)
        softplus(SP8, SPt[2], SPt[0], SPt[1], tv)
        t_sp = ts_(SP8, SP8, 8.0, None, MUL, None)
        NSP8 = m2("NSP8", 16)
        t_sp = ts_(NSP8, SP8, -1.0, None, MUL, None)

        def attend(h):
            Q, K, VT = QKV[h]
            i, b0, fr = sring.get()
            tt = mm(b0, ident[0:4, h:h + 1].to_broadcast([4, 128]), RC, *fr, *rc_tok[0])
            i1, b1, fr1 = sring.get()
            w = [t for t in qk_toks[h]]
            mm(b1[:, 0:256], K[:, 0, 0:128], Q[:, 0, :], *fr1, *w, start=True, stop=False, inc=False)
            mm(b1[:, 0:256], K[:, 1, 0:128], Q[:, 1, :], start=False, stop=True, inc=False)
            mm(b1[:, 256:384], K[:, 0, 128:256], Q[:, 0, 128:256], start=True, stop=False, inc=False)
            ts1 = mm(b1[:, 256:384], K[:, 1, 128:256], Q[:, 1, 128:256], start=False, stop=True)
            yield
            te = act(EM, b0[:, 256:512], ACT.Copy, tt, V.last)
            t1 = tt_(EB[:, 0:256], b0[:, 0:256], cs("mask", 256), ADD, tt, te, T_last[0])
            t1 = tt_(EB[:, 256:384], b0[:, 128:256], cs("mask", 128), ADD)
            ta = act(EB[:, 0:256], EB[:, 0:256], ACT.Exp, t1, bias=AT[:, h:h + 1])
            ta = act(EB[:, 256:384], EB[:, 256:384], ACT.Exp, bias=AT[:, 4 + h:5 + h])
            sring.free(i, ta)
            t1 = tt_(EB, EB, b1[:, 0:384], MUL, ta, ts1)
            sring.free(i1, t1)
            yield
            id_, bd, fr = sring.get()
            mm(bd[:, 0:256], ones, EB[:, 0:256], *fr, t1, start=True, stop=False, inc=False)
            td = mm(bd[:, 128:256], ones, EB[:, 256:384], start=False, stop=True)
            nb = []
            for n in range(2):
                ib, bn, fr = sring.get()
                for j in range(2):
                    d = 2 * n + j
                    mm(bn[:, 256 * j:256 * j + 256], VT[:, 0, 128 * d:128 * d + 128], EB[:, 0:256], *fr,
                       start=True, stop=False, inc=False)
                    tn_ = mm(bn[:, 256 * j + 128:256 * j + 256], VT[:, 1, 128 * d:128 * d + 128],
                             EB[:, 256:384], start=False, stop=True)
                nb.append((ib, bn))
            T_last[0] = T.last
            yield
            stt(DN, bd[:, 0:256], -1.0, EM, MUL, MAX, td, te)
            tt_(DN, bd[:, 0:256], DN, MAX)
            t = recip_(DN, DN)
            sring.free(id_, t)
            for n in range(2):
                t = tt_(HB[:, 2 * n:2 * n + 2, :], v3(nb[n][1], 2), DN.unsqueeze(1).to_broadcast([128, 2, 256]),
                        MUL, tn_, A.last)
                sring.free(nb[n][0], t)
            i, bk, fr = sring.get()
            tq = sumsq(lambda k: HB[:, k:k + 2, :].rearrange("p a b -> p (a b)"), 4, t, bk, *fr)
            yield
            ta = rs_from(RS2, bk[:, 0:256], 512, tq)
            sring.free(i, ta)
            for j in range(4):
                stt(HB[:, j, :], HB[:, j, :], cv("m_norm", 4 * h + j), RS2, MUL, MUL, ta)
            t = tt_(HB, HB, OZ[:, 4 * h:4 * h + 4, :], MUL)
            ys_t[h] = split(YS[:, 16 + 4 * h:20 + 4 * h, :], HB, t, T_last[0])
        ys_t = {}
        T_last = [None]

        def all_heads():
            for h in range(4):
                yield from attend(h)
                yield

        heads = start(all_heads())
        xl_t = {}

        def xl_epi(j):
            def f(bank, tt):
                tv = evac_rs(XL[:, j % 2, 3:259], bank, tt)
                if j % 2:
                    for i in range(2):
                        k = j - 1 + i
                        t = conv(XC[:, i, :], XL[:, i, :], lambda t, k=k: cv("conv_l_w", 16 * t + k),
                                 cv("conv_l_b", k), 4, tv)
                    xl_t[j // 2] = split(YS[:, j - 1:j + 1, :], XC, t)
                return (tv,)
            return f

        def zl_epi(j):
            def f(bank, tt):
                tv = evac_rs(ZB[:, j % 2, :], bank, tt)
                if j % 2:
                    act(ZB, ZB, ACT.Silu, tv)
                return (tv,)
            return f

        def ri_epi(j, buf, nm):
            def f(bank, tt):
                tv = evac(buf[:, j % 2, :], bank, tt)
                if j % 2 and nm == "lru_bx":
                    lru_tail(j - 1, tv)
                return (tv,)
            return f

        def lru_tail(j0, tv):
            for i in range(2):
                k = j0 + i
                act(RB[:, i, :], RB[:, i, :], ACT.Sigmoid, tv, bias=cv("lru_ba", k))
                act(IB[:, i, :], IB[:, i, :], ACT.Sigmoid, bias=cv("lru_bx", k))
            TH = XL[:, :, 0:256]
            ti = A.last
            tu = tt_(IB, IB, XC, MUL, ti)
            for i in range(2):
                k = j0 + i
                act(TH[:, i, :], RB[:, i, :], ACT.Tanh, t_sp, scale=SP8[:, k:k + 1])
            for i in range(2):
                k = j0 + i
                act(RB[:, i, :], RB[:, i, :], ACT.Exp, scale=NSP8[:, k:k + 1])
            act(XC, TH, ACT.Ln, tu, bias=1.0)
            ta = act(TH, TH, ACT.Ln, scale=2.0)
            t = tt_(TH, TH, XC, SUB, ta)
            ta = act(TH, TH, ACT.Exp, t, scale=0.5)
            t = tt_(IB, IB, TH, MUL, ta)
            for i in range(2):
                scan_(XC[:, i, :], RB[:, i, :], IB[:, i, :], 0.0, MUL, ADD)
            t = tt_(XC, XC, ZB, MUL)
            split(YS[:, j0:j0 + 2, :], XC, t, ys_l_free)
            memset_(XL[:, :, 0:3], 0.0, E=V)
            A.wait(V.last)

        ys_l_free = T.last
        for j in range(0, 16, 2):
            for i in range(2):
                gemm("e_w_in", 128 * (j + i), 16, xn, xl_epi(j + i))
            for i in range(2):
                gemm("e_w_in", 4096 + 128 * (j + i), 16, xn, zl_epi(j + i))
            for nm, wn, buf in (("lru_ba", "e_lru_wa", RB), ("lru_bx", "e_lru_wx", IB)):
                for i in range(2):
                    flush()
                    gemm(wn, (j + i, 0), 1, lambda k, i=i: YS[:, j + i, :], ri_epi(j + i, buf, nm), xl_t[j // 2])
            flush()
        finish(heads)
        ys_done = V.last
        barrier(V, A, G)

        def out_proj(name, kt, ys, X, load_tok, first_wait, nm):
            def epi(n):
                def f(bank, tt):
                    t = tt_(X[:, n, :], X[:, n, :], bank[:, 0:256], ADD, tt, load_tok)
                    nm.tile(t)
                    return (t,)
                return f
            T.wait(first_wait)
            for n in range(16):
                gemm(name, 128 * n, kt, lambda k: ys(k), epi(n))
            flush()
            return V.last

        XT = (end - 18 * 1024 - 64) // 32 * 32
        m = Map(nc, XT, end)
        X = v3(m("X1", 16 * 256), 16)
        TMP = v3(m("TMP1", 512), 2)
        t_x = load(X, args["x"], V.last, A.last, T.last)
        nm = Norm(X, "o_norm", TMP)
        t = out_proj("e_w_out", 32, lambda k: YS[:, k, :], X, t_x, ys_done, nm)

        stores = [0]

        def store_x(X, t):
            S.op(lambda e: e.dma_start(scratch, X).then_inc(st_sem, 16), t, inc=False, chain=False)
            stores[0] += 16
            return (st_sem, stores[0])

        t_st = store_x(X, t)
        nm.end()
        barrier(V, A)
        m = Map(nc, R0, end)
        YS = v3(m("YS2", 32 * 512, F32R), 32)
        CSX = m("CSX", 384, rows=64)
        DTR = m("DTR", 256, rows=64)
        NCST = m("NCST", 128)
        DTT = m("DTT", 128)
        XP = v3(m("XP", 6 * 259), 6)
        XV = [v3(m(f"XV{i}", 6 * 256), 6) for i in range(2)]
        ZB = v3(m("ZB2", 4 * 256), 4)
        XDT = v3(m("XDT", 1024), 2)
        CBm = m("CBm", 384)
        DB = [m(f"DB{i}", 384) for i in range(3)]
        YB = v3(m("YB", 1024), 4)
        RS3 = m("RS3", 256)
        RT = [XV[0][0:64, i, :] for i in range(4)]
        ONE64 = XV[0][0:64, 4, :]
        EA = XV[0][0:64, 5, 0:1]
        memset_(XP[:, :, 0:3], 0.0, E=V)

        dt_tok = []

        def dt_epi(bank, tt):
            tv = evac_rs(RT[0], bank, tt, rows=slice(0, 64))
            t = ts_(RT[0], RT[0], cv("dt_bias", 0, rows=slice(0, 64)), None, ADD, None)
            memset_(ONE64, 1.0, E=V)
            t = softplus(DTR, RT[0], RT[1], RT[2], V.last)
            ta = act(EA, cv("a_log", 0, rows=slice(0, 64)), ACT.Exp)
            ts_(RT[3], DTR, EA, -1.0, MUL, MUL, ta)
            scan_(CSX[:, 0:256], ONE64, RT[3], 0.0, MUL, ADD)
            dt_tok.append(copy_(CSX[:, 256:384], CSX[:, 128:256]))
            return (tv,)

        def dt_side():
            while not dt_tok:
                yield
            yield
            i, bk, fr = sring.get()
            idn = ident[0:64, 0:64]
            transpose(bk[:, 0:64], CSX[:, 0:128], idn, *fr, dt_tok[0], inc=False)
            transpose(bk[:, 64:128], CSX[:, 128:256], idn, inc=False)
            transpose(bk[:, 128:192], DTR[:, 0:128], idn, inc=False)
            tt = transpose(bk[:, 192:256], DTR[:, 128:256], idn)
            yield
            ts_(NCST, bk[:, 0:128], -1.0, None, MUL, None, tt)
            t = copy_(DTT, bk[:, 128:256])
            sring.free(i, t)
            A.wait(t)
            dts_done.append(t)

        dts_done = []
        gemm("o_w_in", 10240, 16, xn, dt_epi, width=64)
        flush()
        dts = start(dt_side())
        xv_free = [None, None]
        z_tok, v_tok, zb_free = {}, {}, [None]

        def xv_epi(g, s):
            ch = [32 + g, 40 + g, 4 * g, 4 * g + 1, 4 * g + 2, 4 * g + 3]

            def f(bank, tt):
                tv = evac_rs(XP[:, s, 3:259], bank, tt)
                k = ch[s]
                t = conv(XV[g % 2][:, s, :], XP[:, s, :], lambda t: cv("o_conv_w", 48 * t + k),
                         cv("o_conv_b", k), 4, tv, xv_free[g % 2])
                if s == 5:
                    v_tok[g] = act(XV[g % 2], XV[g % 2], ACT.Silu, t)
                return (tv,)
            return f

        def zs_epi(g, j):
            def f(bank, tt):
                tv = evac_rs(ZB[:, j, :], bank, tt)
                if j == 3:
                    z_tok[g] = act(ZB, ZB, ACT.Silu, tv)
                return (tv,)
            return f

        def ssd(g):
            B_, C_, XS_ = XV[g % 2][:, 0, :], XV[g % 2][:, 1, :], XV[g % 2][:, 2:6, :]
            tk = v_tok[g]
            ic, bc, fr = sring.get()
            mm(bc[:, 0:256], B_[:, 0:128], C_, *fr, tk, start=True, stop=True, inc=False)
            tt = mm(bc[:, 256:384], B_[:, 128:256], C_[:, 128:256], start=True, stop=True)
            tx = []
            for t in range(2):
                i, b, fr = sring.get()
                for j in range(4):
                    t2 = transpose(b[:, 128 * j:128 * j + 128], XS_[:, j, 128 * t:128 * t + 128], ident, *fr,
                                   inc=(j == 3))
                tx.append((i, b, t2))
            yield
            ta = act(CBm, bc[:, 0:384], ACT.Copy, tt, V.last)
            sring.free(ic, ta)
            for t in range(2):
                i, b, t2 = tx[t]
                tv = tt_(XDT[:, t, :].rearrange("p (h d) -> p h d", h=8), b.rearrange("p (h d) -> p h d", h=8),
                         DTT[:, 64 * t + 8 * g:64 * t + 8 * g + 8].unsqueeze(2).to_broadcast([128, 8, 64]),
                         MUL, t2, y_last[0])
                sring.free(i, tv)
            t_xdt = V.last
            tg = {}
            banks = {}

            def bc_mm(e):
                h = 8 * g + e
                i, b, fr = sring.get()
                mm(b[:, 0:384], identr, maskr, *fr, start=True, stop=False, inc=False)
                banks[e] = (i, b, mm(b[:, 0:384], ident[0:64, h:h + 1].to_broadcast([64, 128]), CSX,
                                     start=False, stop=True))

            def dec(e):
                i, b, t = banks[e]
                h = 8 * g + e
                d = DB[e % 3]
                act(d[:, 0:256], b[:, 0:256], ACT.Exp, t, d_free[e % 3], bias=NCST[:, h:h + 1])
                ta = act(d[:, 256:384], b[:, 256:384], ACT.Exp, bias=NCST[:, 64 + h:65 + h])
                sring.free(i, ta)
                tg[e] = tt_(d, d, CBm, MUL, ta)

            yb = {}

            def y_mm(e):
                if e % 4 == 0:
                    i, b, fr = sring.get()
                    yb[e // 4] = [i, b, None]
                    T.wait(*fr)
                i, b, _ = yb[e // 4]
                c = 256 * ((e % 4) // 2)
                r = 64 * (e % 2)
                d = DB[e % 3]
                mm(b[r:r + 64, c:c + 256], XDT[:, 0, 64 * e:64 * e + 64], d[:, 0:256], tg[e], t_xdt,
                   start=True, stop=False, inc=False)
                t = mm(b[r:r + 64, c + 128:c + 256], XDT[:, 1, 64 * e:64 * e + 64], d[:, 256:384],
                       start=False, stop=True)
                d_free[e % 3] = t
                yb[e // 4][2] = t

            bc_mm(0)
            yield
            for e in range(8):
                dec(e)
                if e < 7:
                    bc_mm(e + 1)
                if e > 0:
                    y_mm(e - 1)
                yield
            y_mm(7)
            y_last[0] = T.last
            yield
            for n in range(2):
                i, b, t = yb[n]
                for j in range(2):
                    q = 2 * n + j
                    tv = stt(YB[:, q, :], XS_[:, q, :], cv("d_skip", 4 * g + q), b[:, 256 * j:256 * j + 256],
                             MUL, ADD, t, A.last)
                sring.free(i, tv)
            xv_free[g % 2] = tv
            t = tt_(YB, YB, ZB, MUL, z_tok[g])
            zb_free[0] = t
            i, bk, fr = sring.get()
            tq = sumsq(lambda k: YB[:, k:k + 2, :].rearrange("p a b -> p (a b)"), 4, t, bk, *fr)
            yield
            ta = rs_from(RS3, bk[:, 0:256], 512, tq)
            sring.free(i, ta)
            for j in range(4):
                t = stt(YB[:, j, :], YB[:, j, :], cv("gnorm", 4 * g + j), RS3, MUL, MUL, ta)
            split(YS[:, 4 * g:4 * g + 4, :], YB, t)

        y_last = [None]
        d_free = [None] * 3
        prev = None
        for g in range(8):
            if g == 1:
                finish(dts)
            if g == 0:
                xv_free[0] = V.last
            cols = [8192 + 128 * g, 9216 + 128 * g] + [4096 + 512 * g + 128 * j for j in range(4)]
            for s in range(6):
                gemm("o_w_in", cols[s], 16, xn, xv_epi(g, s))
            flush()
            if prev is not None:
                finish(prev)
            finish(dts)
            for e_ in (V, A):
                e_.wait(t_st)
            for j in range(4):
                gemm("o_w_in", 512 * g + 128 * j, 16, xn, zs_epi(g, j))
                if j == 0:
                    prev = start(ssd(g))
            flush()
        finish(prev)
        ys_done = V.last
        barrier(V, A, G)
        m = Map(nc, XT, end)
        X = v3(m("X2", 16 * 256), 16)
        TMP = v3(m("TMP2", 512), 2)
        t_x = load(X, scratch, V.last, A.last, T.last, t_st)
        nm = Norm(X, "norm_mix", TMP, first="final_norm")
        t = out_proj("o_w_out", 32, lambda k: YS[:, k, :], X, t_x, ys_done, nm)
        nm.end(RST)
        for k in range(16):
            t = stt(X[:, k, :], X[:, k, :], cv("final_norm", k), RS1, MUL, MUL, A.last)
        t_st = store_x(X, t)
        barrier(V, A, G)

        m = Map(nc, R0, end)
        GOS = v3(m("GOS", 8 * 512, F32R), 8)
        mz = Map(nc, m.at, end)
        ZS = v3(mz("ZS", 8 * 512, F32R), 8)
        TB = m("TB", 2 * 8 * 256).rearrange("p (c a b) -> p c a b", c=2, a=8)
        US = v3(m("US", 8 * 256), 8)
        BR = v3(m("BR", 8 * 128), 8)
        BI = v3(m("BI", 8 * 128), 8)
        CR = v3(m("CR", 32 * 32), 32)
        CI = v3(m("CI", 32 * 32), 32)
        MB_ = v3(m("MB_", 512), 2)
        GB_ = v3(m("GB_", 512), 2)
        HBs = [v3(m(f"HBs{i}", 512), 2) for i in range(2)]
        PW = m("PW", 2 * 8 * 32).rearrange("p (c l a) -> p c l a", c=2, l=8)
        P1 = [m(f"P1{i}", 32) for i in range(10)]
        w3 = m.at
        tbf = TB.rearrange("p c a b -> p (c a b)")
        CRR, CIR = v3(tbf[:, 0:1024], 32), v3(tbf[:, 1024:2048], 32)
        C1, C2 = v3(tbf[:, 2048:3072], 32), v3(tbf[:, 3072:4096], 32)
        t_b1 = load(BR, args["b_re"], T.last, V.last, A.last)
        t_b2 = load(BI, args["b_im"])
        t_c1 = load(CRR, args["c_re"])
        t_c2 = load(CIR, args["c_im"])

        def s5_consts():
            lr, dt, mag, th, r, s1, c1, den, fr_, fi_ = P1
            li = cv("a_im", 0, 32)
            ts_(lr, cv("a_re", 0, 32), -1e-4, None, MIN, None)
            ta = act(dt, cv("log_dt", 0, 32), ACT.Exp)
            tv = tt_(mag, dt, lr, MUL, ta)
            act(mag, mag, ACT.Exp, tv)
            tt_(th, dt, li, MUL)
            ts_(r, th, 1.0 / TWO_PI, 12582912.0, MUL, ADD)
            ts_(r, r, -12582912.0, None, ADD, None)
            ts_(c1, r, -6.28125, None, MUL, None)
            tt_(th, th, c1, ADD)
            stt(th, r, -0.0019350051879882812, th, MUL, ADD)
            stt(th, r, -3.0199160505063e-07, th, MUL, ADD)
            tv = ts_(th, th, 3.1415925, -3.1415925, MIN, MAX)
            ta = act(s1, th, ACT.Sin, tv)
            ta = act(c1, th, ACT.Sin, scale=0.5)
            tt_(c1, c1, c1, MUL, ta)
            ts_(c1, c1, -2.0, 1.0, MUL, ADD)
            yield
            copy_(PW[:, 0, 0, :], c1)
            copy_(PW[:, 1, 0, :], s1)
            for l in range(1, 8):
                c_, s_ = PW[:, 0, l - 1, :], PW[:, 1, l - 1, :]
                tt_(den, s_, s_, MUL)
                tt_(fr_, c_, c_, MUL)
                tt_(PW[:, 0, l, :], fr_, den, SUB)
                tv = stt(PW[:, 1, l, :], s_, 2.0, c_, MUL, MUL)
            pw_tok.append(tv)
            yield
            tt_(fr_, mag, c1, MUL)
            ts_(fr_, fr_, -1.0, None, ADD, None)
            tt_(fi_, mag, s1, MUL)
            tt_(c1, lr, lr, MUL)
            tt_(den, li, li, MUL)
            tt_(den, den, c1, ADD)
            recip_(den, den)
            tt_(c1, fr_, lr, MUL)
            tt_(s1, fi_, li, MUL)
            tt_(r, c1, s1, ADD)
            tt_(c1, fi_, lr, MUL)
            tt_(s1, fr_, li, MUL)
            tt_(c1, c1, s1, SUB)
            tt_(fr_, r, den, MUL)
            tt_(fi_, c1, den, MUL)
            frb, fib = [x.unsqueeze(2).to_broadcast([128, 32, 32]) for x in (fr_, fi_)]
            tt_(C1, CRR, frb, MUL, t_c1, t_c2)
            tt_(C2, CIR, fib, MUL)
            tt_(CR, C1, C2, SUB)
            yield
            tt_(C1, CRR, fib, MUL)
            tt_(C2, CIR, frb, MUL)
            tv = stt(CI, C1, -1.0, C2, MUL, SUB)
            cc_tok.append(tv)

        pw_tok, cc_tok = [], []
        s5c = start(s5_consts())
        us_t = {}

        def u_epi(j):
            def f(bank, tt):
                tv = evac_rs(US[:, j, :], bank, tt)
                us_t[j] = tv
                return (tv,)
            return f

        for j in range(8):
            gemm("w_in_2", 128 * j, 16, xn, u_epi(j))
        flush()
        finish(s5c)
        A.wait(V.last)

        m = Map(nc, w3, end)

        def phases(b, *waits):
            a = slice(8 * b, 8 * b + 8)
            G.wait(*waits)
            memset_(TB[:, 0, :, 0:1], 1.0, E=G)
            memset_(TB[:, 1, :, 0:1], 0.0, E=G)
            for l in range(8):
                d = 1 << l
                c_, s_ = TB[:, 0, :, 0:d], TB[:, 1, :, 0:d]
                C = PW[:, 0, l, a].unsqueeze(2).to_broadcast([128, 8, d])
                Sn = PW[:, 1, l, a].unsqueeze(2).to_broadcast([128, 8, d])
                cn, sn = TB[:, 0, :, d:2 * d], TB[:, 1, :, d:2 * d]
                q = min(d, 64)
                for o in range(0, d, q):
                    t1 = v3(PT, 8)[:, :, 0:q]
                    x, y = slice(o, o + q), slice(d + o, d + o + q)
                    Cq = PW[:, 0, l, a].unsqueeze(2).to_broadcast([128, 8, q])
                    Sq = PW[:, 1, l, a].unsqueeze(2).to_broadcast([128, 8, q])
                    tt_(TB[:, 0, :, y], TB[:, 0, :, x], Cq, MUL, E=G)
                    tt_(t1, TB[:, 1, :, x], Sq, MUL, E=G)
                    tt_(TB[:, 0, :, y], TB[:, 0, :, y], t1, SUB, E=G)
                    tt_(TB[:, 1, :, y], TB[:, 0, :, x], Sq, MUL, E=G)
                    tt_(t1, TB[:, 1, :, x], Cq, MUL, E=G)
                    tg = tt_(TB[:, 1, :, y], TB[:, 1, :, y], t1, ADD, E=G)
            return tg

        PT = m("PT", 512)
        ALR = m("ALR", 256, rows=16)
        WG = m("WG", 512, rows=16)
        GQ = m("GQ", 256)
        GK = m("GK", 256)
        GR = v3(m("GR", 512), 2)
        GVT = v3(m("GVT", 1024), 2)
        CUM = m("CUM", 256)
        GE1 = m("GE1", 256)
        GE2 = m("GE2", 256)
        GE3 = m("GE3", 256)
        DL = m("DL", 8)
        KTM = m("KTM", 8 * 128).rearrange("p (a b) -> p a b", a=8)
        SC = v3(m("SC", 256), 2)
        ST = m("ST", 7 * 256).rearrange("p (a b) -> p a b", a=7)
        OB = v3(m("OB", 512), 2)
        RS4 = m("RS4", 256)
        w4 = m.at
        t_wg = load(WG, args["w_gate"])
        LAM = P1[0]

        def s5():
            tg = phases(0, pw_tok[0], cc_tok[0], V.last)
            hfree = [None, None]
            for b in range(4):
                for a in range(8):
                    n = 8 * b + a
                    ft, q = n // 4, n % 4
                    rows = slice(32 * q, 32 * q + 32)
                    i, bx, fr = sring.get()
                    mm(bx[:, 0:256], BR[rows, ft, :], US[rows, ft, :], *fr, us_t[ft], t_b1, t_b2,
                       start=True, stop=True, inc=False)
                    tt = mm(bx[:, 256:512], BI[rows, ft, :], US[rows, ft, :], start=True, stop=True)
                    if q == 0:
                        iy, by, fry = yring.get()
                        T.wait(*fry)
                    yield
                    if a == 0:
                        V.wait(tg)
                    c2 = TB[:, 0, a, :].unsqueeze(1).to_broadcast([128, 2, 256])
                    cc, ss = TB[:, 0, a, :], TB[:, 1, a, :]
                    H = HBs[n % 2]
                    tt_(MB_, v3(bx, 2), c2, MUL, tt)
                    tt_(GB_[:, 0, :], bx[:, 256:512], ss, MUL)
                    tv = tt_(GB_[:, 1, :], bx[:, 0:256], ss, MUL)
                    sring.free(i, tv)
                    tt_(MB_[:, 0, :], MB_[:, 0, :], GB_[:, 0, :], ADD)
                    tt_(MB_[:, 1, :], MB_[:, 1, :], GB_[:, 1, :], SUB)
                    mg = P1[2][:, n:n + 1].to_broadcast([128, 256])
                    for c in range(2):
                        scan_(GB_[:, c, :], mg, MB_[:, c, :], 0.0, MUL, ADD)
                    tt_(H, GB_, c2, MUL, hfree[n % 2])
                    tt_(MB_[:, 0, :], GB_[:, 1, :], ss, MUL)
                    tt_(MB_[:, 1, :], GB_[:, 0, :], ss, MUL)
                    tt_(H[:, 0, :], H[:, 0, :], MB_[:, 0, :], SUB)
                    tv = tt_(H[:, 1, :], H[:, 1, :], MB_[:, 1, :], ADD)
                    if a == 7 and b < 3:
                        tg = phases(b + 1, tv)
                    yield
                    mm(by[rows, 0:256], CR[:, n, :], H[:, 0, :], tv, start=True, stop=False, inc=False)
                    hfree[n % 2] = ty = mm(by[rows, 0:256], CI[:, n, :], H[:, 1, :], start=False, stop=True)
                    if q == 3:
                        yield
                        tv = stt(US[:, ft, :], US[:, ft, :], cv("ssm_d", ft), by[:, 0:256], MUL, ADD, ty)
                        yring.free(iy, tv)
            ta = act(US, US, ACT.Gelu_apprx_tanh, V.last)
            t_zs.append(split(ZS, US, ta))

        yring = Ring([PS[7]])
        assert not any(sring.held)
        sring = Ring(PS[4:7])
        V.wait(A.last)
        A.wait(V.last)
        T.wait(V.last, A.last)
        for e_ in (V, A):
            e_.wait(T.last)
        t_zs = []
        s5g = start(s5())

        V.wait(t_st)
        A.wait(t_st)
        g_tok = {}

        def alr_epi(bank, tt):
            tv = evac_rs(ALR, bank, tt, rows=slice(0, 16))
            g_tok["alr"] = tv
            return (tv,)

        gemm("w_in_2", 4096, 16, xn, alr_epi, width=16)

        def save(dst, key, act_fn=None, last=True):
            def f(bank, tt):
                tv = evac_rs(dst, bank, tt, side_free[0])
                g_tok[key] = tv
                return (tv,)
            return f
        side_free = [None]

        def vt_epi(dst, key):
            def f(b0, b1, tt):
                A.wait(side_free[0])
                act(dst[:, 0, :], b0, ACT.Copy, tt, scale=RST[:, 0:1])
                t = act(dst[:, 1, :], b1, ACT.Copy, scale=RST[:, 1:2])
                g_tok[key] = t
                return t
            return f

        def rms_out(bk_i, bk, t_o, wname, wcols, OS, h, gate, extra):
            ia, ba, fr = sring.get()
            ta = act(SQ[:, 0, :], bk, ACT.Square, t_o, sq_free[0], sq_free[1])
            mm(ba[:, 0:256], ones, SQ[:, 0, 0:256], ta, *fr, start=True, stop=False, inc=False)
            tt = mm(ba[:, 0:256], ones, SQ[:, 0, 256:512], start=False, stop=True)
            sq_free[0] = tt
            yield
            ta = rs_from(RS4, ba[:, 0:256], 256, tt)
            sring.free(ia, ta)
            for j in range(2):
                t = stt(OB[:, j, :], bk[:, 256 * j:256 * j + 256], wcols(j), RS4, MUL, MUL, ta)
            sring.free(bk_i, t)
            if gate is not None:
                t = tt_(OB, OB, gate, MUL)
            split(OS[:, 2 * h:2 * h + 2, :], OB, t)

        def gla(h):
            hv = h % 2
            i, bk, fr = sring.get()
            tt = mm(bk[:, 0:256], WG[:, 128 * h:128 * h + 128], ALR, *fr, g_tok["alr"], t_wg)
            yield
            act(GE1, bk[:, 0:256], ACT.Identity, tt, bias=cv("gla_b", h))
            sring.free(i, A.last)
            act(GE2, GE1, ACT.Abs)
            act(GE2, GE2, ACT.Exp, scale=-1.0)
            ta = act(GE2, GE2, ACT.Ln, bias=1.0)
            stt(GE1, GE1, 0.0, GE2, MIN, SUB, ta)
            tv = scan_(CUM, cs("creset"), GE1, 0.0, MUL, ADD)
            c3 = CUM.rearrange("p (a b) -> p a b", a=8)
            lastc = c3[:, :, 31:32]
            tv = tt_(GE3.rearrange("p (a b) -> p a b", a=8), lastc.to_broadcast([128, 8, 32]), c3, SUB)
            act(GE1, CUM, ACT.Exp, tv, scale=1.0 / 16)
            act(GE2, CUM, ACT.Exp, scale=-1.0 / 16)
            act(GE3, GE3, ACT.Exp, scale=1.0 / 16)
            ta = act(DL.unsqueeze(2), lastc, ACT.Exp, scale=1.0 / 16)
            stt(GE1, GQ, 128.0 ** -0.5, GE1, MUL, MUL, ta, g_tok["q"])
            tt_(GE3, GK, GE3, MUL, g_tok["k"])
            tv = tt_(GE2, GK, GE2, MUL)
            side_free[0] = tv
            yield
            i, bk, fr = sring.get()
            for j in range(2):
                transpose(bk[:, 128 * j:128 * j + 128], GE3[:, 128 * j:128 * j + 128], ident, tv, *fr, inc=False)
            for j in range(2):
                tt = mm(bk[:, 256 + 128 * j:384 + 128 * j], GE2[:, 128 * j:128 * j + 128],
                        GE1[:, 128 * j:128 * j + 128])
            yield
            for c in range(7):
                ta = act(KTM[:, c, :], bk[:, 128 * (c // 4):128 * (c // 4) + 128], ACT.Copy, tt,
                         scale=cs("cmask", 1, c % 4))
            tv = tt_(SC, v3(bk[:, 256:512], 2), cs("gmask").unsqueeze(1).to_broadcast([128, 2, 128]), MUL, tt, ta)
            sring.free(i, ta, tv)
            yield
            for p in range(4):
                i, bk, fr = sring.get()
                for c in (2 * p, 2 * p + 1):
                    if c == 7:
                        break
                    tt = mm(bk[:, 256 * (c % 2):256 * (c % 2) + 256], KTM[:, c, :],
                            GVT[:, c // 4, 256 * hv:256 * hv + 256], *fr, ta, g_tok["v"])
                yield
                for c in (2 * p, 2 * p + 1):
                    if c == 7:
                        break
                    src = bk[:, 256 * (c % 2):256 * (c % 2) + 256]
                    if c == 0:
                        ts = copy_(ST[:, 0, :], src, tt, o_last[0])
                    else:
                        ts = stt(ST[:, c, :], ST[:, c - 1, :], DL[:, c:c + 1], src, MUL, ADD, tt)
                sring.free(i, ts)
            yield
            i, bk, fr = sring.get()
            for d in range(2):
                for j in range(2):
                    mm(bk[:, 256 * d + 128 * j:256 * d + 128 * j + 128],
                       GVT[:, j, 256 * hv + 128 * d:256 * hv + 128 * d + 128], SC[:, j, :], *fr, tv, ts,
                       start=(j == 0), stop=False, inc=False)
                for c in range(1, 8):
                    tt = mm(bk[:, 256 * d + 32 * c:256 * d + 32 * c + 32], ST[:, c - 1, 128 * d:128 * d + 128],
                            GE1[:, 32 * c:32 * c + 32], start=False, stop=(c == 7))
            o_last[0] = tt
            V.wait(tt)
            A.wait(tt)
            yield
            act(GR, GR, ACT.Silu, g_tok["r"])
            yield from rms_out(i, bk, tt, "gla_norm", lambda j: cv("gla_norm", j), GOS, h, GR, 1.0)
            side_free[0] = V.last
        o_last = [None]

        cur = None
        for h in range(4):
            if h % 2 == 0:
                if cur:
                    flush()
                    finish(cur)
                gemm_t("w_in_2", 2048 + 512 * (h // 2), 16, xn, vt_epi(GVT, "v"))
                flush()
            elif cur:
                finish(cur)
            gemm("w_in_2", 1024 + 128 * h, 16, xn, save(GQ, "q"))
            gemm("w_in_2", 1536 + 128 * h, 16, xn, save(GK, "k"))
            for j in range(2):
                gemm("w_in_2", 3072 + 256 * h + 128 * j, 16, xn, save(GR[:, j, :], "r"))
            flush()
            cur = start(gla(h))
        finish(cur)
        finish(s5g)
        barrier(V, A, G)
        S.wait(V.last, A.last, T.last, G.last)

        m = Map(nc, R0 + 2 * 16384, end)
        DOS = v3(m("DOS", 8 * 512, F32R), 8)
        DQ0 = v3(m("DQ0", 4 * 256), 4)
        DVT0 = v3(m("DVT0", 1024), 2)
        w6 = m.at
        DQ = [DQ0, v3(m("DQ1", 4 * 256), 4)]
        DVT = [DVT0, v3(m("DVT1", 1024), 2)]
        DBI = m("DBI", 1024)
        DS = [m(f"DS{i}", 384) for i in range(2)]
        WT = m("WT", 384)
        DST = m("DST", 16)
        LQ = m("LQ", 8)
        DNW = m("DNW", 2)
        OB = v3(m("OB2", 512), 2)
        RS4 = m("RS42", 256)
        t_db = load(DBI, args["dbias"])
        ts_(DNW, cv("diff_norm", 0, 2), 0.8, None, MUL, None)
        dl = cv("diff_lam", 0, 4).rearrange("p (a b) -> p a b", b=2)
        tv = tt_(LQ[:, 0:2], dl[:, :, 0], dl[:, :, 1], MUL)
        i, bk, fr = sring.get()
        tt = mm(bk[:, 0:2], ones, LQ[:, 0:2], tv, *fr)
        ta = act(LQ[:, 2:4], bk[:, 0:2], ACT.Exp, tt)
        sring.free(i, ta)
        tt_(LQ[:, 4:5], LQ[:, 3:4], LQ[:, 2:3], SUB, ta)
        ts_(LQ[:, 4:5], LQ[:, 4:5], -(0.8 - 0.6), None, ADD, None)
        dq_t, dv_t = {}, {}
        dq_free, dv_free = [None, None], [None, None]

        def dq_epi(h, j):
            def f(bank, tt):
                tv = evac_rs(DQ[h % 2][:, j, :], bank, tt, dq_free[h % 2])
                dq_t[h] = tv
                return (tv,)
            return f

        def dv_epi(n):
            def f(b0, b1, tt):
                act(DVT[n % 2][:, 0, :], b0, ACT.Copy, tt, dv_free[n % 2], scale=RST[:, 0:1])
                dv_t[n] = act(DVT[n % 2][:, 1, :], b1, ACT.Copy, scale=RST[:, 1:2])
                return dv_t[n]
            return f

        def diff(h):
            Q = DQ[h % 2]
            VT = DVT[(h // 2) % 2]
            bks = []
            for j in range(2):
                i, bk, fr = sring.get()
                mm(bk[:, 0:256], Q[:, j, 128:256], Q[:, 2 + j, :], dq_t[h], *fr, inc=False)
                tt = mm(bk[:, 256:384], Q[:, j, 0:128], Q[:, 2 + j, 0:128])
                bks.append((i, bk))
            dq_free[h % 2] = tt
            yield
            bias = DBI[:, 256 * h:256 * h + 256]
            for j in range(2):
                i, bk = bks[j]
                stt(DS[j][:, 0:256], bk[:, 0:256], 128.0 ** -0.5, bias, MUL, ADD, tt, t_db)
                t = stt(DS[j][:, 256:384], bk[:, 256:384], 128.0 ** -0.5, bias[:, 128:256], MUL, ADD)
                sring.free(i, t)
                rmax_(DST[:, 2 * j:2 * j + 1], DS[j][:, 0:256])
                rmax_(DST[:, 2 * j + 1:2 * j + 2], DS[j][:, 256:384])
            tv = ts_(DST[:, 4:8], DST[:, 0:4], -1.0, None, MUL, None)
            for j in range(2):
                act(DS[j][:, 0:256], DS[j][:, 0:256], ACT.Exp, tv, bias=DST[:, 4 + 2 * j:5 + 2 * j],
                    accum=DST[:, 8 + 2 * j:9 + 2 * j])
                ta = act(DS[j][:, 256:384], DS[j][:, 256:384], ACT.Exp, bias=DST[:, 5 + 2 * j:6 + 2 * j],
                         accum=DST[:, 9 + 2 * j:10 + 2 * j])
            yield
            recip_(DST[:, 12:16], DST[:, 8:12], ta)
            ts_(DST[:, 14:16], DST[:, 14:16], LQ[:, 4:5], None, MUL, None)
            for b, c in ((0, slice(0, 256)), (1, slice(256, 384))):
                ts_(DS[0][:, c], DS[0][:, c], DST[:, 12 + b:13 + b], None, MUL, None)
                tv = stt(DS[0][:, c], DS[1][:, c], DST[:, 14 + b:15 + b], DS[0][:, c], MUL, ADD)
            i, bk, fr = sring.get()
            transpose(bk[:, 0:128], DS[0][:, 256:384], ident, tv, *fr, inc=False)
            transpose(bk[:, 128:256], DS[0][:, 0:128], ident, inc=False)
            tt = transpose(bk[:, 256:384], DS[0][:, 128:256], ident)
            V.wait(tt)
            yield
            ta = act(WT, bk[:, 0:384], ACT.Copy, tt)
            sring.free(i, ta)
            yield
            i, bk, fr = sring.get()
            for d in range(2):
                c = 256 * (h % 2) + 128 * d
                mm(bk[:, 256 * d:256 * d + 256], VT[:, 0, c:c + 128], WT[:, 0:256], ta, dv_t[h // 2], *fr,
                   start=True, stop=False, inc=False)
                tt = mm(bk[:, 256 * d + 128:256 * d + 256], VT[:, 1, c:c + 128], WT[:, 256:384],
                        start=False, stop=True)
            dv_free[(h // 2) % 2] = tt
            A.wait(tt)
            yield
            yield from rms_out2(i, bk, tt, h)

        def rms_out2(bk_i, bk, t_o, h):
            ia, ba, fr = sring.get()
            ta = act(SQ[:, 0, :], bk, ACT.Square, t_o, sq_free[0], sq_free[1])
            mm(ba[:, 0:256], ones, SQ[:, 0, 0:256], ta, *fr, start=True, stop=False, inc=False)
            tt = mm(ba[:, 0:256], ones, SQ[:, 0, 256:512], start=False, stop=True)
            sq_free[0] = tt
            yield
            ta = rs_from(RS4, ba[:, 0:256], 256, tt)
            sring.free(ia, ta)
            for j in range(2):
                t = stt(OB[:, j, :], bk[:, 256 * j:256 * j + 256], DNW[:, j:j + 1], RS4, MUL, MUL, ta)
            sring.free(bk_i, t)
            split(DOS[:, 2 * h:2 * h + 2, :], OB, t)

        cur = None
        for h in range(4):
            if h % 2 == 0:
                gemm_t("w_in_2", 6160 + 512 * (h // 2), 16, xn, dv_epi(h // 2))
            for j in range(2):
                gemm("w_in_2", 4112 + 256 * h + 128 * j, 16, xn, dq_epi(h, j))
            for j in range(2):
                gemm("w_in_2", 5136 + 256 * h + 128 * j, 16, xn, dq_epi(h, 2 + j))
            flush()
            if cur:
                finish(cur)
            cur = start(diff(h))
        m2 = Map(nc, w6, end)
        MS = v3(m2("MS", 16 * 512, F32R), 16)
        SG = DQ[0]
        VB = v3(DVT[0][:, 0, :], 2)
        V.wait(dq_free[0], dv_free[0])
        ms_t = []

        def merge_epi(key, n):
            sl = {"g0": 0, "g1": 1, "g2": 2, "gate": 3}

            def f(bank, tt):
                if key in sl:
                    tv = (evac if key == "gate" else evac_rs)(SG[:, sl[key], :], bank, tt)
                    if key == "gate":
                        sg_t[0] = act(SG, SG, ACT.Sigmoid, tv)
                    return (tv,)
                if key == "val":
                    tv = evac(VB[:, 0, :], bank, tt)
                    tt_(SG[:, 3, :], SG[:, 3, :], SG[:, 0, :], MUL, sg_t[0])
                    tt_(VB[:, 0, :], VB[:, 0, :], SG[:, 3, :], MUL)
                    return (tv,)
                c = 1 if key == "yb" else 2
                tv = evac(VB[:, 1, :], bank, tt)
                tt_(VB[:, 1, :], VB[:, 1, :], SG[:, c, :], MUL)
                t = tt_(VB[:, 0, :], VB[:, 0, :], VB[:, 1, :], ADD)
                if key == "yc":
                    ms_t.append(split(MS[:, n, :], VB[:, 0, :], t))
                return (tv,)
            return f
        sg_t = [None]
        for n in range(16):
            for c in range(3):
                gemm("w_in_2", 7184 + 2048 * c + 128 * n, 16, xn, merge_epi(f"g{c}", n))
            flush()
            gemm("ssm_w_glu_2", 2048 + 128 * n, 8, lambda k: ZS[:, k, :], merge_epi("gate", n), t_zs[0])
            gemm("ssm_w_glu_2", 128 * n, 8, lambda k: ZS[:, k, :], merge_epi("val", n))
            gemm("gla_w_br_2", 128 * n, 8, lambda k: GOS[:, k, :], merge_epi("yb", n))
            if n == 0:
                flush()
                finish(cur)
                T.wait(V.last)
                for e_ in (V, A):
                    e_.wait(V.last, A.last, T.last)
            gemm("diff_w_br_2", 128 * n, 8, lambda k: DOS[:, k, :], merge_epi("yc", n))
        flush()
        m = Map(nc, R0, end)
        X = v3(m("X3", 16 * 256), 16)
        TMP = v3(m("TMP3", 512), 2)
        t_x = load(X, scratch, V.last, A.last, T.last, t_st)
        V.wait(T.last)
        A.wait(T.last)
        nm = Norm(X, "norm_ffn", TMP)
        t = out_proj("w_out_2", 16, lambda k: MS[:, k, :], X, t_x, ms_t[-1], nm)

        t_st = store_x(X, t)
        nm.end()
        barrier(V, A)
        m = Map(nc, R0, end)
        HS = v3(m("HS", 43 * 512, F32R), 43)
        X = v3(m("X4", 16 * 256), 16)
        w5 = m.at
        TMP = v3(m("TMP4", 512), 2)
        S.wait(t_st, A.last, V.last, T.last)
        t_x = load(X, scratch)
        UP = v3(m("UP", 2 * 258), 2)
        VG = TMP
        memset_(UP[:, :, 0:2], 0.0, E=V)

        def up_epi(i, s):
            def f(bank, tt):
                tv = evac_rs(UP[:, s, 2:258], bank, tt)
                k = 43 * s + i
                t = conv(VG[:, s, :], UP[:, s, :], lambda t: cv("ffn_w", 86 * t + k), cv("ffn_b", k), 3,
                         tv, V.last)
                if s == 0:
                    return (tv,)
                ta = act(VG[:, 1, :], VG[:, 1, :], ACT.Silu, t)
                t = tt_(VG[:, 0, :], VG[:, 0, :], VG[:, 1, :], MUL, ta)
                hs_t.append(split(HS[:, i, :], VG[:, 0, :], t))
                return (tv,)
            return f
        hs_t = []
        for i in range(43):
            gemm("ffn_w_up_2", 128 * i, 16, xn, up_epi(i, 0))
            gemm("ffn_w_up_2", 5504 + 128 * i, 16, xn, up_epi(i, 1))
        flush()
        SUMB = sring.get()
        T.wait(hs_t[-1], *SUMB[2])
        sums = []

        def down_epi(n):
            def f(bank, tt):
                t = tt_(X[:, n, :], X[:, n, :], bank[:, 0:256], ADD, tt, t_x)
                tq = act(SQ4[:, n % 4, :], X[:, n, :], ACT.Square, t, sq4_free[n % 4])
                for g in sums:
                    g()
                sums[:] = [lambda: sq4_free.__setitem__(n % 4, mm(
                    SUMB[1][:, 0:256], ones, SQ4[:, n % 4, :], tq, start=(n == 0), stop=(n == 15)))]
                return (t,)
            return f
        for n in range(16):
            gemm("ffn_w_down_2", 128 * n, 43, lambda k: HS[:, k, :], down_epi(n))
        flush()
        for g in sums:
            g()
        ta = rs_from(RSB, SUMB[1][:, 0:256], 2048, T.last, V.last)
        for k in range(16):
            t = stt(X[:, k, :], X[:, k, :], cv("norm_final", k), RSB, MUL, MUL, ta)
            if k % 4 == 3:
                S.op(lambda e, k=k: e.dma_start(out[:, k - 3:k + 1, :], X[:, k - 3:k + 1, :]).then_inc(out_sem, 16),
                     t, inc=False, chain=False)
        S.wait((out_sem, 64))
        S.wait((st_sem, stores[0]))
        assert blk[0] == NBLOCKS, (blk[0], NBLOCKS)

        block = ctx.enter_context(nc.Block())

        @block.sync
        def _(e):
            S.run(e)

        @block.scalar
        def _(e):
            A.run(e)

        @block.vector
        def _(e):
            V.run(e)

        @block.gpsimd
        def _(e):
            G.run(e)

        @block.tensor
        def _(e):
            T.run(e)
    return order



def cols(a, n):
    return np.ascontiguousarray(np.asarray(a, np.float32).reshape(-1, 128).T)


def vectors(I):
    v = np.zeros((128, NVEC), np.float32)

    def put(name, a):
        v[:a.shape[0], VOFF[name]:VOFF[name] + a.shape[1]] = a

    for name, key in [("e_norm", "e_norm"), ("conv_l_w", "e_conv_l_w"), ("conv_l_b", "e_conv_l_b"),
                      ("lru_ba", "e_lru_ba"), ("lru_bx", "e_lru_bx"), ("lru_lam", "e_lru_lam"),
                      ("conv_m_w", "e_conv_m_w"), ("conv_m_b", "e_conv_m_b"), ("m_norm", "e_m_norm"),
                      ("o_norm", "o_norm"), ("o_conv_w", "o_conv_w"), ("o_conv_b", "o_conv_b"),
                      ("gnorm", "o_gnorm"), ("final_norm", "final_norm"), ("norm_mix", "norm_mix_w_2"),
                      ("ssm_d", "ssm_d_2"), ("gla_b", "gla_b_gate_2"), ("gla_norm", "gla_norm_w_2"),
                      ("diff_norm", "diff_norm_w_2"), ("norm_ffn", "norm_ffn_w_2"),
                      ("ffn_w", "ffn_conv_w_2"), ("ffn_b", "ffn_conv_b_2"), ("norm_final", "norm_final_w_2")]:
        put(name, cols(I[key], 0))
    b = I["e_b_if"][0]
    v[0:4, VOFF["b_if"]] = b[0:4]
    v[32:36, VOFF["b_if"]] = b[4:8]
    put("dt_bias", I["o_dt_bias"][0].reshape(64, 1))
    put("a_log", I["o_a_log"][0].reshape(64, 1))
    put("d_skip", np.repeat(I["o_d_skip"][0].reshape(32, 2), 64, axis=1).T)
    put("a_re", I["ssm_a_re_2"][0].reshape(32, 128).T)
    put("a_im", I["ssm_a_im_2"][0].reshape(32, 128).T)
    put("log_dt", np.repeat(I["ssm_log_dt_2"][0].reshape(32, 2), 64, axis=1).T)
    put("diff_lam", np.stack([I[f"diff_lam_{n}_2"][0] for n in ("q1", "k1", "q2", "k2")], axis=1))
    return v


def shapes():
    c = np.zeros((128, NSHP), np.float32)
    p = np.arange(128)[:, None]
    j = np.arange(256)[None, :]

    def put(name, a):
        c[:, SOFF[name]:SOFF[name] + a.shape[1]] = a

    put("ident", np.eye(128, dtype=np.float32))
    put("ones", np.ones((128, 128), np.float32))
    m = np.where(p <= j, 0.0, NEG).astype(np.float32)
    put("mask", np.concatenate([m, m[:, 0:128]], axis=1))
    q = np.arange(128)[None, :]
    put("gmask", ((p <= q) & (p // 32 == q // 32)).astype(np.float32))
    put("creset", np.broadcast_to((j % 32 != 0).astype(np.float32), (128, 256)))
    put("cmask", (p // 32 == np.arange(8)[None, :] % 4).astype(np.float32))
    rel = (128 + p - j).astype(np.float32)
    d = [np.where(rel >= 0, -(2.0 ** (-8.0 * (h + 1) / 4)) * rel, NEG) for h in range(4)]
    return c, np.concatenate(d, axis=1).astype(np.float32)


def pack_weights(I, order):
    w = np.zeros((NUNITS, 128, UB, 128), np.float32)
    for n, (name, k, c, width) in enumerate(order):
        a = I[name][0]
        if isinstance(c, tuple):
            a, c = a[c[0]], c[1]
        w[n // UB, :, n % UB, :width] = a[128 * k:128 * k + 128, c:c + width]
    return w.reshape(NUNITS, 128, UB * 128)


def host_arrays(I, order):
    I = {k: np.asarray(v) for k, v in I.items()}
    x = np.ascontiguousarray(I["x"][0].T.reshape(16, 128, 256).transpose(1, 0, 2))
    wif = I["e_w_if"][0].reshape(32, 128, 8).transpose(1, 0, 2)
    w_if = np.zeros((128, 32, 36), np.float32)
    w_if[:, :, 0:4] = wif[:, :, 0:4]
    w_if[:, :, 32:36] = wif[:, :, 4:8]
    b = {}
    for n in ("re", "im"):
        s = I[f"ssm_b_{n}_2"][0].reshape(8, 4, 2, 64, 16)
        t = np.zeros((4, 2, 16, 8, 2, 64), np.float32)
        c = np.zeros((2, 64, 32, 2, 16), np.float32)
        g = I[f"ssm_c_{n}_2"][0].reshape(32, 2, 16, 64)
        for i in range(2):
            t[:, i, :, :, i, :] = s[:, :, i].transpose(1, 3, 0, 2)
            c[i, :, :, i, :] = g[:, i].transpose(2, 0, 1)
        b["b_" + n] = t.reshape(128, 8, 128)
        b["c_" + n] = c.reshape(128, 32, 32)
    shp, dbias = shapes()
    return {"x": x, "vec": vectors(I), "shp": shp, "dbias": dbias, "w_if": w_if, "w_gate": I["gla_w_gate_2"][0],
            "w": pack_weights(I, order), **b}


_SHAPES = {"x": (128, 16, 256), "vec": (128, NVEC), "shp": (128, NSHP), "dbias": (128, 1024),
           "w_if": (128, 32, 36), "w_gate": (16, 512), "w": (NUNITS, 128, UB * 128),
           "b_re": (128, 8, 128), "b_im": (128, 8, 128), "c_re": (128, 32, 32), "c_im": (128, 32, 32)}


def program(nc):
    args = {n: nc.dram_tensor(f"in_{n}", s, F32, kind="ExternalInput").ap() for n, s in _SHAPES.items()}
    out = nc.dram_tensor("out_0", (128, 16, 256), F32, kind="ExternalOutput").ap()
    scratch = nc.dram_tensor("scratch_0", (128, 16, 256), F32).ap()
    return build(nc, args, out, scratch)


def kernel(**inputs):
    import concourse.bacc as _bacc
    from concourse.bass_utils import run_bass_kernel_spmd as _run

    nc = _bacc.Bacc("TRN2", target_bir_lowering=False, num_devices=1)
    order = program(nc)
    arrays = {f"in_{n}": np.ascontiguousarray(a) for n, a in host_arrays(inputs, order).items()}
    r = _run(nc, [arrays], core_ids=[0])
    o = r.results[0]["out_0"]
    return np.ascontiguousarray(o.transpose(1, 0, 2).reshape(2048, 256).T)[None]
```

```python
from contextlib import ExitStack

import numpy as np

from concourse import mybir

F32 = mybir.dt.float32
F32R = mybir.dt.float32r
ACT = mybir.ActivationFunctionType
ALU = mybir.AluOpType
AX = mybir.AxisListType.X

UB = 8
NRAW = 4
NW = 4
NEG = -1.0e30
TWO_PI = 6.283185307179586


VEC = [
    ("e_norm", 16), ("conv_l_w", 64), ("conv_l_b", 16), ("lru_ba", 16), ("lru_bx", 16),
    ("lru_lam", 16), ("conv_m_w", 64), ("conv_m_b", 16), ("b_if", 1), ("m_norm", 16),
    ("o_norm", 16), ("o_conv_w", 192), ("o_conv_b", 48), ("dt_bias", 1), ("a_log", 1),
    ("d_skip", 32), ("gnorm", 32), ("final_norm", 16), ("norm_mix", 16), ("a_re", 32),
    ("a_im", 32), ("log_dt", 32), ("ssm_d", 8), ("gla_b", 4), ("gla_norm", 2),
    ("diff_lam", 4), ("diff_norm", 2), ("norm_ffn", 16), ("ffn_w", 258), ("ffn_b", 86),
    ("norm_final", 16),
]
VOFF = {}
_at = 0
for _n, _c in VEC:
    VOFF[_n] = _at
    _at += _c
NVEC = _at
SHP = [("ident", 128), ("ones", 128), ("mask", 384), ("gmask", 128), ("creset", 256), ("cmask", 8)]
SOFF = {}
_at = 0
for _n, _c in SHP:
    SOFF[_n] = _at
    _at += _c
NSHP = _at

NBLOCKS = 16 * 64 + 4 * (8 + 8 + 16 + 16) + 16 * 2 + 32 * 16 + 81 * 16 + 32 * 16 + \
    16 * (8 + 4 + 4 + 8 + 8 + 1 + 8 + 8 + 8 + 48) + 32 * 8 + 16 * 8 * 2 + 16 * 16 + 86 * 16 + 43 * 16
NUNITS = -(-NBLOCKS // UB)


class Eng:

    def __init__(self, name, sem):
        self.name, self.sem, self.n, self.q, self.seen = name, sem, 0, [], {}

    def wait(self, *tokens):
        for t in tokens:
            if t is None:
                continue
            sem, v = t
            if self.seen.get(id(sem), 0) < v:
                self.seen[id(sem)] = v
                self.q.append(lambda e, sem=sem, v=v: e.wait_ge(sem, v))

    def op(self, fn, *waits, inc=True, chain=True):
        self.wait(*waits)
        if chain and self.n:
            self.wait((self.sem, self.n))
        if inc:
            self.n += 1
            self.q.append(lambda e: fn(e).then_inc(self.sem, 1))
            return (self.sem, self.n)
        self.q.append(fn)
        return None

    @property
    def last(self):
        return (self.sem, self.n) if self.n else None

    def run(self, e):
        for f in self.q:
            f(e)


class Ring:

    def __init__(self, banks, toks, held, ids):
        self.banks, self.toks, self.held, self.ids, self.i = banks, toks, held, ids, 0

    def get(self):
        n = len(self.ids)
        j = next((j for j in range(self.i, self.i + n) if not self.held[self.ids[j % n]]), None)
        assert j is not None, "no bank is free"
        self.i = j % n + 1
        k = self.ids[j % n]
        self.held[k] = True
        return k, self.banks[k], self.toks[k]

    def free(self, k, *tokens):
        assert self.held[k]
        self.toks[k], self.held[k] = tokens, False


class Map:

    def __init__(self, nc, base, end):
        self.nc, self.at, self.end = nc, base, end

    def __call__(self, name, cols, dt=F32, rows=128):
        t = self.nc.alloc_sbuf_tensor_at(name, [rows, cols], dt, offset=self.at)
        self.at += (cols * 4 + 31) // 32 * 32
        assert self.at <= self.end, (name, self.at, self.end)
        return t[:, :]


def v3(ap, a):
    return ap.rearrange("p (a b) -> p a b", a=a)


def build(nc, args, out, scratch):
    order = []
    ctx = ExitStack()
    with ctx:
        def sem(name):
            return ctx.enter_context(nc.semaphore(name))

        base = (nc.sbuf_base + 31) // 32 * 32
        end = nc.sbuf_usable_end
        fx = Map(nc, base, end)
        RAW = v3(fx("RAW", NRAW * UB * 128), NRAW)
        WH = v3(fx("WH", NW * UB * 128, F32R), NW)
        WL = v3(fx("WL", NW * UB * 128, F32R), NW)
        XN = v3(fx("XN", 16 * 512, F32R), 16)
        CV = fx("CV", NVEC)
        CS = fx("CS", NSHP)
        RSB = fx("RSB", 256)
        SQF = fx("SQ", 1024)
        SQ, SQ4 = v3(SQF, 2), v3(SQF, 4)
        RS1 = fx("RS1", 256)
        RST = fx("RST", 2)
        identr = fx("identr", 128, F32R)
        maskr = fx("maskr", 384, F32R)
        EPSC = fx("epsc", 1)
        R0 = fx.at

        PS = [ctx.enter_context(nc.psum_tensor(f"ps{i}", [128, 512], F32))[:, :] for i in range(8)]

        T = Eng("T", sem("s_t"))
        V = Eng("V", sem("s_v"))
        A = Eng("A", sem("s_a"))
        G = Eng("G", sem("s_g"))
        S = Eng("S", sem("s_s"))
        raw_sem = [sem(f"s_raw{i}") for i in range(NRAW)]
        in_sems = [sem(f"s_in{i}") for i in range(20)]
        st_sem = sem("s_store")
        out_sem = sem("s_out")

        def cv(name, c, n=1, rows=slice(0, 128)):
            return CV[rows, VOFF[name] + c:VOFF[name] + c + n]

        def cs(name, n=None, c=0, rows=slice(0, 128)):
            w = dict(SHP)[name]
            return CS[rows, SOFF[name] + c:SOFF[name] + c + (n or w)]

        ident, ones = cs("ident"), cs("ones")

        n_in = [0]

        def load(dst, src, *waits):
            s = in_sems[n_in[0]]
            n_in[0] += 1
            S.op(lambda e: e.dma_start(dst, src).then_inc(s, 16), *waits, inc=False, chain=False)
            return (s, 16)

        t_cv = load(CV, args["vec"])
        t_cs = load(CS, args["shp"])

        raw_free = [None] * NRAW
        w_free = [None] * NW
        loaded, split_at = [0], [0]
        split_tok, round_tok = {}, {}

        def load_unit():
            u = loaded[0]
            loaded[0] += 1
            k = u % NRAW
            S.op(lambda e: e.dma_start(RAW[:, k, :], args["w"][u]).then_inc(raw_sem[k], 16),
                 *(raw_free[k] or ()), inc=False, chain=False)

        def round_unit():
            u = split_at[0]
            split_at[0] += 1
            k, w = u % NRAW, u % NW
            got = (raw_sem[k], 16 * (u // NRAW + 1))
            round_tok[u] = (got, A.op(lambda e: e.activation(WH[:, w, :], RAW[:, k, :], ACT.Copy),
                                      got, w_free[w], chain=False), w_free[w])

        def rest_unit(u):
            k, w = u % NRAW, u % NW
            tv = V.op(lambda e: e.tensor_tensor(WL[:, w, :], RAW[:, k, :], WH[:, w, :].bitcast(F32),
                                                ALU.subtract), *round_tok[u], chain=False)
            split_tok[u] = tv
            raw_free[k] = (tv,)
            if loaded[0] < NUNITS:
                load_unit()

        for _ in range(NRAW):
            load_unit()

        blk = [0]
        since = [0]
        every = [16]

        deferred = []

        def run_deferred():
            q, deferred[:] = list(deferred), []
            for f in q:
                f()

        def unit_ready():
            u = blk[0] // UB
            if blk[0] % UB == 0:
                run_deferred()
                while split_at[0] < min(u + NW, NUNITS):
                    round_unit()
                for w in range(u, min(u + NW - 1, NUNITS)):
                    if w not in split_tok:
                        rest_unit(w)
            return u, blk[0] % UB

        def unit_done(u, b):
            if b == UB - 1:
                w_free[u % NW] = T.last

        tasks = []

        def step(g):
            try:
                next(g)
                return True
            except StopIteration:
                return False

        def tick():
            for g in list(tasks):
                if not step(g):
                    tasks.remove(g)

        def start(g):
            tasks.append(g)
            return g

        def finish(*gs):
            while any(g in tasks for g in gs):
                tick()

        btoks, bheld = [()] * 8, [False] * 8

        def ring(*ids):
            return Ring(PS, btoks, bheld, list(ids))

        gring, sring = ring(0, 1, 2, 3), ring(4, 5, 6, 7)
        pend = []

        def flush():
            while pend:
                pend.pop(0)()

        def gemm(name, c0, kt, rhs, epi, *waits, k0=0, width=128):
            i, bank, fr = gring.get()
            T.wait(*fr, *waits)
            for k in range(kt):
                order.append((name, k0 + k, c0, width))
                u, b = unit_ready()
                T.wait(split_tok[u])
                h, l = WH[:, u % NW, b * 128:b * 128 + 128], WL[:, u % NW, b * 128:b * 128 + 128]
                x = rhs(k)
                if rhs is xn:
                    T.wait(xn_tok[k])
                last = k == kt - 1
                for j, (p, q) in enumerate(((h, x[:, 0:256]), (h, x[:, 256:512]), (l, x[:, 0:256]))):
                    tt = T.op(lambda e, p=p, q=q, s=(k == 0 and j == 0), f=(last and j == 2): e.matmul(
                        bank[:, 0:256], p, q, start=s, stop=f, skip_group_check=True),
                        inc=(j == 2 and (last or b == UB - 1)), chain=False)
                unit_done(u, b)
                blk[0] += 1
                since[0] += 1
                if since[0] >= every[0] and not last:
                    since[0] = 0
                    flush()
                    tick()
            flush()
            pend.append(lambda: gring.free(i, *epi(bank, tt)))
            if since[0] >= every[0]:
                since[0] = 0
                tick()

        def gemm_t(name, c0, kt, lhs, epi, *waits):
            i0, b0, f0 = gring.get()
            i1, b1, f1 = gring.get()
            T.wait(*f0, *f1, *waits)
            for k in range(kt):
                for j in range(4):
                    order.append((name, k, c0 + 128 * j, 128))
                u, b = unit_ready()
                assert b % 4 == 0
                T.wait(split_tok[u])
                h, l = WH[:, u % NW, b * 128:b * 128 + 512], WL[:, u % NW, b * 128:b * 128 + 512]
                x = lhs(k)
                if lhs is xn:
                    T.wait(xn_tok[k])
                for t, bank in ((0, b0), (1, b1)):
                    xh, xl = x[:, 128 * t:128 * t + 128], x[:, 256 + 128 * t:384 + 128 * t]
                    for m, (p, q) in enumerate(((xh, h), (xh, l), (xl, h))):
                        fin = t == 1 and m == 2 and (k == kt - 1 or b == UB - 4)
                        tt = T.op(lambda e, p=p, q=q, bank=bank, s=(k == 0 and m == 0), f=(k == kt - 1 and m == 2):
                                  e.matmul(bank, p, q, start=s, stop=f, skip_group_check=True),
                                  inc=fin, chain=False)
                blk[0] += 4
                unit_done(u, b + 3)
                since[0] += 4
                if since[0] >= every[0] and k < kt - 1:
                    since[0] = 0
                    flush()
                    tick()
            flush()

            def go():
                t = epi(b0, b1, tt)
                gring.free(i0, t)
                gring.free(i1, t)
            pend.append(go)
            if since[0] >= every[0]:
                since[0] = 0
                tick()

        def evac(dst, bank, *waits, rows=slice(0, 128)):
            return copy_(dst, bank[rows, 0:256], *waits)

        def evac_rs(dst, bank, *waits, rows=slice(0, 128)):
            return tt_(dst, bank[rows, 0:256], RSB[rows, :], ALU.mult, *waits)

        def xn(k):
            return XN[:, k, :]

        def copy_(dst, src, *waits):
            return V.op(lambda e: e.tensor_copy(dst, src), *waits)

        def memset_(dst, v, E=V):
            return E.op(lambda e: e.memset(dst, v))

        def rmax_(dst, src):
            return V.op(lambda e: e.tensor_reduce(dst, src, AX, MAX))

        def recip_(dst, src, *waits):
            return V.op(lambda e: e.reciprocal(dst, src), *waits)

        def scan_(dst, a, b, init, o0, o1, *waits):
            return V.op(lambda e: e.tensor_tensor_scan(dst, a, b, init, o0, o1), *waits)

        def act(dst, src, f, *waits, bias=0.0, scale=1.0, accum=None):
            if accum is None:
                return A.op(lambda e: e.activation(dst, src, f, bias=bias, scale=scale), *waits)
            return A.op(lambda e: e.activation(dst, src, f, bias=bias, scale=scale, accum_out=accum), *waits)

        def tt_(dst, a, b, op, *waits, E=None):
            return (E or V).op(lambda e: e.tensor_tensor(dst, a, b, op), *waits)

        def ts_(dst, a, s1, s2, o0, o1, *waits, E=None):
            if s2 is None:
                return (E or V).op(lambda e: e.tensor_scalar(dst, a, s1, None, o0), *waits)
            return (E or V).op(lambda e: e.tensor_scalar(dst, a, s1, s2, o0, o1), *waits)

        def stt(dst, a, s, b, o0, o1, *waits, E=None):
            return (E or V).op(lambda e: e.scalar_tensor_tensor(out=dst, in0=a, scalar=s, in1=b, op0=o0, op1=o1), *waits)

        MUL, ADD, SUB, MAX, MIN = ALU.mult, ALU.add, ALU.subtract, ALU.max, ALU.min

        def mm(dst, l, r, *waits, start=True, stop=True, inc=True):
            return T.op(lambda e: e.matmul(dst, l, r, start=start, stop=stop, skip_group_check=True),
                        *waits, inc=inc, chain=False)

        def transpose(dst, src, idn, *waits, inc=True):
            return T.op(lambda e: e.transpose(dst, src, idn), *waits, inc=inc, chain=False)

        def split(dst, src, t_src, *waits):
            n = len(src.shape)
            hi = dst[:, :, 0:256] if n == 3 else dst[:, 0:256]
            lo = dst[:, :, 256:512] if n == 3 else dst[:, 256:512]
            ta = act(hi, src, ACT.Copy, t_src, *waits)
            return tt_(lo, src, hi.bitcast(F32), SUB, ta, *waits)

        def barrier(*engines):
            toks = [x.last for x in (T, V, A, G)]
            for x in engines:
                x.wait(*toks)

        def softplus(dst, x, t1, t2, t_x, positive_only=False):
            act(t1, x, ACT.Abs, t_x)
            ta = act(t1, t1, ACT.Exp, scale=-1.0)
            tv = ts_(t2, t1, 1.0, None, ADD, None, ta)
            ta = act(dst, t2, ACT.Ln, tv)
            ts_(t2, t2, -1.0, 1e-30, ADD, ADD, ta)
            recip_(t2, t2)
            stt(dst, dst, 1e-30, t2, ADD, MUL)
            tt_(dst, dst, t1, MUL)
            return stt(dst, x, 0.0, dst, MAX, ADD)

        def rs_from(dst, bank_ap, n, t_ps, *waits):
            act(dst, bank_ap, ACT.Ln, t_ps, *waits, bias=EPSC, scale=1.0 / n)
            return act(dst, dst, ACT.Exp, scale=-0.5)

        def sumsq(src, nt, t_src, bank, *waits):
            tt = None
            for k in range(0, nt, 2):
                w = (k // 2) % 2
                ta = act(SQ[:, w, :], src(k), ACT.Square, t_src, sq_free[w])
                mm(bank[:, 0:256], ones, SQ[:, w, 0:256], ta, *waits, start=(k == 0), stop=False, inc=False)
                tt = mm(bank[:, 0:256], ones, SQ[:, w, 256:512], start=False, stop=(k == nt - 2))
                sq_free[w] = tt
            return tt

        sq_free = [None, None]

        class Norm:

            def __init__(self, X, wname, tmp, first=None):
                self.X, self.w, self.tmp, self.first = X, wname, tmp, first
                self.i, self.bank, self.fr = sring.get()
                if first:
                    self.j, self.bank2, self.fr2 = sring.get()
                self.later, self.n = [], 0
                self.tmp_free = [None, None]

            def run_later(self):
                q, self.later = self.later, []
                for f in q:
                    f()

            def tile(self, t_x):
                k, self.n = self.n, self.n + 1
                X, tmp = self.X[:, k, :], self.tmp[:, k % 2, :]
                last = k == 15
                t = t_x
                if self.first:
                    t = ts_(tmp, X, cv(self.first, k), None, MUL, None, t_x, self.tmp_free[k % 2])
                    ta2 = act(SQ4[:, 2 + k % 2, :], tmp, ACT.Square, t, sq4_free[2 + k % 2])
                    t = ts_(tmp, tmp, cv(self.w, k), None, MUL, None, ta2)
                else:
                    t = ts_(tmp, X, cv(self.w, k), None, MUL, None, t_x, self.tmp_free[k % 2])
                self.run_later()
                hi, lo = XN[:, k, 0:256], XN[:, k, 256:512]
                ta = act(hi, tmp, ACT.Copy, t)
                tq = act(SQ4[:, k % 2, :], X, ACT.Square, t_x, sq4_free[k % 2])

                def rest():
                    xn_tok[k] = self.tmp_free[k % 2] = tt_(lo, tmp, hi.bitcast(F32), SUB, ta)
                    sq4_free[k % 2] = self.tt = mm(self.bank[:, 0:256], ones, SQ4[:, k % 2, :], tq, *self.fr,
                                                   start=(k == 0), stop=last)
                    if self.first:
                        sq4_free[2 + k % 2] = self.tt = mm(self.bank2[:, 0:256], ones, SQ4[:, 2 + k % 2, :],
                                                           *self.fr2, start=(k == 0), stop=last)
                self.later.append(rest)
                if last:
                    self.run_later()

            def end(self, rst=None):
                ta = rs_from(RSB, self.bank[:, 0:256], 2048, self.tt, V.last)
                sring.free(self.i, ta)
                if self.first:
                    V.op(lambda e: e.tensor_copy(RS1, RSB), ta)
                    t = V.last
                    t = tt_(RSB, RSB, RSB, MUL)
                    t = tt_(RSB, RSB, self.bank2[:, 0:256], MUL, self.tt)
                    sring.free(self.j, t)
                    ta = rs_from(RSB, RSB, 2048, t)
                    ta = tt_(RSB, RSB, RS1, MUL, ta)
                if rst is not None:
                    i, b, fr = sring.get()
                    mm(b[:, 0:1], RSB[0:1, 0:128], ones[0:1, 0:1], ta, *fr, inc=False)
                    tt = mm(b[:, 1:2], RSB[0:1, 128:256], ones[0:1, 0:1])
                    t = copy_(rst, b[:, 0:2], tt)
                    sring.free(i, t)
                    A.wait(t)
                V.wait(ta)
                return ta

        sq4_free = [None] * 4
        xn_tok = [None] * 16

        memset_(EPSC, 1e-6, E=V)
        copy_(identr, ident, t_cs)
        t0 = copy_(maskr, cs("mask"))
        A.wait(t0, t_cv, t_cs)
        V.wait(t_cv, t_cs)
        T.wait(t_cv, t_cs, t0)
        G.wait(t_cv, t_cs, t0)

        m = Map(nc, R0, end)
        YS = v3(m("YS1", 32 * 512, F32R), 32)
        ys0 = R0
        OZ = v3(m("OZ", 16 * 256), 16)
        w1 = m.at
        mm_ = Map(nc, ys0, end)
        XMS = [v3(mm_(f"XMS{i}", 4 * 512, F32R), 4) for i in range(2)]
        XCS = [v3(mm_(f"XCS{i}", 4 * 512, F32R), 4) for i in range(2)]
        QKV = [(v3(mm_(f"Q{i}", 512), 2), v3(mm_(f"K{i}", 512), 2), v3(mm_(f"VT{i}", 1024), 2)) for i in range(4)]
        m = Map(nc, w1, end)
        WIF = m("WIF", 32 * 36).rearrange("p (a b) -> p a b", a=32)
        XMP = [v3(m(f"XMP{i}", 4 * 259), 4) for i in range(2)]
        XMC = v3(m("XMC", 1024), 4)
        VF = v3(m("VF", 1024), 4)
        t_wif = load(WIF, args["w_if"])
        mt = Map(nc, w1 + 5120, end)
        X0 = v3(mt("X0", 16 * 256), 16)
        TMP0 = v3(mt("TMP0", 512), 2)
        nm = Norm(X0, "e_norm", TMP0)
        for q in range(4):
            t_x = load(X0[:, 4 * q:4 * q + 4, :], args["x"][:, 4 * q:4 * q + 4, :])
            for k in range(4):
                nm.tile(t_x)
        nm.end()
        barrier(V, A)
        for i in range(2):
            memset_(XMP[i][:, :, 0:3], 0.0, E=V)

        def conv(dst, src, w, b, taps, t_src, *waits):
            tv = ts_(dst, src[:, taps - 1:taps + 255], w(taps - 1), b, MUL, ADD, t_src, *waits)
            for t in range(taps - 2, -1, -1):
                tv = stt(dst, src[:, t:t + 256], w(t), dst, MUL, ADD, tv)
            return tv

        t_xm = {}
        xms_free, xcs_free, xmp_free = [(), ()], [(), ()], [None, None]
        t_q, t_k, t_vt = {}, {}, {}
        gi, GB, gfr = sring.get()
        gate_n = [0]
        qk_toks = {}
        conv_toks = {}

        def xm_epi(h, j):
            def f(bank, tt):
                p = h % 2
                tv = evac_rs(XMP[p][:, j, 3:259], bank, tt, xmp_free[p])
                if j == 3:
                    finish_xm(h, tv)
                return (tv,)
            return f

        def finish_xm(h, tv):
            p = h % 2
            for j in range(4):
                k = 4 * h + j
                t = conv(XMC[:, j, :], XMP[p][:, j, :], lambda t, k=k: cv("conv_m_w", 16 * t + k),
                         cv("conv_m_b", k), 4, tv)
            t = act(XMC, XMC, ACT.Silu, t)
            t_xc = split(XCS[p], XMC, t, *xcs_free[p])
            t_x_ = split(XMS[p], XMP[p][:, :, 3:259], tv, *xms_free[p])
            xmp_free[p] = t_x_
            conv_toks[h] = (t_xc, t_x_)

        def gate_mm(kt, src, tok, last=False):
            tt = mm(GB[0:36, 0:256], WIF[:, kt, :], src, tok, t_wif, start=(gate_n[0] == 0),
                    stop=(gate_n[0] == 31))
            gate_n[0] += 1
            return tt

        vf_i = [0]
        vf_free = [None] * 4
        side_q = []

        def qk_epi(h, j, isk):
            def f(bank, tt):
                dst = QKV[h][1 if isk else 0][:, j, :]
                tv = evac(dst, bank, tt)
                t = tv
                if isk:
                    t = act(dst, dst, ACT.Copy, tv, scale=0.0625)
                qk_toks.setdefault(h, []).append(t)
                side_q.append(lambda: gate_mm((8 if isk else 0) + 2 * h + j, dst, t))
                return (tv,)
            return f

        def v_epi(h, j):
            def f(bank, tt):
                s = vf_i[0] % 4
                vf_i[0] += 1
                tv = evac(VF[:, s, :], bank, tt, vf_free[s])

                def side():
                    gate_mm(16 + 4 * h + j, VF[:, s, :], tv)
                    i, sbk, fr = sring.get()
                    transpose(sbk[:, 0:128], VF[:, s, 0:128], ident, *fr, inc=False)
                    t2 = transpose(sbk[:, 128:256], VF[:, s, 128:256], ident)
                    vf_free[s] = t2
                    t3 = act(QKV[h][2][:, :, 128 * j:128 * j + 128], v3(sbk[:, 0:256], 2), ACT.Copy, t2)
                    sring.free(i, t3)
                    qk_toks.setdefault(h, []).append(t3)
                side_q.append(side)
                return (tv,)
            return f

        def o_epi(h, j):
            def f(bank, tt):
                tv = evac(OZ[:, 4 * h + j, :], bank, tt)
                if j == 3:
                    oz_t[h] = act(OZ[:, 4 * h:4 * h + 4, :], OZ[:, 4 * h:4 * h + 4, :], ACT.Sigmoid, tv)
                return (tv,)
            return f
        oz_t = {}

        def drain_side():
            while True:
                q, side_q[:] = list(side_q), []
                for f in q:
                    f()
                yield

        dr = start(drain_side())
        for h in range(5):
            if h < 4:
                for j in range(4):
                    gemm("e_w_in", 2048 + 512 * h + 128 * j, 16, xn, xm_epi(h, j))
            if h > 0:
                g = h - 1
                p = g % 2
                if h == 4:
                    flush()
                t_xc, t_x_ = conv_toks[g]
                for j in range(2):
                    gemm("e_w_q", (g, 128 * j), 4, lambda k: XCS[p][:, k, :], qk_epi(g, j, False), t_xc)
                for j in range(2):
                    gemm("e_w_k", (g, 128 * j), 4, lambda k: XCS[p][:, k, :], qk_epi(g, j, True))
                xcs_free[p] = (T.last,)
                for j in range(4):
                    gemm("e_w_v", (g, 128 * j), 4, lambda k: XMS[p][:, k, :], v_epi(g, j), t_x_)
                for j in range(4):
                    gemm("e_w_o", (g, 128 * j), 4, lambda k: XMS[p][:, k, :], o_epi(g, j))
                xms_free[p] = (T.last,)

        flush()
        tick()
        tick()
        tasks.remove(dr)
        barrier(V, A, G)
        m = Map(nc, w1, end)
        ZQ = v3(m("ZQ", 1024), 4)
        ROWS = [m(f"ROW{i}", 256, rows=4) for i in range(6)]
        ONER = m("ONER", 256, rows=4)
        top = Map(nc, (end - 2304) // 32 * 32, end)
        top_at = top.at
        RC = top("RC", 512, rows=4)
        AT = top("AT", 8)
        bank_g = GB
        zq_free = [None]

        def gates():
            GI, FX, L1, L2, L3, GC = ROWS
            memset_(ONER, 1.0, E=V)
            act(GI, bank_g[0:4, 0:256], ACT.Identity, T.last, bias=cv("b_if", 0, rows=slice(0, 4)))
            ta = act(FX, bank_g[32:36, 0:256], ACT.Identity, bias=cv("b_if", 0, rows=slice(32, 36)))
            sring.free(gi, ta)
            tv = ts_(FX, FX, -1.0, None, MUL, None, ta)
            yield
            tv = softplus(L3, FX, L1, L2, tv)
            yield
            ts_(L3, L3, -1.0, None, MUL, None)
            scan_(GC, ONER, L3, 0.0, MUL, ADD)
            tt_(L1, GI, GC, SUB)
            ts_(L2, L1, 0.0, None, MUL, None)
            scan_(FX, L1, L2, 0.0, MAX, MAX)
            tv = tt_(L2, FX, GC, ADD)
            ts_(RC[:, 0:256], FX, -1.0, None, MUL, None)
            ta = act(RC[:, 256:512], L2, ACT.Exp, tv, scale=-1.0)
            yield
            i, bk, fr = sring.get()
            mm(bk[:, 0:4], L1[:, 0:128], ident[0:4, 0:4], *fr, tv, inc=False)
            tt = mm(bk[:, 4:8], L1[:, 128:256], ident[0:4, 0:4])
            t = copy_(AT, bk[:, 0:8], tt)
            sring.free(i, t)
            rc_tok.append((ta, t, V.last))

        rc_tok = []
        gt = start(gates())

        def z_epi(j):
            def f(bank, tt):
                tv = evac_rs(ZQ[:, j % 4, :], bank, tt)
                if j % 4 == 3:
                    q = slice(j - 3, j + 1)
                    ta = act(ZQ, ZQ, ACT.Silu, tv)
                    t = tt_(OZ[:, q, :], OZ[:, q, :], ZQ, MUL, ta, oz_t[j // 4])
                return (tv,)
            return f

        for j in range(16):
            gemm("e_w_in", 4096 + 2048 + 128 * j, 16, xn, z_epi(j))
        flush()
        finish(gt)
        barrier(V, A, G)

        m = Map(nc, w1, end)
        XL = v3(m("XL", 2 * 259), 2)
        XC = v3(m("XC", 512), 2)
        RB = v3(m("RB", 512), 2)
        IB = v3(m("IB", 512), 2)
        ZB = v3(m("ZB", 512), 2)
        m2 = Map(nc, m.at, top_at)
        EB = m2("EB", 384)
        EM = m2("EM", 256)
        DN = m2("DN", 256)
        HB = v3(m2("HB", 1024), 4)
        RS2 = m2("RS2", 256)
        SP8 = m2("SP8", 16)
        SPt = [m2(f"SPt{i}", 16) for i in range(3)]
        memset_(XL[:, :, 0:3], 0.0, E=V)
        tv = ts_(SPt[2], cv("lru_lam", 0, 16), -1.0, None, MUL, None)
        softplus(SP8, SPt[2], SPt[0], SPt[1], tv)
        t_sp = ts_(SP8, SP8, 8.0, None, MUL, None)
        NSP8 = m2("NSP8", 16)
        t_sp = ts_(NSP8, SP8, -1.0, None, MUL, None)

        def attend(h):
            Q, K, VT = QKV[h]
            i, b0, fr = sring.get()
            tt = mm(b0, ident[0:4, h:h + 1].to_broadcast([4, 128]), RC, *fr, *rc_tok[0])
            i1, b1, fr1 = sring.get()
            w = [t for t in qk_toks[h]]
            mm(b1[:, 0:256], K[:, 0, 0:128], Q[:, 0, :], *fr1, *w, start=True, stop=False, inc=False)
            mm(b1[:, 0:256], K[:, 1, 0:128], Q[:, 1, :], start=False, stop=True, inc=False)
            mm(b1[:, 256:384], K[:, 0, 128:256], Q[:, 0, 128:256], start=True, stop=False, inc=False)
            ts1 = mm(b1[:, 256:384], K[:, 1, 128:256], Q[:, 1, 128:256], start=False, stop=True)
            yield
            te = act(EM, b0[:, 256:512], ACT.Copy, tt, V.last)
            t1 = tt_(EB[:, 0:256], b0[:, 0:256], cs("mask", 256), ADD, tt, te, T_last[0])
            t1 = tt_(EB[:, 256:384], b0[:, 128:256], cs("mask", 128), ADD)
            ta = act(EB[:, 0:256], EB[:, 0:256], ACT.Exp, t1, bias=AT[:, h:h + 1])
            ta = act(EB[:, 256:384], EB[:, 256:384], ACT.Exp, bias=AT[:, 4 + h:5 + h])
            sring.free(i, ta)
            t1 = tt_(EB, EB, b1[:, 0:384], MUL, ta, ts1)
            sring.free(i1, t1)
            yield
            id_, bd, fr = sring.get()
            mm(bd[:, 0:256], ones, EB[:, 0:256], *fr, t1, start=True, stop=False, inc=False)
            td = mm(bd[:, 128:256], ones, EB[:, 256:384], start=False, stop=True)
            nb = []
            for n in range(2):
                ib, bn, fr = sring.get()
                for j in range(2):
                    d = 2 * n + j
                    mm(bn[:, 256 * j:256 * j + 256], VT[:, 0, 128 * d:128 * d + 128], EB[:, 0:256], *fr,
                       start=True, stop=False, inc=False)
                    tn_ = mm(bn[:, 256 * j + 128:256 * j + 256], VT[:, 1, 128 * d:128 * d + 128],
                             EB[:, 256:384], start=False, stop=True)
                nb.append((ib, bn))
            T_last[0] = T.last
            yield
            stt(DN, bd[:, 0:256], -1.0, EM, MUL, MAX, td, te)
            tt_(DN, bd[:, 0:256], DN, MAX)
            t = recip_(DN, DN)
            sring.free(id_, t)
            for n in range(2):
                t = tt_(HB[:, 2 * n:2 * n + 2, :], v3(nb[n][1], 2), DN.unsqueeze(1).to_broadcast([128, 2, 256]),
                        MUL, tn_, A.last)
                sring.free(nb[n][0], t)
            i, bk, fr = sring.get()
            tq = sumsq(lambda k: HB[:, k:k + 2, :].rearrange("p a b -> p (a b)"), 4, t, bk, *fr)
            yield
            ta = rs_from(RS2, bk[:, 0:256], 512, tq)
            sring.free(i, ta)
            for j in range(4):
                stt(HB[:, j, :], HB[:, j, :], cv("m_norm", 4 * h + j), RS2, MUL, MUL, ta)
            t = tt_(HB, HB, OZ[:, 4 * h:4 * h + 4, :], MUL)
            ys_t[h] = split(YS[:, 16 + 4 * h:20 + 4 * h, :], HB, t, T_last[0])
        ys_t = {}
        T_last = [None]

        def all_heads():
            for h in range(4):
                yield from attend(h)
                yield

        heads = start(all_heads())
        xl_t = {}

        def xl_epi(j):
            def f(bank, tt):
                tv = evac_rs(XL[:, j % 2, 3:259], bank, tt)
                if j % 2:
                    for i in range(2):
                        k = j - 1 + i
                        t = conv(XC[:, i, :], XL[:, i, :], lambda t, k=k: cv("conv_l_w", 16 * t + k),
                                 cv("conv_l_b", k), 4, tv)
                    xl_t[j // 2] = split(YS[:, j - 1:j + 1, :], XC, t)
                return (tv,)
            return f

        def zl_epi(j):
            def f(bank, tt):
                tv = evac_rs(ZB[:, j % 2, :], bank, tt)
                if j % 2:
                    act(ZB, ZB, ACT.Silu, tv)
                return (tv,)
            return f

        def ri_epi(j, buf, nm):
            def f(bank, tt):
                tv = evac(buf[:, j % 2, :], bank, tt)
                if j % 2 and nm == "lru_bx":
                    lru_tail(j - 1, tv)
                return (tv,)
            return f

        def lru_tail(j0, tv):
            for i in range(2):
                k = j0 + i
                act(RB[:, i, :], RB[:, i, :], ACT.Sigmoid, tv, bias=cv("lru_ba", k))
                act(IB[:, i, :], IB[:, i, :], ACT.Sigmoid, bias=cv("lru_bx", k))
            TH = XL[:, :, 0:256]
            ti = A.last
            tu = tt_(IB, IB, XC, MUL, ti)
            for i in range(2):
                k = j0 + i
                act(TH[:, i, :], RB[:, i, :], ACT.Tanh, t_sp, scale=SP8[:, k:k + 1])
            for i in range(2):
                k = j0 + i
                act(RB[:, i, :], RB[:, i, :], ACT.Exp, scale=NSP8[:, k:k + 1])
            act(XC, TH, ACT.Ln, tu, bias=1.0)
            ta = act(TH, TH, ACT.Ln, scale=2.0)
            t = tt_(TH, TH, XC, SUB, ta)
            ta = act(TH, TH, ACT.Exp, t, scale=0.5)
            t = tt_(IB, IB, TH, MUL, ta)
            for i in range(2):
                scan_(XC[:, i, :], RB[:, i, :], IB[:, i, :], 0.0, MUL, ADD)
            t = tt_(XC, XC, ZB, MUL)
            split(YS[:, j0:j0 + 2, :], XC, t, ys_l_free)
            memset_(XL[:, :, 0:3], 0.0, E=V)
            A.wait(V.last)

        ys_l_free = T.last
        for j in range(0, 16, 2):
            for i in range(2):
                gemm("e_w_in", 128 * (j + i), 16, xn, xl_epi(j + i))
            for i in range(2):
                gemm("e_w_in", 4096 + 128 * (j + i), 16, xn, zl_epi(j + i))
            for nm, wn, buf in (("lru_ba", "e_lru_wa", RB), ("lru_bx", "e_lru_wx", IB)):
                for i in range(2):
                    flush()
                    gemm(wn, (j + i, 0), 1, lambda k, i=i: YS[:, j + i, :], ri_epi(j + i, buf, nm), xl_t[j // 2])
            flush()
        finish(heads)
        ys_done = V.last
        barrier(V, A, G)

        def out_proj(name, kt, ys, X, load_tok, first_wait, nm):
            def epi(n):
                def f(bank, tt):
                    t = tt_(X[:, n, :], X[:, n, :], bank[:, 0:256], ADD, tt, load_tok)
                    nm.tile(t)
                    return (t,)
                return f
            T.wait(first_wait)
            for n in range(16):
                gemm(name, 128 * n, kt, lambda k: ys(k), epi(n))
            flush()
            return V.last

        XT = (end - 18 * 1024 - 64) // 32 * 32
        m = Map(nc, XT, end)
        X = v3(m("X1", 16 * 256), 16)
        TMP = v3(m("TMP1", 512), 2)
        t_x = load(X, args["x"], V.last, A.last, T.last)
        nm = Norm(X, "o_norm", TMP)
        t = out_proj("e_w_out", 32, lambda k: YS[:, k, :], X, t_x, ys_done, nm)

        stores = [0]

        def store_x(X, t):
            S.op(lambda e: e.dma_start(scratch, X).then_inc(st_sem, 16), t, inc=False, chain=False)
            stores[0] += 16
            return (st_sem, stores[0])

        t_st = store_x(X, t)
        nm.end()
        barrier(V, A)
        m = Map(nc, R0, end)
        YS = v3(m("YS2", 32 * 512, F32R), 32)
        CSX = m("CSX", 384, rows=64)
        DTR = m("DTR", 256, rows=64)
        NCST = m("NCST", 128)
        DTT = m("DTT", 128)
        XP = v3(m("XP", 6 * 259), 6)
        XV = [v3(m(f"XV{i}", 6 * 256), 6) for i in range(2)]
        ZB = v3(m("ZB2", 4 * 256), 4)
        XDT = v3(m("XDT", 1024), 2)
        CBm = m("CBm", 384)
        DB = [m(f"DB{i}", 384) for i in range(3)]
        YB = v3(m("YB", 1024), 4)
        RS3 = m("RS3", 256)
        RT = [XV[0][0:64, i, :] for i in range(4)]
        ONE64 = XV[0][0:64, 4, :]
        EA = XV[0][0:64, 5, 0:1]
        memset_(XP[:, :, 0:3], 0.0, E=V)

        dt_tok = []

        def dt_epi(bank, tt):
            tv = evac_rs(RT[0], bank, tt, rows=slice(0, 64))
            t = ts_(RT[0], RT[0], cv("dt_bias", 0, rows=slice(0, 64)), None, ADD, None)
            memset_(ONE64, 1.0, E=V)
            t = softplus(DTR, RT[0], RT[1], RT[2], V.last)
            ta = act(EA, cv("a_log", 0, rows=slice(0, 64)), ACT.Exp)
            ts_(RT[3], DTR, EA, -1.0, MUL, MUL, ta)
            scan_(CSX[:, 0:256], ONE64, RT[3], 0.0, MUL, ADD)
            dt_tok.append(copy_(CSX[:, 256:384], CSX[:, 128:256]))
            return (tv,)

        def dt_side():
            while not dt_tok:
                yield
            yield
            i, bk, fr = sring.get()
            idn = ident[0:64, 0:64]
            transpose(bk[:, 0:64], CSX[:, 0:128], idn, *fr, dt_tok[0], inc=False)
            transpose(bk[:, 64:128], CSX[:, 128:256], idn, inc=False)
            transpose(bk[:, 128:192], DTR[:, 0:128], idn, inc=False)
            tt = transpose(bk[:, 192:256], DTR[:, 128:256], idn)
            yield
            ts_(NCST, bk[:, 0:128], -1.0, None, MUL, None, tt)
            t = copy_(DTT, bk[:, 128:256])
            sring.free(i, t)
            A.wait(t)
            dts_done.append(t)

        dts_done = []
        gemm("o_w_in", 10240, 16, xn, dt_epi, width=64)
        flush()
        dts = start(dt_side())
        xv_free = [None, None]
        z_tok, v_tok, zb_free = {}, {}, [None]

        def xv_epi(g, s):
            ch = [32 + g, 40 + g, 4 * g, 4 * g + 1, 4 * g + 2, 4 * g + 3]

            def f(bank, tt):
                tv = evac_rs(XP[:, s, 3:259], bank, tt)
                k = ch[s]
                t = conv(XV[g % 2][:, s, :], XP[:, s, :], lambda t: cv("o_conv_w", 48 * t + k),
                         cv("o_conv_b", k), 4, tv, xv_free[g % 2])
                if s == 5:
                    v_tok[g] = act(XV[g % 2], XV[g % 2], ACT.Silu, t)
                return (tv,)
            return f

        def zs_epi(g, j):
            def f(bank, tt):
                tv = evac_rs(ZB[:, j, :], bank, tt)
                if j == 3:
                    z_tok[g] = act(ZB, ZB, ACT.Silu, tv)
                return (tv,)
            return f

        def ssd(g):
            B_, C_, XS_ = XV[g % 2][:, 0, :], XV[g % 2][:, 1, :], XV[g % 2][:, 2:6, :]
            tk = v_tok[g]
            ic, bc, fr = sring.get()
            mm(bc[:, 0:256], B_[:, 0:128], C_, *fr, tk, start=True, stop=True, inc=False)
            tt = mm(bc[:, 256:384], B_[:, 128:256], C_[:, 128:256], start=True, stop=True)
            tx = []
            for t in range(2):
                i, b, fr = sring.get()
                for j in range(4):
                    t2 = transpose(b[:, 128 * j:128 * j + 128], XS_[:, j, 128 * t:128 * t + 128], ident, *fr,
                                   inc=(j == 3))
                tx.append((i, b, t2))
            yield
            ta = act(CBm, bc[:, 0:384], ACT.Copy, tt, V.last)
            sring.free(ic, ta)
            for t in range(2):
                i, b, t2 = tx[t]
                tv = tt_(XDT[:, t, :].rearrange("p (h d) -> p h d", h=8), b.rearrange("p (h d) -> p h d", h=8),
                         DTT[:, 64 * t + 8 * g:64 * t + 8 * g + 8].unsqueeze(2).to_broadcast([128, 8, 64]),
                         MUL, t2, y_last[0])
                sring.free(i, tv)
            t_xdt = V.last
            tg = {}
            banks = {}

            def bc_mm(e):
                h = 8 * g + e
                i, b, fr = sring.get()
                mm(b[:, 0:384], identr, maskr, *fr, start=True, stop=False, inc=False)
                banks[e] = (i, b, mm(b[:, 0:384], ident[0:64, h:h + 1].to_broadcast([64, 128]), CSX,
                                     start=False, stop=True))

            def dec(e):
                i, b, t = banks[e]
                h = 8 * g + e
                d = DB[e % 3]
                act(d[:, 0:256], b[:, 0:256], ACT.Exp, t, d_free[e % 3], bias=NCST[:, h:h + 1])
                ta = act(d[:, 256:384], b[:, 256:384], ACT.Exp, bias=NCST[:, 64 + h:65 + h])
                sring.free(i, ta)
                tg[e] = tt_(d, d, CBm, MUL, ta)

            yb = {}

            def y_mm(e):
                if e % 4 == 0:
                    i, b, fr = sring.get()
                    yb[e // 4] = [i, b, None]
                    T.wait(*fr)
                i, b, _ = yb[e // 4]
                c = 256 * ((e % 4) // 2)
                r = 64 * (e % 2)
                d = DB[e % 3]
                mm(b[r:r + 64, c:c + 256], XDT[:, 0, 64 * e:64 * e + 64], d[:, 0:256], tg[e], t_xdt,
                   start=True, stop=False, inc=False)
                t = mm(b[r:r + 64, c + 128:c + 256], XDT[:, 1, 64 * e:64 * e + 64], d[:, 256:384],
                       start=False, stop=True)
                d_free[e % 3] = t
                yb[e // 4][2] = t

            bc_mm(0)
            yield
            for e in range(8):
                dec(e)
                if e < 7:
                    bc_mm(e + 1)
                if e > 0:
                    y_mm(e - 1)
                yield
            y_mm(7)
            y_last[0] = T.last
            yield
            for n in range(2):
                i, b, t = yb[n]
                for j in range(2):
                    q = 2 * n + j
                    tv = stt(YB[:, q, :], XS_[:, q, :], cv("d_skip", 4 * g + q), b[:, 256 * j:256 * j + 256],
                             MUL, ADD, t, A.last)
                sring.free(i, tv)
            xv_free[g % 2] = tv
            t = tt_(YB, YB, ZB, MUL, z_tok[g])
            zb_free[0] = t
            i, bk, fr = sring.get()
            tq = sumsq(lambda k: YB[:, k:k + 2, :].rearrange("p a b -> p (a b)"), 4, t, bk, *fr)
            yield
            ta = rs_from(RS3, bk[:, 0:256], 512, tq)
            sring.free(i, ta)
            for j in range(4):
                t = stt(YB[:, j, :], YB[:, j, :], cv("gnorm", 4 * g + j), RS3, MUL, MUL, ta)
            split(YS[:, 4 * g:4 * g + 4, :], YB, t)

        y_last = [None]
        d_free = [None] * 3
        prev = None
        for g in range(8):
            if g == 1:
                finish(dts)
            if g == 0:
                xv_free[0] = V.last
            cols = [8192 + 128 * g, 9216 + 128 * g] + [4096 + 512 * g + 128 * j for j in range(4)]
            for s in range(6):
                gemm("o_w_in", cols[s], 16, xn, xv_epi(g, s))
            flush()
            if prev is not None:
                finish(prev)
            finish(dts)
            for e_ in (V, A):
                e_.wait(t_st)
            for j in range(4):
                gemm("o_w_in", 512 * g + 128 * j, 16, xn, zs_epi(g, j))
                if j == 0:
                    prev = start(ssd(g))
            flush()
        finish(prev)
        ys_done = V.last
        barrier(V, A, G)
        m = Map(nc, XT, end)
        X = v3(m("X2", 16 * 256), 16)
        TMP = v3(m("TMP2", 512), 2)
        t_x = load(X, scratch, V.last, A.last, T.last, t_st)
        nm = Norm(X, "norm_mix", TMP, first="final_norm")
        t = out_proj("o_w_out", 32, lambda k: YS[:, k, :], X, t_x, ys_done, nm)
        nm.end(RST)
        for k in range(16):
            t = stt(X[:, k, :], X[:, k, :], cv("final_norm", k), RS1, MUL, MUL, A.last)
        t_st = store_x(X, t)
        barrier(V, A, G)

        m = Map(nc, R0, end)
        GOS = v3(m("GOS", 8 * 512, F32R), 8)
        r1 = m.at
        PSM = v3(m("PSM", 16 * 256), 16)
        DOS = v3(m("DOS", 8 * 512, F32R), 8)
        r2 = m.at
        MS = v3(Map(nc, R0, end)("MS", 16 * 512, F32R), 16)
        DQ0 = v3(m("DQ0", 4 * 256), 4)
        DVT0 = v3(m("DVT0", 1024), 2)
        r3 = m.at
        DBI = m("DBI", 1024)
        P1 = [m(f"P1{i}", 32) for i in range(10)]
        PW = m("PW", 2 * 8 * 32).rearrange("p (c l a) -> p c l a", c=2, l=8)
        ZS = v3(Map(nc, m.at, end)("ZS", 8 * 512, F32R), 8)
        TB = m("TB", 2 * 2 * 2 * 256).rearrange("p (s c a b) -> p s c a b", s=2, c=2, a=2)
        BR = v3(m("BR", 8 * 128), 8)
        BI = v3(m("BI", 8 * 128), 8)
        CR = v3(m("CR", 32 * 32), 32)
        CI = v3(m("CI", 32 * 32), 32)
        US = v3(m("US", 8 * 256), 8)
        BX = [v3(m(f"BX{i}", 512), 2) for i in range(2)]
        BS = v3(m("BS", 512), 2)
        HH = v3(m("HH", 512), 2)
        PT = m("PT", 2 * 64)
        CUM = m("CUM", 256)
        RS4 = m("RS4", 256)
        mt = Map(nc, r1, r2)
        CRR, CIR = v3(mt("CRR", 1024), 32), v3(mt("CIR", 1024), 32)
        C1, C2 = v3(mt("C1", 1024), 32), v3(mt("C2", 1024), 32)
        t_b1 = load(BR, args["b_re"], T.last, V.last, A.last)
        t_b2 = load(BI, args["b_im"])
        t_c1 = load(CRR, args["c_re"])
        t_c2 = load(CIR, args["c_im"])

        def s5_consts():
            lr, dt, mag, th, r, s1, c1, den, fr_, fi_ = P1
            li = cv("a_im", 0, 32)
            ts_(lr, cv("a_re", 0, 32), -1e-4, None, MIN, None)
            ta = act(dt, cv("log_dt", 0, 32), ACT.Exp)
            tv = tt_(mag, dt, lr, MUL, ta)
            act(mag, mag, ACT.Exp, tv)
            tt_(th, dt, li, MUL)
            ts_(r, th, 1.0 / TWO_PI, 12582912.0, MUL, ADD)
            ts_(r, r, -12582912.0, None, ADD, None)
            ts_(c1, r, -6.28125, None, MUL, None)
            tt_(th, th, c1, ADD)
            stt(th, r, -0.0019350051879882812, th, MUL, ADD)
            stt(th, r, -3.0199160505063e-07, th, MUL, ADD)
            tv = ts_(th, th, 3.1415925, -3.1415925, MIN, MAX)
            ta = act(s1, th, ACT.Sin, tv)
            ta = act(c1, th, ACT.Sin, scale=0.5)
            tt_(c1, c1, c1, MUL, ta)
            ts_(c1, c1, -2.0, 1.0, MUL, ADD)
            yield
            copy_(PW[:, 0, 0, :], c1)
            copy_(PW[:, 1, 0, :], s1)
            for l in range(1, 8):
                c_, s_ = PW[:, 0, l - 1, :], PW[:, 1, l - 1, :]
                tt_(den, s_, s_, MUL)
                tt_(fr_, c_, c_, MUL)
                tt_(PW[:, 0, l, :], fr_, den, SUB)
                tv = stt(PW[:, 1, l, :], s_, 2.0, c_, MUL, MUL)
            pw_tok.append(tv)
            yield
            tt_(fr_, mag, c1, MUL)
            ts_(fr_, fr_, -1.0, None, ADD, None)
            tt_(fi_, mag, s1, MUL)
            tt_(c1, lr, lr, MUL)
            tt_(den, li, li, MUL)
            tt_(den, den, c1, ADD)
            recip_(den, den)
            tt_(c1, fr_, lr, MUL)
            tt_(s1, fi_, li, MUL)
            tt_(r, c1, s1, ADD)
            tt_(c1, fi_, lr, MUL)
            tt_(s1, fr_, li, MUL)
            tt_(c1, c1, s1, SUB)
            tt_(fr_, r, den, MUL)
            tt_(fi_, c1, den, MUL)
            frb, fib = [x.unsqueeze(2).to_broadcast([128, 32, 32]) for x in (fr_, fi_)]
            tt_(C1, CRR, frb, MUL, t_c1, t_c2)
            tt_(C2, CIR, fib, MUL)
            tt_(CR, C1, C2, SUB)
            yield
            tt_(C1, CRR, fib, MUL)
            tt_(C2, CIR, frb, MUL)
            tv = stt(CI, C1, -1.0, C2, MUL, SUB)
            cc_tok.append(tv)

        pw_tok, cc_tok = [], []
        s5c = start(s5_consts())
        us_t = {}

        def u_epi(j):
            def f(bank, tt):
                tv = evac_rs(US[:, j, :], bank, tt, t_st)
                us_t[j] = tv
                return (tv,)
            return f

        for j in range(8):
            gemm("w_in_2", 128 * j, 16, xn, u_epi(j))
        flush()
        finish(s5c)
        A.wait(V.last)

        every[0] = 8
        gring, sring, yring = ring(0, 1, 2), ring(3, 4, 5, 6), ring(7)
        mt = Map(nc, r1, r2)
        GQ = [mt(f"GQ{i}", 256) for i in range(2)]
        GK = [mt(f"GK{i}", 256) for i in range(2)]
        GR = [v3(mt(f"GR{i}", 512), 2) for i in range(2)]
        GVT = [v3(mt("GVT0", 1024), 2), v3(DBI, 2)]
        GE1s = [mt("GE10", 256), m("GE11", 256)]
        GE2 = mt("GE2", 256)
        GE3 = mt("GE3", 256)
        KTM = mt("KTM", 7 * 128).rearrange("p (a b) -> p a b", a=7)
        SC = v3(mt("SC", 256), 2)
        ST = mt("ST", 7 * 256).rearrange("p (a b) -> p a b", a=7)
        ALR = mt("ALR", 256, rows=16)
        WG = mt("WG", 512, rows=16)
        DLs = [mt(f"DL{i}", 8) for i in range(2)]
        t_wg = load(WG, args["w_gate"], V.last, A.last)
        MAG = P1[2]
        OB = v3(mt("OB", 512), 2)

        def phases(b):
            tb = TB[:, b % 2]
            a = slice(2 * b, 2 * b + 2)
            G.wait(tb_free[b % 2])
            memset_(tb[:, 0, :, 0:1], 1.0, E=G)
            memset_(tb[:, 1, :, 0:1], 0.0, E=G)
            for l in range(8):
                d = 1 << l
                q = min(d, 64)
                Cq = PW[:, 0, l, a].unsqueeze(2).to_broadcast([128, 2, q])
                Sq = PW[:, 1, l, a].unsqueeze(2).to_broadcast([128, 2, q])
                t1 = v3(PT, 2)[:, :, 0:q]
                for o in range(0, d, q):
                    x, y = slice(o, o + q), slice(d + o, d + o + q)
                    tt_(tb[:, 0, :, y], tb[:, 0, :, x], Cq, MUL, E=G)
                    tt_(t1, tb[:, 1, :, x], Sq, MUL, E=G)
                    tt_(tb[:, 0, :, y], tb[:, 0, :, y], t1, SUB, E=G)
                    tt_(tb[:, 1, :, y], tb[:, 0, :, x], Sq, MUL, E=G)
                    tt_(t1, tb[:, 1, :, x], Cq, MUL, E=G)
                    tg = tt_(tb[:, 1, :, y], tb[:, 1, :, y], t1, ADD, E=G)
                    if l > 5:
                        yield
                if l == 5:
                    yield
            tb_t[b] = tg

        tb_free, tb_t = [None, None], {}
        bx_free, hh_free = [None, None], [None]
        y_bank, bs_free = [], []

        def s5_tile(n):
            ft, q = n // 4, n % 4
            rows = slice(32 * q, 32 * q + 32)
            tb = TB[:, (n // 2) % 2]
            cc, ss = tb[:, 0, n % 2, :], tb[:, 1, n % 2, :]
            c2 = cc.unsqueeze(1).to_broadcast([128, 2, 256])
            s2 = ss.unsqueeze(1).to_broadcast([128, 2, 256])
            b = BX[n % 2]
            i, bk, fr = sring.get()
            mm(bk[:, 0:256], BR[rows, ft, :], US[rows, ft, :], *fr, us_t[ft], t_b1, t_b2,
               start=True, stop=True, inc=False)
            tt = mm(bk[:, 256:512], BI[rows, ft, :], US[rows, ft, :], start=True, stop=True)
            yield
            act(b, v3(bk, 2), ACT.Copy, tt, bx_free[n % 2])
            act(BS[:, 0, :], bk[:, 256:512], ACT.Copy, *bs_free)
            ta = act(BS[:, 1, :], bk[:, 0:256], ACT.Copy, scale=-1.0)
            sring.free(i, ta)
            yield
            tg = tt_(BS, BS, s2, MUL, ta, E=G)
            tt_(b, b, c2, MUL, ta, tb_t[n // 2])
            yield
            tt_(b, b, BS, ADD, tg)
            mg = MAG[:, n:n + 1].to_broadcast([128, 256])
            for c in range(2):
                tv = scan_(BS[:, c, :], mg, b[:, c, :], 0.0, MUL, ADD)
            tt_(b[:, 0, :], BS[:, 1, :], ss, MUL, tv, E=G)
            tg = tt_(b[:, 1, :], BS[:, 0, :], ss, MUL, E=G)
            tv = tt_(HH, BS, c2, MUL, hh_free[0])
            tb_free[(n // 2) % 2] = tv
            bs_free[:] = [tv, tg]
            if n % 2:
                batch_done.append(n // 2)
            yield
            yield
            tt_(HH[:, 0, :], HH[:, 0, :], b[:, 0, :], SUB, tg)
            tv = tt_(HH[:, 1, :], HH[:, 1, :], b[:, 1, :], ADD)
            bx_free[n % 2] = tv
            yield
            if q == 0:
                y_bank[:] = yring.get()
                T.wait(*y_bank[2])
            iy, by, _ = y_bank
            mm(by[rows, 0:256], CR[:, n, :], HH[:, 0, :], tv, start=True, stop=False, inc=False)
            ty = mm(by[rows, 0:256], CI[:, n, :], HH[:, 1, :], start=False, stop=True)
            hh_free[0] = ty
            if q == 3:
                yield
                tv = stt(US[:, ft, :], US[:, ft, :], cv("ssm_d", ft), by[:, 0:256], MUL, ADD, ty)
                yring.free(iy, tv)

        batch_done = []

        def s5():
            gens, ph = [], phases(0)
            nb, at, due, n = 1, 0, 0, 0
            while True:
                if ph is not None and not step(ph):
                    ph = None
                if ph is None and nb < 16 and (nb < 2 or nb - 2 in batch_done):
                    ph = phases(nb)
                    nb += 1
                gens = [g for g in gens if step(g)]
                if n < 32 and at >= due and (n // 2) in tb_t:
                    g = s5_tile(n)
                    step(g)
                    gens.append(g)
                    n += 1
                    due = at + 5
                at += 1
                if n == 32 and not gens:
                    break
                yield
            yield
            ta = act(US, US, ACT.Gelu_apprx_tanh, V.last)
            yield
            G.wait(T.last)
            V.wait(G.last, T.last)
            t_zs.append(split(ZS, US, ta, V.last, T.last, G.last))

        V.wait(A.last)
        A.wait(V.last)
        G.wait(V.last)
        T.wait(V.last, A.last)
        t_zs = []
        s5g = start(s5())

        g_tok = {}

        def alr_epi(bank, tt):
            tv = evac_rs(ALR, bank, tt, rows=slice(0, 16))
            g_tok["alr"] = tv
            return (tv,)

        V.wait(t_st)
        A.wait(t_st)
        gemm("w_in_2", 4096, 16, xn, alr_epi, width=16)

        def save(dst, key, act_fn=None, last=True):
            def f(bank, tt):
                tv = evac_rs(dst, bank, tt, gla_free[0])
                g_tok[key] = tv
                return (tv,)
            return f
        gla_free = [None]

        def vt_epi(dst, key):
            def f(b0, b1, tt):
                act(dst[:, 0, :], b0, ACT.Copy, tt, gla_free[0], scale=RST[:, 0:1])
                t = act(dst[:, 1, :], b1, ACT.Copy, scale=RST[:, 1:2])
                g_tok[key] = t
                return t
            return f

        def rms_tail(bk_i, bk, t_o, wcols, OS, OB, h, gate):
            ta = act(SQ[:, 0, :], bk, ACT.Square, t_o, sq_free[0], sq_free[1])
            yield
            ia, ba, fr = sring.get()
            mm(ba[:, 0:256], ones, SQ[:, 0, 0:256], ta, *fr, start=True, stop=False, inc=False)
            tt = mm(ba[:, 0:256], ones, SQ[:, 0, 256:512], start=False, stop=True)
            sq_free[0] = tt
            yield
            ta = rs_from(RS4, ba[:, 0:256], 256, tt, V.last)
            sring.free(ia, ta)
            yield
            for j in range(2):
                t = stt(OB[:, j, :], bk[:, 256 * j:256 * j + 256], wcols(j), RS4, MUL, MUL, ta)
            sring.free(bk_i, t)
            if gate is not None:
                t = tt_(OB, OB, gate, MUL)
            ta = act(OS[:, 2 * h:2 * h + 2, 0:256], OB, ACT.Copy, t)
            yield
            tt_(OS[:, 2 * h:2 * h + 2, 256:512], OB, OS[:, 2 * h:2 * h + 2, 0:256].bitcast(F32), SUB, ta)

        main_done = {}

        def decays(h):
            GE1, DL = GE1s[h % 2], DLs[h % 2]
            for _ in range(3 if h else 0):
                yield
            while "alr" not in g_tok:
                yield
            i, bk, fr = sring.get()
            tt = mm(bk[:, 0:256], WG[:, 128 * h:128 * h + 128], ALR, *fr, g_tok["alr"], t_wg)
            yield
            act(GE1, bk[:, 0:256], ACT.Identity, tt, T.last, bias=cv("gla_b", h))
            sring.free(i, A.last)
            act(GE2, GE1, ACT.Abs)
            act(GE2, GE2, ACT.Exp, scale=-1.0)
            ta = act(GE2, GE2, ACT.Ln, bias=1.0)
            yield
            stt(GE1, GE1, 0.0, GE2, MIN, SUB, ta)
            tv = scan_(CUM, cs("creset"), GE1, 0.0, MUL, ADD)
            c3 = CUM.rearrange("p (a b) -> p a b", a=8)
            lastc = c3[:, :, 31:32]
            tv = tt_(GE3.rearrange("p (a b) -> p a b", a=8), lastc.to_broadcast([128, 8, 32]), c3, SUB)
            yield
            act(GE1, CUM, ACT.Exp, tv, scale=1.0 / 16)
            act(GE2, CUM, ACT.Exp, scale=-1.0 / 16)
            act(GE3, GE3, ACT.Exp, scale=1.0 / 16)
            dec_t[h] = act(DL.unsqueeze(2), lastc, ACT.Exp, scale=1.0 / 16)

        dec_t = {}

        def gla(h):
            hv = h % 2
            q_, k_, r_, v_ = GQ[h % 2], GK[h % 2], GR[h % 2], GVT[h // 2]
            t_q, t_k, t_r, t_v = [g_tok[x] for x in "qkrv"]
            GE1, DL = GE1s[h % 2], DLs[h % 2]
            act(r_, r_, ACT.Silu, t_r)
            stt(GE1, q_, 128.0 ** -0.5, GE1, MUL, MUL, dec_t[h], t_q)
            tt_(GE3, k_, GE3, MUL, t_k)
            tv = tt_(GE2, k_, GE2, MUL)
            yield
            i, bk, fr = sring.get()
            for j in range(2):
                transpose(bk[:, 128 * j:128 * j + 128], GE3[:, 128 * j:128 * j + 128], ident, tv, *fr, inc=False)
            for j in range(2):
                tt = mm(bk[:, 256 + 128 * j:384 + 128 * j], GE2[:, 128 * j:128 * j + 128],
                        GE1[:, 128 * j:128 * j + 128])
            yield
            for c in range(7):
                ta = act(KTM[:, c, :], bk[:, 128 * (c // 4):128 * (c // 4) + 128], ACT.Copy, tt,
                         scale=cs("cmask", 1, c % 4))
            tv = tt_(SC, v3(bk[:, 256:512], 2), cs("gmask").unsqueeze(1).to_broadcast([128, 2, 128]), MUL, tt, ta)
            sring.free(i, ta, tv)
            yield
            banks = []

            def kv(p):
                i, bk, fr = sring.get()
                for c in range(2 * p, min(2 * p + 2, 7)):
                    tt = mm(bk[:, 256 * (c % 2):256 * (c % 2) + 256], KTM[:, c, :],
                            v_[:, c // 4, 256 * hv:256 * hv + 256], *fr, ta, t_v)
                banks.append((i, bk, tt))

            def states(p):
                i, bk, tt = banks[p]
                for c in range(2 * p, min(2 * p + 2, 7)):
                    src = bk[:, 256 * (c % 2):256 * (c % 2) + 256]
                    if c == 0:
                        ts = copy_(ST[:, 0, :], src, tt)
                    else:
                        ts = stt(ST[:, c, :], ST[:, c - 1, :], DL[:, c:c + 1], src, MUL, ADD, tt)
                sring.free(i, ts)
                return ts

            kv(0)
            yield
            kv(1)
            states(0)
            yield
            kv(2)
            states(1)
            yield
            kv(3)
            states(2)
            yield
            ts = states(3)
            yield
            i, bk, fr = sring.get()
            for d in range(2):
                for j in range(2):
                    mm(bk[:, 256 * d + 128 * j:256 * d + 128 * j + 128],
                       v_[:, j, 256 * hv + 128 * d:256 * hv + 128 * d + 128], SC[:, j, :], *fr, tv, ts,
                       start=(j == 0), stop=False, inc=False)
                for c in range(1, 8):
                    tt = mm(bk[:, 256 * d + 32 * c:256 * d + 32 * c + 32], ST[:, c - 1, 128 * d:128 * d + 128],
                            GE1[:, 32 * c:32 * c + 32], start=False, stop=(c == 7))
            main_done[h] = tt
            V.wait(tt)
            A.wait(tt)
            yield
            yield from rms_tail(i, bk, tt, lambda j: cv("gla_norm", j), GOS, OB, h, r_)
            gla_free[0] = V.last

        def go_on(gen, done, h):
            while h not in done:
                tick()

        prev, cur = None, None
        for h in range(4):
            dc = start(decays(h))
            if h % 2 == 0:
                gemm_t("w_in_2", 2048 + 512 * (h // 2), 16, xn, vt_epi(GVT[h // 2], "v"))
            gemm("w_in_2", 1024 + 128 * h, 16, xn, save(GQ[h % 2], "q"))
            gemm("w_in_2", 1536 + 128 * h, 16, xn, save(GK[h % 2], "k"))
            if prev:
                finish(prev)
            for j in range(2):
                gemm("w_in_2", 3072 + 256 * h + 128 * j, 16, xn, save(GR[h % 2][:, j, :], "r"))
            flush()
            if cur:
                go_on(cur, main_done, h - 1)
            finish(dc)
            prev, cur = cur, start(gla(h))

        mt = Map(nc, r1, r2)
        DQ = [DQ0, v3(mt("DQ1", 4 * 256), 4)]
        DVT = [DVT0, v3(mt("DVT1", 1024), 2)]
        DS = [mt(f"DS{i}", 384) for i in range(2)]
        WT = mt("WT", 384)
        OBD = v3(mt("OBD", 512), 2)
        DST = mt("DST", 16)
        LQ = mt("LQ", 8)
        DNW = mt("DNW", 2)
        dq_t, dv_t = {}, {}
        dq_free, dv_free = [None, None], [None, None]
        t_db = []

        def dq_epi(h, j):
            def f(bank, tt):
                tv = evac_rs(DQ[h % 2][:, j, :], bank, tt, dq_free[h % 2])
                dq_t[h] = tv
                return (tv,)
            return f

        def dv_epi(n):
            def f(b0, b1, tt):
                act(DVT[n % 2][:, 0, :], b0, ACT.Copy, tt, dv_free[n % 2], scale=RST[:, 0:1])
                dv_t[n] = act(DVT[n % 2][:, 1, :], b1, ACT.Copy, scale=RST[:, 1:2])
                return dv_t[n]
            return f

        def lam():
            ts_(DNW, cv("diff_norm", 0, 2), 0.8, None, MUL, None)
            dl = cv("diff_lam", 0, 4).rearrange("p (a b) -> p a b", b=2)
            tv = tt_(LQ[:, 0:2], dl[:, :, 0], dl[:, :, 1], MUL)
            i, bk, fr = sring.get()
            tt = mm(bk[:, 0:2], ones, LQ[:, 0:2], tv, *fr)
            yield
            ta = act(LQ[:, 2:4], bk[:, 0:2], ACT.Exp, tt)
            sring.free(i, ta)
            yield
            tt_(LQ[:, 4:5], LQ[:, 3:4], LQ[:, 2:3], SUB, ta)
            ts_(LQ[:, 4:5], LQ[:, 4:5], -(0.8 - 0.6), None, ADD, None)

        def diff(h):
            Q = DQ[h % 2]
            VT = DVT[(h // 2) % 2]
            if h == 0:
                yield from lam()
            bks = []
            for j in range(2):
                i, bk, fr = sring.get()
                mm(bk[:, 0:256], Q[:, j, 128:256], Q[:, 2 + j, :], dq_t[h], *fr, inc=False)
                tt = mm(bk[:, 256:384], Q[:, j, 0:128], Q[:, 2 + j, 0:128])
                bks.append((i, bk))
            dq_free[h % 2] = tt
            yield
            bias = DBI[:, 256 * h:256 * h + 256]
            for j in range(2):
                i, bk = bks[j]
                stt(DS[j][:, 0:256], bk[:, 0:256], 128.0 ** -0.5, bias, MUL, ADD, tt, t_db[0])
                t = stt(DS[j][:, 256:384], bk[:, 256:384], 128.0 ** -0.5, bias[:, 128:256], MUL, ADD)
                sring.free(i, t)
                rmax_(DST[:, 2 * j:2 * j + 1], DS[j][:, 0:256])
                rmax_(DST[:, 2 * j + 1:2 * j + 2], DS[j][:, 256:384])
            tv = ts_(DST[:, 4:8], DST[:, 0:4], -1.0, None, MUL, None)
            yield
            for j in range(2):
                act(DS[j][:, 0:256], DS[j][:, 0:256], ACT.Exp, tv, bias=DST[:, 4 + 2 * j:5 + 2 * j],
                    accum=DST[:, 8 + 2 * j:9 + 2 * j])
                ta = act(DS[j][:, 256:384], DS[j][:, 256:384], ACT.Exp, bias=DST[:, 5 + 2 * j:6 + 2 * j],
                         accum=DST[:, 9 + 2 * j:10 + 2 * j])
            yield
            recip_(DST[:, 12:16], DST[:, 8:12], ta)
            ts_(DST[:, 14:16], DST[:, 14:16], LQ[:, 4:5], None, MUL, None)
            for b, c in ((0, slice(0, 256)), (1, slice(256, 384))):
                ts_(DS[0][:, c], DS[0][:, c], DST[:, 12 + b:13 + b], None, MUL, None)
                tv = stt(DS[0][:, c], DS[1][:, c], DST[:, 14 + b:15 + b], DS[0][:, c], MUL, ADD)
            yield
            i, bk, fr = sring.get()
            transpose(bk[:, 0:128], DS[0][:, 256:384], ident, tv, *fr, inc=False)
            transpose(bk[:, 128:256], DS[0][:, 0:128], ident, inc=False)
            tt = transpose(bk[:, 256:384], DS[0][:, 128:256], ident)
            V.wait(tt)
            yield
            ta = act(WT, bk[:, 0:384], ACT.Copy, tt)
            sring.free(i, ta)
            yield
            i, bk, fr = sring.get()
            for d in range(2):
                c = 256 * (h % 2) + 128 * d
                mm(bk[:, 256 * d:256 * d + 256], VT[:, 0, c:c + 128], WT[:, 0:256], ta, dv_t[h // 2], *fr,
                   start=True, stop=False, inc=False)
                tt = mm(bk[:, 256 * d + 128:256 * d + 256], VT[:, 1, c:c + 128], WT[:, 256:384],
                        start=False, stop=True)
            dv_free[(h // 2) % 2] = tt
            A.wait(tt)
            yield
            yield from rms_tail(i, bk, tt, lambda j: DNW[:, j:j + 1], DOS, OBD, h, None)

        for h in range(4):
            if h % 2 == 0:
                gemm_t("w_in_2", 6160 + 512 * (h // 2), 16, xn, dv_epi(h // 2))
            for j in range(2):
                gemm("w_in_2", 4112 + 256 * h + 128 * j, 16, xn, dq_epi(h, j))
            for j in range(2):
                gemm("w_in_2", 5136 + 256 * h + 128 * j, 16, xn, dq_epi(h, 2 + j))
            flush()
            if prev:
                finish(prev)
                prev = None
            finish(cur)
            if h == 0:
                for e_ in (V, A):
                    e_.wait(T.last, V.last, A.last)
                t_db.append(load(DBI, args["dbias"], T.last))
            cur = start(diff(h))

        SG = DQ[0]
        VB = v3(DVT[0].rearrange("p a b -> p (a b)"), 4)
        V.wait(dq_free[0], dv_free[0])
        sg_t, ms_t = {}, []

        def g12_epi(n, c):
            s = 2 * (n % 2)

            def f(bank, tt):
                tv = evac_rs(SG[:, s + c, :], bank, tt)
                if c == 1:
                    sg_t[n] = act(SG[:, s:s + 2, :], SG[:, s:s + 2, :], ACT.Sigmoid, tv)
                return (tv,)
            return f

        def y12_epi(n, c):
            s = 2 * (n % 2)

            def f(bank, tt):
                if c == 0:
                    return (tt_(PSM[:, n, :], bank[:, 0:256], SG[:, s, :], MUL, tt, sg_t[n]),)
                tv = tt_(VB[:, n % 2, :], bank[:, 0:256], SG[:, s + 1, :], MUL, tt)
                tt_(PSM[:, n, :], PSM[:, n, :], VB[:, n % 2, :], ADD)
                return (tv,)
            return f

        for n in range(16):
            for c in range(2):
                gemm("w_in_2", 7184 + 2048 * (c + 1) + 128 * n, 16, xn, g12_epi(n, c))
            if n == 0:
                flush()
                finish(cur)
                T.wait(V.last)
                V.wait(A.last, T.last)
            gemm("gla_w_br_2", 128 * n, 8, lambda k: GOS[:, k, :], y12_epi(n, 0))
            gemm("diff_w_br_2", 128 * n, 8, lambda k: DOS[:, k, :], y12_epi(n, 1))
        flush()
        t_read = T.last
        A.wait(t_read, V.last)
        V.wait(t_read, A.last)

        def g0_epi(n):
            s = 2 * (n % 2)

            def f(bank, tt):
                tv = evac_rs(SG[:, s, :], bank, tt)
                act(SG[:, s, :], SG[:, s, :], ACT.Sigmoid, tv)
                return (tv,)
            return f

        def gate_epi(n):
            s = 2 * (n % 2)

            def f(bank, tt):
                ta = act(SG[:, s + 1, :], bank[:, 0:256], ACT.Sigmoid, tt, sg_t.get(("v", n - 2)))
                sg_t["v", n] = tt_(SG[:, s, :], SG[:, s, :], SG[:, s + 1, :], MUL, ta)
                return (ta,)
            return f

        def val_epi(n):
            s = 2 * (n % 2)

            def f(bank, tt):
                tv = tt_(VB[:, n % 2, :], bank[:, 0:256], SG[:, s, :], MUL, tt)
                t = tt_(VB[:, n % 2, :], VB[:, n % 2, :], PSM[:, n, :], ADD)
                ms_t.append(split(MS[:, n, :], VB[:, n % 2, :], t))
                return (tv,)
            return f

        for n in range(16):
            gemm("w_in_2", 7184 + 128 * n, 16, xn, g0_epi(n))
            if n == 0:
                flush()
                finish(s5g)
                m = Map(nc, XT, end)
                X = v3(m("X3", 16 * 256), 16)
                TMP = v3(m("TMP3", 512), 2)
                t_x = load(X, scratch, V.last, A.last, T.last, G.last)
            gemm("ssm_w_glu_2", 2048 + 128 * n, 8, lambda k: ZS[:, k, :], gate_epi(n), t_zs[0])
            gemm("ssm_w_glu_2", 128 * n, 8, lambda k: ZS[:, k, :], val_epi(n))
        flush()
        V.wait(T.last)
        A.wait(T.last)
        gring, sring = ring(0, 1, 2, 3), ring(4, 5, 6, 7)
        every[0] = 16
        nm = Norm(X, "norm_ffn", TMP)
        t = out_proj("w_out_2", 16, lambda k: MS[:, k, :], X, t_x, ms_t[-1], nm)

        nm.end()
        barrier(V, A)
        m = Map(nc, R0, XT)
        HS = v3(m("HS", 43 * 512, F32R), 43)
        UP = v3(m("UP", 2 * 258), 2)
        VG = [v3(m(f"VG{i}", 512), 2) for i in range(2)]
        memset_(UP[:, :, 0:2], 0.0, E=V)
        hs_t, vg_free = {}, [None, None]

        def up_epi(i, s):
            vg = VG[i % 2]

            def f(bank, tt):
                tv = evac_rs(UP[:, s, 2:258], bank, tt)
                k = 43 * s + i
                t = conv(vg[:, s, :], UP[:, s, :], lambda t: cv("ffn_w", 86 * t + k), cv("ffn_b", k), 3, tv,
                         vg_free[i % 2])
                if s == 1:
                    ta = act(vg[:, 1, :], vg[:, 1, :], ACT.Silu, t)
                    deferred.append(lambda: product(ta))
                return (tv,)

            def product(ta):
                t = tt_(vg[:, 0, :], vg[:, 0, :], vg[:, 1, :], MUL, ta)
                ta = act(HS[:, i, 0:256], vg[:, 0, :], ACT.Copy, t)
                deferred.append(lambda: rest(ta))

            def rest(ta):
                hs_t[i] = tt_(HS[:, i, 256:512], vg[:, 0, :], HS[:, i, 0:256].bitcast(F32), SUB, ta)
                vg_free[i % 2] = hs_t[i]
            return f
        for i in range(43):
            gemm("ffn_w_up_2", 128 * i, 16, xn, up_epi(i, 0))
            gemm("ffn_w_up_2", 5504 + 128 * i, 16, xn, up_epi(i, 1))
        flush()
        SUMB = sring.get()
        T.wait(*SUMB[2])
        sums = []

        def down_epi(n):
            def f(bank, tt):
                t = tt_(X[:, n, :], X[:, n, :], bank[:, 0:256], ADD, tt)
                tq = act(SQ4[:, n % 4, :], X[:, n, :], ACT.Square, t, sq4_free[n % 4])
                for g in sums:
                    g()
                sums[:] = [lambda: sq4_free.__setitem__(n % 4, mm(
                    SUMB[1][:, 0:256], ones, SQ4[:, n % 4, :], tq, start=(n == 0), stop=(n == 15)))]
                return (t,)
            return f

        def hs(k):
            T.wait(hs_t[k])
            return HS[:, k, :]
        for n in range(16):
            gemm("ffn_w_down_2", 128 * n, 43, hs, down_epi(n))
        flush()
        for g in sums:
            g()
        ta = rs_from(RSB, SUMB[1][:, 0:256], 2048, T.last, V.last)
        for k in range(16):
            t = stt(X[:, k, :], X[:, k, :], cv("norm_final", k), RSB, MUL, MUL, ta)
            if k % 4 == 3:
                S.op(lambda e, k=k: e.dma_start(out[:, k - 3:k + 1, :], X[:, k - 3:k + 1, :]).then_inc(out_sem, 16),
                     t, inc=False, chain=False)
        S.wait((out_sem, 64))
        S.wait((st_sem, stores[0]))
        assert blk[0] == NBLOCKS, (blk[0], NBLOCKS)

        block = ctx.enter_context(nc.Block())

        @block.sync
        def _(e):
            S.run(e)

        @block.scalar
        def _(e):
            A.run(e)

        @block.vector
        def _(e):
            V.run(e)

        @block.gpsimd
        def _(e):
            G.run(e)

        @block.tensor
        def _(e):
            T.run(e)
    return order



def cols(a, n):
    return np.ascontiguousarray(np.asarray(a, np.float32).reshape(-1, 128).T)


def vectors(I):
    v = np.zeros((128, NVEC), np.float32)

    def put(name, a):
        v[:a.shape[0], VOFF[name]:VOFF[name] + a.shape[1]] = a

    for name, key in [("e_norm", "e_norm"), ("conv_l_w", "e_conv_l_w"), ("conv_l_b", "e_conv_l_b"),
                      ("lru_ba", "e_lru_ba"), ("lru_bx", "e_lru_bx"), ("lru_lam", "e_lru_lam"),
                      ("conv_m_w", "e_conv_m_w"), ("conv_m_b", "e_conv_m_b"), ("m_norm", "e_m_norm"),
                      ("o_norm", "o_norm"), ("o_conv_w", "o_conv_w"), ("o_conv_b", "o_conv_b"),
                      ("gnorm", "o_gnorm"), ("final_norm", "final_norm"), ("norm_mix", "norm_mix_w_2"),
                      ("ssm_d", "ssm_d_2"), ("gla_b", "gla_b_gate_2"), ("gla_norm", "gla_norm_w_2"),
                      ("diff_norm", "diff_norm_w_2"), ("norm_ffn", "norm_ffn_w_2"),
                      ("ffn_w", "ffn_conv_w_2"), ("ffn_b", "ffn_conv_b_2"), ("norm_final", "norm_final_w_2")]:
        put(name, cols(I[key], 0))
    b = I["e_b_if"][0]
    v[0:4, VOFF["b_if"]] = b[0:4]
    v[32:36, VOFF["b_if"]] = b[4:8]
    put("dt_bias", I["o_dt_bias"][0].reshape(64, 1))
    put("a_log", I["o_a_log"][0].reshape(64, 1))
    put("d_skip", np.repeat(I["o_d_skip"][0].reshape(32, 2), 64, axis=1).T)
    put("a_re", I["ssm_a_re_2"][0].reshape(32, 128).T)
    put("a_im", I["ssm_a_im_2"][0].reshape(32, 128).T)
    put("log_dt", np.repeat(I["ssm_log_dt_2"][0].reshape(32, 2), 64, axis=1).T)
    put("diff_lam", np.stack([I[f"diff_lam_{n}_2"][0] for n in ("q1", "k1", "q2", "k2")], axis=1))
    return v


def shapes():
    c = np.zeros((128, NSHP), np.float32)
    p = np.arange(128)[:, None]
    j = np.arange(256)[None, :]

    def put(name, a):
        c[:, SOFF[name]:SOFF[name] + a.shape[1]] = a

    put("ident", np.eye(128, dtype=np.float32))
    put("ones", np.ones((128, 128), np.float32))
    m = np.where(p <= j, 0.0, NEG).astype(np.float32)
    put("mask", np.concatenate([m, m[:, 0:128]], axis=1))
    q = np.arange(128)[None, :]
    put("gmask", ((p <= q) & (p // 32 == q // 32)).astype(np.float32))
    put("creset", np.broadcast_to((j % 32 != 0).astype(np.float32), (128, 256)))
    put("cmask", (p // 32 == np.arange(8)[None, :] % 4).astype(np.float32))
    rel = (128 + p - j).astype(np.float32)
    d = [np.where(rel >= 0, -(2.0 ** (-8.0 * (h + 1) / 4)) * rel, NEG) for h in range(4)]
    return c, np.concatenate(d, axis=1).astype(np.float32)


def pack_weights(I, order):
    w = np.zeros((NUNITS, 128, UB, 128), np.float32)
    for n, (name, k, c, width) in enumerate(order):
        a = I[name][0]
        if isinstance(c, tuple):
            a, c = a[c[0]], c[1]
        w[n // UB, :, n % UB, :width] = a[128 * k:128 * k + 128, c:c + width]
    return w.reshape(NUNITS, 128, UB * 128)


def host_arrays(I, order):
    I = {k: np.asarray(v) for k, v in I.items()}
    x = np.ascontiguousarray(I["x"][0].T.reshape(16, 128, 256).transpose(1, 0, 2))
    wif = I["e_w_if"][0].reshape(32, 128, 8).transpose(1, 0, 2)
    w_if = np.zeros((128, 32, 36), np.float32)
    w_if[:, :, 0:4] = wif[:, :, 0:4]
    w_if[:, :, 32:36] = wif[:, :, 4:8]
    b = {}
    for n in ("re", "im"):
        s = I[f"ssm_b_{n}_2"][0].reshape(8, 4, 2, 64, 16)
        t = np.zeros((4, 2, 16, 8, 2, 64), np.float32)
        c = np.zeros((2, 64, 32, 2, 16), np.float32)
        g = I[f"ssm_c_{n}_2"][0].reshape(32, 2, 16, 64)
        for i in range(2):
            t[:, i, :, :, i, :] = s[:, :, i].transpose(1, 3, 0, 2)
            c[i, :, :, i, :] = g[:, i].transpose(2, 0, 1)
        b["b_" + n] = t.reshape(128, 8, 128)
        b["c_" + n] = c.reshape(128, 32, 32)
    shp, dbias = shapes()
    return {"x": x, "vec": vectors(I), "shp": shp, "dbias": dbias, "w_if": w_if, "w_gate": I["gla_w_gate_2"][0],
            "w": pack_weights(I, order), **b}


_SHAPES = {"x": (128, 16, 256), "vec": (128, NVEC), "shp": (128, NSHP), "dbias": (128, 1024),
           "w_if": (128, 32, 36), "w_gate": (16, 512), "w": (NUNITS, 128, UB * 128),
           "b_re": (128, 8, 128), "b_im": (128, 8, 128), "c_re": (128, 32, 32), "c_im": (128, 32, 32)}


def program(nc):
    args = {n: nc.dram_tensor(f"in_{n}", s, F32, kind="ExternalInput").ap() for n, s in _SHAPES.items()}
    out = nc.dram_tensor("out_0", (128, 16, 256), F32, kind="ExternalOutput").ap()
    scratch = nc.dram_tensor("scratch_0", (128, 16, 256), F32).ap()
    return build(nc, args, out, scratch)


def kernel(**inputs):
    import concourse.bacc as _bacc
    from concourse.bass_utils import run_bass_kernel_spmd as _run

    nc = _bacc.Bacc("TRN2", target_bir_lowering=False, num_devices=1)
    order = program(nc)
    arrays = {f"in_{n}": np.ascontiguousarray(a) for n, a in host_arrays(inputs, order).items()}
    r = _run(nc, [arrays], core_ids=[0])
    o = r.results[0]["out_0"]
    return np.ascontiguousarray(o.transpose(1, 0, 2).reshape(2048, 256).T)[None]
```

```python
from contextlib import ExitStack

import numpy as np

from concourse import mybir

F32 = mybir.dt.float32
F32R = mybir.dt.float32r
ACT = mybir.ActivationFunctionType
ALU = mybir.AluOpType
AX = mybir.AxisListType.X

UB = 8
NRAW = 4
NW = 4
NEG = -1.0e30
TWO_PI = 6.283185307179586


VEC = [
    ("e_norm", 16), ("conv_l_w", 64), ("conv_l_b", 16), ("lru_ba", 16), ("lru_bx", 16),
    ("lru_lam", 16), ("conv_m_w", 64), ("conv_m_b", 16), ("b_if", 1), ("m_norm", 16),
    ("o_norm", 16), ("o_conv_w", 192), ("o_conv_b", 48), ("dt_bias", 1), ("a_log", 1),
    ("d_skip", 32), ("gnorm", 32), ("final_norm", 16), ("norm_mix", 16), ("a_re", 32),
    ("a_im", 32), ("log_dt", 32), ("ssm_d", 8), ("gla_b", 4), ("gla_norm", 2),
    ("diff_lam", 4), ("diff_norm", 2), ("norm_ffn", 16), ("ffn_w", 258), ("ffn_b", 86),
    ("norm_final", 16),
]
VOFF = {}
_at = 0
for _n, _c in VEC:
    VOFF[_n] = _at
    _at += _c
NVEC = _at
SHP = [("ident", 128), ("ones", 128), ("mask", 384), ("gmask", 128), ("creset", 256), ("cmask", 8)]
SOFF = {}
_at = 0
for _n, _c in SHP:
    SOFF[_n] = _at
    _at += _c
NSHP = _at

NBLOCKS = 16 * 64 + 4 * (8 + 8 + 16 + 16) + 16 * 2 + 32 * 16 + 81 * 16 + 32 * 16 + \
    16 * (8 + 4 + 4 + 8 + 8 + 1 + 8 + 8 + 8 + 48) + 32 * 8 + 16 * 8 * 2 + 16 * 16 + 86 * 16 + 43 * 16
NUNITS = -(-NBLOCKS // UB)


class Eng:

    def __init__(self, name, sem):
        self.name, self.sem, self.n, self.q, self.seen = name, sem, 0, [], {}

    def wait(self, *tokens):
        for t in tokens:
            if t is None:
                continue
            sem, v = t
            if self.seen.get(id(sem), 0) < v:
                self.seen[id(sem)] = v
                self.q.append(lambda e, sem=sem, v=v: e.wait_ge(sem, v))

    def op(self, fn, *waits, inc=True, chain=True):
        self.wait(*waits)
        if chain and self.n:
            self.wait((self.sem, self.n))
        if inc:
            self.n += 1
            self.q.append(lambda e: fn(e).then_inc(self.sem, 1))
            return (self.sem, self.n)
        self.q.append(fn)
        return None

    @property
    def last(self):
        return (self.sem, self.n) if self.n else None

    def run(self, e):
        for f in self.q:
            f(e)


class Ring:

    def __init__(self, banks, toks, held, ids):
        self.banks, self.toks, self.held, self.ids, self.i = banks, toks, held, ids, 0

    def get(self):
        n = len(self.ids)
        j = next((j for j in range(self.i, self.i + n) if not self.held[self.ids[j % n]]), None)
        assert j is not None, "no bank is free"
        self.i = j % n + 1
        k = self.ids[j % n]
        self.held[k] = True
        return k, self.banks[k], self.toks[k]

    def free(self, k, *tokens):
        assert self.held[k]
        self.toks[k], self.held[k] = tokens, False


class Map:

    def __init__(self, nc, base, end):
        self.nc, self.at, self.end = nc, base, end

    def __call__(self, name, cols, dt=F32, rows=128):
        t = self.nc.alloc_sbuf_tensor_at(name, [rows, cols], dt, offset=self.at)
        self.at += (cols * 4 + 31) // 32 * 32
        assert self.at <= self.end, (name, self.at, self.end)
        return t[:, :]


def v3(ap, a):
    return ap.rearrange("p (a b) -> p a b", a=a)


def build(nc, args, out, scratch):
    order = []
    ctx = ExitStack()
    with ctx:
        def sem(name):
            return ctx.enter_context(nc.semaphore(name))

        base = (nc.sbuf_base + 31) // 32 * 32
        end = nc.sbuf_usable_end
        fx = Map(nc, base, end)
        RAW = v3(fx("RAW", NRAW * UB * 128), NRAW)
        WH = v3(fx("WH", NW * UB * 128, F32R), NW)
        WL = v3(fx("WL", NW * UB * 128, F32R), NW)
        XN = v3(fx("XN", 16 * 512, F32R), 16)
        CV = fx("CV", NVEC)
        CS = fx("CS", NSHP)
        RSB = fx("RSB", 256)
        SQF = fx("SQ", 1024)
        SQ, SQ4 = v3(SQF, 2), v3(SQF, 4)
        RS1 = fx("RS1", 256)
        RST = fx("RST", 2)
        identr = fx("identr", 128, F32R)
        maskr = fx("maskr", 384, F32R)
        EPSC = fx("epsc", 1)
        R0 = fx.at

        PS = [ctx.enter_context(nc.psum_tensor(f"ps{i}", [128, 512], F32))[:, :] for i in range(8)]

        T = Eng("T", sem("s_t"))
        V = Eng("V", sem("s_v"))
        A = Eng("A", sem("s_a"))
        G = Eng("G", sem("s_g"))
        S = Eng("S", sem("s_s"))
        raw_sem = [sem(f"s_raw{i}") for i in range(NRAW)]
        in_sems = [sem(f"s_in{i}") for i in range(20)]
        st_sem = sem("s_store")
        out_sem = sem("s_out")

        def cv(name, c, n=1, rows=slice(0, 128)):
            return CV[rows, VOFF[name] + c:VOFF[name] + c + n]

        def cs(name, n=None, c=0, rows=slice(0, 128)):
            w = dict(SHP)[name]
            return CS[rows, SOFF[name] + c:SOFF[name] + c + (n or w)]

        ident, ones = cs("ident"), cs("ones")

        n_in = [0]

        def load(dst, src, *waits):
            s = in_sems[n_in[0]]
            n_in[0] += 1
            S.op(lambda e: e.dma_start(dst, src).then_inc(s, 16), *waits, inc=False, chain=False)
            return (s, 16)

        t_cv = load(CV, args["vec"])
        mt = Map(nc, R0 + 32 * 2048 + 16 * 1024 + 5120, end)
        X0 = v3(mt("X0", 16 * 256), 16)
        TMP0 = v3(mt("TMP0", 512), 2)

        def load_x0(q):
            return load(X0[:, 4 * q:4 * q + 4, :], args["x"][:, 4 * q:4 * q + 4, :])
        t_x0 = [load_x0(0)]
        t_cs = load(CS, args["shp"])

        raw_free = [None] * NRAW
        w_free = [None] * NW
        loaded, split_at = [0], [0]
        split_tok, round_tok = {}, {}

        def load_unit():
            u = loaded[0]
            loaded[0] += 1
            k = u % NRAW
            S.op(lambda e: e.dma_start(RAW[:, k, :], args["w"][u]).then_inc(raw_sem[k], 16),
                 *(raw_free[k] or ()), inc=False, chain=False)

        def round_unit():
            u = split_at[0]
            split_at[0] += 1
            k, w = u % NRAW, u % NW
            got = (raw_sem[k], 16 * (u // NRAW + 1))
            round_tok[u] = (got, A.op(lambda e: e.activation(WH[:, w, :], RAW[:, k, :], ACT.Copy),
                                      got, w_free[w], chain=False), w_free[w])

        def rest_unit(u):
            k, w = u % NRAW, u % NW
            tv = V.op(lambda e: e.tensor_tensor(WL[:, w, :], RAW[:, k, :], WH[:, w, :].bitcast(F32),
                                                ALU.subtract), *round_tok[u], chain=False)
            split_tok[u] = tv
            raw_free[k] = (tv,)
            if loaded[0] < NUNITS:
                load_unit()

        load_unit()
        t_x0 += [load_x0(1), load_x0(2)]
        load_unit()
        t_x0.append(load_x0(3))
        for _ in range(2, NRAW):
            load_unit()

        blk = [0]
        since = [0]
        every = [16]

        deferred = []

        def run_deferred():
            q, deferred[:] = list(deferred), []
            for f in q:
                f()

        def unit_ready():
            u = blk[0] // UB
            if blk[0] % UB == 0:
                run_deferred()
                while split_at[0] < min(u + NW, NUNITS):
                    round_unit()
                for w in range(u, min(u + NW - 1, NUNITS)):
                    if w not in split_tok:
                        rest_unit(w)
            return u, blk[0] % UB

        def unit_done(u, b):
            if b == UB - 1:
                w_free[u % NW] = T.last

        tasks = []

        def step(g):
            try:
                next(g)
                return True
            except StopIteration:
                return False

        def tick():
            for g in list(tasks):
                if not step(g):
                    tasks.remove(g)

        def start(g):
            tasks.append(g)
            return g

        def finish(*gs):
            while any(g in tasks for g in gs):
                for g in gs:
                    if g in tasks and not step(g):
                        tasks.remove(g)

        btoks, bheld = [()] * 8, [False] * 8

        def ring(*ids):
            return Ring(PS, btoks, bheld, list(ids))

        gring, sring = ring(0, 1, 2, 3), ring(4, 5, 6, 7)
        pend = []

        def flush():
            while pend:
                pend.pop(0)()

        def products(bank, name, c0, ks, rhs, first=True, last=True, k0=0, width=128):
            for n, k in enumerate(ks):
                order.append((name, k0 + k, c0, width))
                u, b = unit_ready()
                T.wait(split_tok[u])
                h, l = WH[:, u % NW, b * 128:b * 128 + 128], WL[:, u % NW, b * 128:b * 128 + 128]
                x = rhs(k)
                if rhs is xn:
                    T.wait(xn_tok[k])
                end_ = n == len(ks) - 1
                for j, (p, q) in enumerate(((h, x[:, 0:256]), (h, x[:, 256:512]), (l, x[:, 0:256]))):
                    tt = T.op(lambda e, p=p, q=q, s=(first and n == 0 and j == 0), f=(last and end_ and j == 2):
                              e.matmul(bank[:, 0:256], p, q, start=s, stop=f, skip_group_check=True),
                              inc=(j == 2 and (end_ or b == UB - 1)), chain=False)
                unit_done(u, b)
                blk[0] += 1
                since[0] += 1
                if since[0] >= every[0] and not end_:
                    since[0] = 0
                    flush()
                    tick()
            return tt

        def close(i, bank, tt, epi):
            flush()
            pend.append(lambda: gring.free(i, *epi(bank, tt)))
            if since[0] >= every[0]:
                since[0] = 0
                tick()

        def gemm(name, c0, kt, rhs, epi, *waits, k0=0, width=128):
            i, bank, fr = gring.get()
            T.wait(*fr, *waits)
            tt = products(bank, name, c0, range(kt) if isinstance(kt, int) else kt, rhs, k0=k0, width=width)
            close(i, bank, tt, epi)

        def gemm_t(name, c0, kt, lhs, epi, *waits):
            i0, b0, f0 = gring.get()
            i1, b1, f1 = gring.get()
            T.wait(*f0, *f1, *waits)
            for k in range(kt):
                for j in range(4):
                    order.append((name, k, c0 + 128 * j, 128))
                u, b = unit_ready()
                assert b % 4 == 0
                T.wait(split_tok[u])
                h, l = WH[:, u % NW, b * 128:b * 128 + 512], WL[:, u % NW, b * 128:b * 128 + 512]
                x = lhs(k)
                if lhs is xn:
                    T.wait(xn_tok[k])
                for t, bank in ((0, b0), (1, b1)):
                    xh, xl = x[:, 128 * t:128 * t + 128], x[:, 256 + 128 * t:384 + 128 * t]
                    for m, (p, q) in enumerate(((xh, h), (xh, l), (xl, h))):
                        fin = t == 1 and m == 2 and (k == kt - 1 or b == UB - 4)
                        tt = T.op(lambda e, p=p, q=q, bank=bank, s=(k == 0 and m == 0), f=(k == kt - 1 and m == 2):
                                  e.matmul(bank, p, q, start=s, stop=f, skip_group_check=True),
                                  inc=fin, chain=False)
                blk[0] += 4
                unit_done(u, b + 3)
                since[0] += 4
                if since[0] >= every[0] and k < kt - 1:
                    since[0] = 0
                    flush()
                    tick()
            flush()

            def go():
                t = epi(b0, b1, tt)
                gring.free(i0, t)
                gring.free(i1, t)
            pend.append(go)
            if since[0] >= every[0]:
                since[0] = 0
                tick()

        def evac(dst, bank, *waits, rows=slice(0, 128)):
            return copy_(dst, bank[rows, 0:256], *waits)

        def evac_rs(dst, bank, *waits, rows=slice(0, 128)):
            return tt_(dst, bank[rows, 0:256], RSB[rows, :], ALU.mult, *waits)

        def xn(k):
            return XN[:, k, :]

        def copy_(dst, src, *waits):
            return V.op(lambda e: e.tensor_copy(dst, src), *waits)

        def memset_(dst, v, E=V):
            return E.op(lambda e: e.memset(dst, v))

        def rmax_(dst, src):
            return V.op(lambda e: e.tensor_reduce(dst, src, AX, MAX))

        def recip_(dst, src, *waits):
            return V.op(lambda e: e.reciprocal(dst, src), *waits)

        def scan_(dst, a, b, init, o0, o1, *waits):
            return V.op(lambda e: e.tensor_tensor_scan(dst, a, b, init, o0, o1), *waits)

        def act(dst, src, f, *waits, bias=0.0, scale=1.0, accum=None):
            if accum is None:
                return A.op(lambda e: e.activation(dst, src, f, bias=bias, scale=scale), *waits)
            return A.op(lambda e: e.activation(dst, src, f, bias=bias, scale=scale, accum_out=accum), *waits)

        def tt_(dst, a, b, op, *waits, E=None):
            return (E or V).op(lambda e: e.tensor_tensor(dst, a, b, op), *waits)

        def ts_(dst, a, s1, s2, o0, o1, *waits, E=None):
            if s2 is None:
                return (E or V).op(lambda e: e.tensor_scalar(dst, a, s1, None, o0), *waits)
            return (E or V).op(lambda e: e.tensor_scalar(dst, a, s1, s2, o0, o1), *waits)

        def stt(dst, a, s, b, o0, o1, *waits, E=None):
            return (E or V).op(lambda e: e.scalar_tensor_tensor(out=dst, in0=a, scalar=s, in1=b, op0=o0, op1=o1), *waits)

        MUL, ADD, SUB, MAX, MIN = ALU.mult, ALU.add, ALU.subtract, ALU.max, ALU.min

        def mm(dst, l, r, *waits, start=True, stop=True, inc=True):
            return T.op(lambda e: e.matmul(dst, l, r, start=start, stop=stop, skip_group_check=True),
                        *waits, inc=inc, chain=False)

        def transpose(dst, src, idn, *waits, inc=True):
            return T.op(lambda e: e.transpose(dst, src, idn), *waits, inc=inc, chain=False)

        def split(dst, src, t_src, *waits):
            n = len(src.shape)
            hi = dst[:, :, 0:256] if n == 3 else dst[:, 0:256]
            lo = dst[:, :, 256:512] if n == 3 else dst[:, 256:512]
            ta = act(hi, src, ACT.Copy, t_src, *waits)
            return tt_(lo, src, hi.bitcast(F32), SUB, ta, *waits)

        def barrier(*engines):
            toks = [x.last for x in (T, V, A, G)]
            for x in engines:
                x.wait(*toks)

        def softplus(dst, x, t1, t2, t_x, positive_only=False):
            for _ in softplus_steps(dst, x, t1, t2, t_x):
                pass
            return V.last

        def softplus_steps(dst, x, t1, t2, t_x):
            act(t1, x, ACT.Abs, t_x)
            ta = act(t1, t1, ACT.Exp, scale=-1.0)
            yield
            tv = ts_(t2, t1, 1.0, None, ADD, None, ta)
            yield
            ta = act(dst, t2, ACT.Ln, tv)
            yield
            ts_(t2, t2, -1.0, 1e-30, ADD, ADD, ta)
            recip_(t2, t2)
            stt(dst, dst, 1e-30, t2, ADD, MUL)
            tt_(dst, dst, t1, MUL)
            stt(dst, x, 0.0, dst, MAX, ADD)

        def rs_from(dst, bank_ap, n, t_ps, *waits):
            act(dst, bank_ap, ACT.Ln, t_ps, *waits, bias=EPSC, scale=1.0 / n)
            return act(dst, dst, ACT.Exp, scale=-0.5)

        def sumsq(src, nt, t_src, bank, *waits):
            tt = None
            for k in range(0, nt, 2):
                w = (k // 2) % 2
                ta = act(SQ[:, w, :], src(k), ACT.Square, t_src, sq_free[w])
                mm(bank[:, 0:256], ones, SQ[:, w, 0:256], ta, *waits, start=(k == 0), stop=False, inc=False)
                tt = mm(bank[:, 0:256], ones, SQ[:, w, 256:512], start=False, stop=(k == nt - 2))
                sq_free[w] = tt
            return tt

        sq_free = [None, None]

        def square(k, acc, s, x, t):
            if k == 0:
                sq_acc[s] = act(acc, x, ACT.Square, t)
                return sq_acc[s]
            w = s + k % 2
            ta = act(SQ4[:, w, :], x, ACT.Square, t, sq4_free[w])
            sq4_free[w] = tt_(acc, acc, SQ4[:, w, :], ADD, ta, sq_acc[s], E=G)
            return ta

        sq_acc = {}

        class Norm:

            def __init__(self, X, wname, tmp, first=None):
                self.X, self.w, self.tmp, self.first = X, wname, tmp, first
                self.i, self.bank, self.fr = sring.get()
                if first:
                    self.j, self.bank2, self.fr2 = sring.get()
                self.later, self.n = [], 0
                self.tmp_free = [None, None]

            def run_later(self):
                q, self.later = self.later, []
                for f in q:
                    f()

            def tile(self, t_x):
                k, self.n = self.n, self.n + 1
                X, tmp = self.X[:, k, :], self.tmp[:, k % 2, :]
                last = k == 15
                t = t_x
                if self.first:
                    t = ts_(tmp, X, cv(self.first, k), None, MUL, None, t_x, self.tmp_free[k % 2])
                    ta2 = square(k, RS1, 2, tmp, t)
                    t = ts_(tmp, tmp, cv(self.w, k), None, MUL, None, ta2)
                else:
                    t = ts_(tmp, X, cv(self.w, k), None, MUL, None, t_x, self.tmp_free[k % 2])
                self.run_later()
                hi, lo = XN[:, k, 0:256], XN[:, k, 256:512]
                ta = act(hi, tmp, ACT.Copy, t)
                square(k, RSB, 0, X, t_x)

                def rest():
                    xn_tok[k] = self.tmp_free[k % 2] = tt_(lo, tmp, hi.bitcast(F32), SUB, ta)
                self.later.append(rest)
                if last:
                    self.run_later()

            def end(self, rst=None):
                self.tt = mm(self.bank[:, 0:256], ones, RSB, G.last, *self.fr)
                if self.first:
                    self.tt = mm(self.bank2[:, 0:256], ones, RS1, *self.fr2)
                ta = rs_from(RSB, self.bank[:, 0:256], 2048, self.tt, V.last)
                sring.free(self.i, ta)
                if self.first:
                    V.op(lambda e: e.tensor_copy(RS1, RSB), ta)
                    t = V.last
                    t = tt_(RSB, RSB, RSB, MUL)
                    t = tt_(RSB, RSB, self.bank2[:, 0:256], MUL, self.tt)
                    sring.free(self.j, t)
                    ta = rs_from(RSB, RSB, 2048, t)
                    ta = tt_(RSB, RSB, RS1, MUL, ta)
                if rst is not None:
                    i, b, fr = sring.get()
                    mm(b[:, 0:1], RSB[0:1, 0:128], ones[0:1, 0:1], ta, *fr, inc=False)
                    tt = mm(b[:, 1:2], RSB[0:1, 128:256], ones[0:1, 0:1])
                    t = copy_(rst, b[:, 0:2], tt)
                    sring.free(i, t)
                    A.wait(t)
                V.wait(ta)
                return ta

        sq4_free = [None] * 4
        xn_tok = [None] * 16

        memset_(EPSC, 1e-6, E=V)
        A.wait(V.last, t_cv, t_cs)
        V.wait(t_cv, t_cs)
        T.wait(t_cv, t_cs)
        G.wait(t_cv, t_cs)

        m = Map(nc, R0, end)
        YS = v3(m("YS1", 32 * 512, F32R), 32)
        ys0 = R0
        OZ = v3(m("OZ", 16 * 256), 16)
        w1 = m.at
        mm_ = Map(nc, ys0, end)
        XMS = [v3(mm_(f"XMS{i}", 4 * 512, F32R), 4) for i in range(2)]
        XCS = [v3(mm_(f"XCS{i}", 4 * 512, F32R), 4) for i in range(2)]
        QKV = [(v3(mm_(f"Q{i}", 512), 2), v3(mm_(f"K{i}", 512), 2), v3(mm_(f"VT{i}", 1024), 2)) for i in range(4)]
        m = Map(nc, w1, end)
        WIF = m("WIF", 32 * 36).rearrange("p (a b) -> p a b", a=32)
        XMP = [v3(m(f"XMP{i}", 4 * 259), 4) for i in range(2)]
        XMC = v3(m("XMC", 1024), 4)
        VF = v3(m("VF", 1024), 4)
        t_wif = load(WIF, args["w_if"])
        nm = Norm(X0, "e_norm", TMP0)
        first = []
        for j in range(4):
            i, bank, fr = gring.get()
            first.append((i, bank))
        nm.tile(t_x0[0])
        for k in range(16):
            if k < 15:
                nm.tile(t_x0[(k + 1) // 4])
            for j in range(4):
                tt = products(first[j][1], "e_w_in", 2048 + 128 * j, [k], xn, first=(k == 0), last=(k == 15))
                first[j] = first[j][:2] + (tt,)
        copy_(identr, ident)
        t0 = copy_(maskr, cs("mask"))
        T.wait(t0)
        nm.end()
        barrier(V, A)
        for i in range(2):
            memset_(XMP[i][:, :, 0:3], 0.0, E=V)

        def conv(dst, src, w, b, taps, t_src, *waits):
            tv = ts_(dst, src[:, taps - 1:taps + 255], w(taps - 1), b, MUL, ADD, t_src, *waits)
            for t in range(taps - 2, -1, -1):
                tv = stt(dst, src[:, t:t + 256], w(t), dst, MUL, ADD, tv)
            return tv

        t_xm = {}
        xms_free, xcs_free, xmp_free = [(), ()], [(), ()], [None, None]
        t_q, t_k, t_vt = {}, {}, {}
        gi, GB, gfr = sring.get()
        gate_n = [0]
        qk_toks = {}
        conv_toks = {}

        def xm_epi(h, j):
            p, k = h % 2, 4 * h + j

            def f(bank, tt):
                tv = evac_rs(XMP[p][:, j, 3:259], bank, tt, xmp_free[p])
                t = conv(XMC[:, j, :], XMP[p][:, j, :], lambda t: cv("conv_m_w", 16 * t + k),
                         cv("conv_m_b", k), 4, tv)
                if j == 3:
                    act(XMC, XMC, ACT.Silu, t)
                    tc = act(XCS[p][:, :, 0:256], XMC, ACT.Copy, *xcs_free[p])
                    tm = act(XMS[p][:, :, 0:256], XMP[p][:, :, 3:259], ACT.Copy, *xms_free[p])
                    deferred.append(lambda: rest(tc, tm))
                return (tv,)

            def rest(tc, tm):
                t_xc = tt_(XCS[p][:, :, 256:512], XMC, XCS[p][:, :, 0:256].bitcast(F32), SUB, tc, *xcs_free[p])
                t_x_ = tt_(XMS[p][:, :, 256:512], XMP[p][:, :, 3:259], XMS[p][:, :, 0:256].bitcast(F32), SUB,
                           tm, *xms_free[p])
                xmp_free[p] = t_x_
                conv_toks[h] = (t_xc, t_x_)
            return f

        def gate_mm(kt, src, tok, last=False):
            tt = mm(GB[0:36, 0:256], WIF[:, kt, :], src, tok, t_wif, start=(gate_n[0] == 0),
                    stop=(gate_n[0] == 31))
            gate_n[0] += 1
            return tt

        vf_i = [0]
        vf_free = [None] * 4
        side_q = []

        def qk_epi(h, j, isk):
            def f(bank, tt):
                dst = QKV[h][1 if isk else 0][:, j, :]
                if isk:
                    t = tv = act(dst, bank[:, 0:256], ACT.Copy, tt, scale=0.0625)
                else:
                    t = tv = evac(dst, bank, tt)
                qk_toks.setdefault(h, []).append(t)
                side_q.append(lambda: gate_mm((8 if isk else 0) + 2 * h + j, dst, t))
                return (tv,)
            return f

        def v_epi(h, j):
            def f(bank, tt):
                s = vf_i[0] % 4
                vf_i[0] += 1
                tv = evac(VF[:, s, :], bank, tt, vf_free[s])

                def side():
                    gate_mm(16 + 4 * h + j, VF[:, s, :], tv)
                    i, sbk, fr = sring.get()
                    transpose(sbk[:, 0:128], VF[:, s, 0:128], ident, *fr, inc=False)
                    t2 = transpose(sbk[:, 128:256], VF[:, s, 128:256], ident)
                    vf_free[s] = t2
                    t3 = act(QKV[h][2][:, :, 128 * j:128 * j + 128], v3(sbk[:, 0:256], 2), ACT.Copy, t2)
                    sring.free(i, t3)
                    qk_toks.setdefault(h, []).append(t3)
                side_q.append(side)
                return (tv,)
            return f

        def o_epi(h, j):
            def f(bank, tt):
                t = oz_t[h] = act(OZ[:, 4 * h + j, :], bank[:, 0:256], ACT.Sigmoid, tt)
                return (t,)
            return f
        oz_t = {}

        def drain_side():
            while True:
                q, side_q[:] = list(side_q), []
                for f in q:
                    f()
                yield

        dr = start(drain_side())
        every[0] = 8
        for h in range(5):
            if h < 4:
                for j in range(4):
                    if h == 0:
                        close(*first[j], xm_epi(h, j))
                    else:
                        gemm("e_w_in", 2048 + 512 * h + 128 * j, 16, xn, xm_epi(h, j))
            if h > 0:
                g = h - 1
                p = g % 2
                if h == 4:
                    flush()
                    run_deferred()
                t_xc, t_x_ = conv_toks[g]
                for j in range(2):
                    gemm("e_w_q", (g, 128 * j), 4, lambda k: XCS[p][:, k, :], qk_epi(g, j, False), t_xc)
                for j in range(2):
                    gemm("e_w_k", (g, 128 * j), 4, lambda k: XCS[p][:, k, :], qk_epi(g, j, True))
                xcs_free[p] = (T.last,)
                for j in range(4):
                    gemm("e_w_v", (g, 128 * j), 4, lambda k: XMS[p][:, k, :], v_epi(g, j), t_x_)
                for j in range(4):
                    gemm("e_w_o", (g, 128 * j), 4, lambda k: XMS[p][:, k, :], o_epi(g, j))
                xms_free[p] = (T.last,)

        flush()
        tick()
        tick()
        tasks.remove(dr)
        barrier(V, A, G)
        m = Map(nc, w1, end)
        ZQ = v3(m("ZQ", 1024), 4)
        ROWS = [m(f"ROW{i}", 256, rows=4) for i in range(6)]
        ONER = m("ONER", 256, rows=4)
        top = Map(nc, (end - 2304) // 32 * 32, end)
        top_at = top.at
        RC = top("RC", 512, rows=4)
        AT = top("AT", 8)
        bank_g = GB
        zq_free = [None]

        def gates():
            GI, FX, L1, L2, L3, GC = ROWS
            memset_(ONER, 1.0, E=V)
            act(GI, bank_g[0:4, 0:256], ACT.Identity, T.last, bias=cv("b_if", 0, rows=slice(0, 4)))
            ta = act(FX, bank_g[32:36, 0:256], ACT.Identity, bias=cv("b_if", 0, rows=slice(32, 36)))
            sring.free(gi, ta)
            tv = ts_(FX, FX, -1.0, None, MUL, None, ta)
            yield
            tv = softplus(L3, FX, L1, L2, tv)
            yield
            ts_(L3, L3, -1.0, None, MUL, None)
            scan_(GC, ONER, L3, 0.0, MUL, ADD)
            tt_(L1, GI, GC, SUB)
            ts_(L2, L1, 0.0, None, MUL, None)
            scan_(FX, L1, L2, 0.0, MAX, MAX)
            tv = tt_(L2, FX, GC, ADD)
            ts_(RC[:, 0:256], FX, -1.0, None, MUL, None)
            ta = act(RC[:, 256:512], L2, ACT.Exp, tv, scale=-1.0)
            yield
            i, bk, fr = sring.get()
            mm(bk[:, 0:4], L1[:, 0:128], ident[0:4, 0:4], *fr, tv, inc=False)
            tt = mm(bk[:, 4:8], L1[:, 128:256], ident[0:4, 0:4])
            t = copy_(AT, bk[:, 0:8], tt)
            sring.free(i, t)
            rc_tok.append((ta, t, V.last))

        rc_tok = []
        gt = start(gates())

        def z_epi(j):
            def f(bank, tt):
                tv = evac_rs(ZQ[:, j % 4, :], bank, tt)
                if j % 4 == 3:
                    q = slice(j - 3, j + 1)
                    ta = act(ZQ, ZQ, ACT.Silu, tv)
                    deferred.append(lambda: tt_(OZ[:, q, :], OZ[:, q, :], ZQ, MUL, ta, oz_t[j // 4]))
                return (tv,)
            return f

        for j in range(16):
            gemm("e_w_in", 4096 + 2048 + 128 * j, 16, xn, z_epi(j))
        flush()
        run_deferred()
        finish(gt)
        barrier(V, A, G)

        m = Map(nc, w1, end)
        XCb = [v3(m(f"XC{i}", 512), 2) for i in range(2)]
        ZBb = [v3(m(f"ZB{i}", 512), 2) for i in range(2)]
        RB = v3(m("RB", 512), 2)
        IB = v3(m("IB", 512), 2)
        TH = v3(m("TH", 512), 2)
        SP8 = m("SP8", 16)
        NSP8 = m("NSP8", 16)
        XT = (end - 18 * 1024 - 64) // 32 * 32
        assert m.at <= XT + 2048
        XL = v3(m("XL", 2 * 259), 2)
        m2 = Map(nc, m.at, top_at)
        EB = m2("EB", 384)
        EM = m2("EM", 256)
        DN = m2("DN", 256)
        HB = v3(m2("HB", 1024), 4)
        RS2 = m2("RS2", 256)
        SPt = [m2(f"SPt{i}", 16) for i in range(3)]
        memset_(XL[:, :, 0:3], 0.0, E=V)
        tv = ts_(SPt[2], cv("lru_lam", 0, 16), -1.0, None, MUL, None)
        softplus(SP8, SPt[2], SPt[0], SPt[1], tv)
        t_sp = ts_(SP8, SP8, 8.0, None, MUL, None)
        t_sp = ts_(NSP8, SP8, -1.0, None, MUL, None)

        def attend(h):
            Q, K, VT = QKV[h]
            i, b0, fr = sring.get()
            tt = mm(b0, ident[0:4, h:h + 1].to_broadcast([4, 128]), RC, *fr, *rc_tok[0])
            i1, b1, fr1 = sring.get()
            w = [t for t in qk_toks[h]]
            mm(b1[:, 0:256], K[:, 0, 0:128], Q[:, 0, :], *fr1, *w, start=True, stop=False, inc=False)
            mm(b1[:, 0:256], K[:, 1, 0:128], Q[:, 1, :], start=False, stop=True, inc=False)
            mm(b1[:, 256:384], K[:, 0, 128:256], Q[:, 0, 128:256], start=True, stop=False, inc=False)
            ts1 = mm(b1[:, 256:384], K[:, 1, 128:256], Q[:, 1, 128:256], start=False, stop=True)
            yield
            te = act(EM, b0[:, 256:512], ACT.Copy, tt, em_last[0])
            yield
            t1 = tt_(EB[:, 0:256], b0[:, 0:256], cs("mask", 256), ADD, tt, te, T_last[0])
            t1 = tt_(EB[:, 256:384], b0[:, 128:256], cs("mask", 128), ADD)
            yield
            ta = act(EB[:, 0:256], EB[:, 0:256], ACT.Exp, t1, bias=AT[:, h:h + 1])
            ta = act(EB[:, 256:384], EB[:, 256:384], ACT.Exp, bias=AT[:, 4 + h:5 + h])
            sring.free(i, ta)
            yield
            t1 = tt_(EB, EB, b1[:, 0:384], MUL, ta, ts1)
            sring.free(i1, t1)
            yield
            id_, bd, fr = sring.get()
            mm(bd[:, 0:256], ones, EB[:, 0:256], *fr, t1, start=True, stop=False, inc=False)
            td = mm(bd[:, 128:256], ones, EB[:, 256:384], start=False, stop=True)
            nb = []
            for n in range(2):
                ib, bn, fr = sring.get()
                for j in range(2):
                    d = 2 * n + j
                    mm(bn[:, 256 * j:256 * j + 256], VT[:, 0, 128 * d:128 * d + 128], EB[:, 0:256], *fr,
                       start=True, stop=False, inc=False)
                    tn_ = mm(bn[:, 256 * j + 128:256 * j + 256], VT[:, 1, 128 * d:128 * d + 128],
                             EB[:, 256:384], start=False, stop=True)
                nb.append((ib, bn))
            T_last[0] = T.last
            yield
            em_last[0] = stt(DN, bd[:, 0:256], -1.0, EM, MUL, MAX, td, te)
            tt_(DN, bd[:, 0:256], DN, MAX)
            t = recip_(DN, DN)
            sring.free(id_, t)
            for n in range(2):
                t = tt_(HB[:, 2 * n:2 * n + 2, :], v3(nb[n][1], 2), DN.unsqueeze(1).to_broadcast([128, 2, 256]),
                        MUL, tn_, A.last)
                sring.free(nb[n][0], t)
            ts = [act(SQ[:, w, :], HB[:, 2 * w:2 * w + 2, :].rearrange("p a b -> p (a b)"), ACT.Square, t, sq_free[w])
                  for w in range(2)]
            tt_(SQ[:, 0, :], SQ[:, 0, :], SQ[:, 1, :], ADD, *ts, E=G)
            tg = tt_(SQ[:, 0, 0:256], SQ[:, 0, 0:256], SQ[:, 0, 256:512], ADD, E=G)
            yield
            i, bk, fr = sring.get()
            sq_free[0] = sq_free[1] = mm(bk[:, 0:256], ones, SQ[:, 0, 0:256], tg, *fr)
            yield
            ta = rs_from(RS2, bk[:, 0:256], 512, sq_free[1])
            sring.free(i, ta)
            yield
            for j in range(4):
                stt(HB[:, j, :], HB[:, j, :], cv("m_norm", 4 * h + j), RS2, MUL, MUL, ta)
            t = tt_(HB, HB, OZ[:, 4 * h:4 * h + 4, :], MUL)
            ta = act(YS[:, 16 + 4 * h:20 + 4 * h, 0:256], HB, ACT.Copy, t, T_last[0])
            yield
            tt_(YS[:, 16 + 4 * h:20 + 4 * h, 256:512], HB,
                YS[:, 16 + 4 * h:20 + 4 * h, 0:256].bitcast(F32), SUB, ta)
        em_last = [None]
        ys_t = {}
        T_last = [None]

        def all_heads():
            for h in range(4):
                yield from attend(h)
                yield

        every[0] = 8
        heads = start(all_heads())
        xl_t, th_t = {}, {}

        def xl_epi(j):
            i, XC = j % 2, XCb[(j // 2) % 2]

            def f(bank, tt):
                tv = evac_rs(XL[:, i, 3:259], bank, tt)
                t = conv(XC[:, i, :], XL[:, i, :], lambda t: cv("conv_l_w", 16 * t + j), cv("conv_l_b", j), 4, tv)
                ta = act(YS[:, j, 0:256], XC[:, i, :], ACT.Copy, t)

                def rest():
                    xl_t[j] = tt_(YS[:, j, 256:512], XC[:, i, :], YS[:, j, 0:256].bitcast(F32), SUB, ta)
                deferred.append(rest)
                return (tv,)
            return f

        def zl_epi(j):
            ZB = ZBb[(j // 2) % 2]

            def f(bank, tt):
                tv = evac_rs(ZB[:, j % 2, :], bank, tt)
                if j % 2:
                    th_t["z", j // 2] = act(ZB, ZB, ACT.Silu, tv)
                return (tv,)
            return f

        def ri_epi(j, buf, nm):
            def f(bank, tt):
                th_t[nm, j] = act(buf[:, j % 2, :], bank[:, 0:256], ACT.Sigmoid, tt, bias=cv(nm, j))
                return (th_t[nm, j],)
            return f

        def lru_tail(p):
            XC, ZB = XCb[p % 2], ZBb[p % 2]
            for i in range(2):
                k = 2 * p + i
                act(TH[:, i, :], RB[:, i, :], ACT.Tanh, t_sp, scale=SP8[:, k:k + 1])
            tu = tt_(IB, IB, XC, MUL, th_t["lru_bx", 2 * p + 1])
            act(XC, TH, ACT.Ln, tu, bias=1.0)
            ta = act(TH, TH, ACT.Ln, scale=2.0)
            yield
            t = tt_(TH, TH, XC, SUB, ta)
            for i in range(2):
                k = 2 * p + i
                act(RB[:, i, :], RB[:, i, :], ACT.Exp, scale=NSP8[:, k:k + 1])
            yield
            ta = act(TH, TH, ACT.Exp, t, scale=0.5)
            yield
            t = tt_(IB, IB, TH, MUL, ta)
            for i in range(2):
                scan_(XC[:, i, :], RB[:, i, :], IB[:, i, :], 0.0, MUL, ADD)
            t = tt_(XC, XC, ZB, MUL)
            yield
            ta = act(YS[:, 2 * p:2 * p + 2, 0:256], XC, ACT.Copy, t)
            yield
            tt_(YS[:, 2 * p:2 * p + 2, 256:512], XC, YS[:, 2 * p:2 * p + 2, 0:256].bitcast(F32), SUB, ta)

        V.wait(T.last)
        A.wait(T.last)
        tail = None
        for p in range(8):
            for i in range(2):
                gemm("e_w_in", 128 * (2 * p + i), 16, xn, xl_epi(2 * p + i))
            for i in range(2):
                gemm("e_w_in", 4096 + 128 * (2 * p + i), 16, xn, zl_epi(2 * p + i))
            flush()
            run_deferred()
            if tail:
                finish(tail)
            for nm, wn, buf in (("lru_ba", "e_lru_wa", RB), ("lru_bx", "e_lru_wx", IB)):
                for i in range(2):
                    j = 2 * p + i
                    gemm(wn, (j, 0), 1, lambda k: YS[:, j, :], ri_epi(j, buf, nm), xl_t[j])
            flush()
            tail = start(lru_tail(p))

        def out_proj(name, early, late, ys, begin):
            now = {}

            def epi(n):
                def f(bank, tt):
                    X = now["x"]
                    t = tt_(X[:, n, :], X[:, n, :], bank[:, 0:256], ADD, tt, now["load"])
                    now["norm"].tile(t)
                    return (t,)
                return f
            flush()
            T.wait(V.last)
            parts = []
            for n in range(4):
                i, bank, fr = gring.get()
                T.wait(*fr)
                products(bank, name, 128 * n, early, ys, last=False)
                parts.append((i, bank))
            flush()
            now["x"], now["load"], now["norm"] = begin()
            run_deferred()
            run_deferred()
            T.wait(V.last)
            for n, (i, bank) in enumerate(parts):
                tt = products(bank, name, 128 * n, late, ys, first=False)
                close(i, bank, tt, epi(n))
            for n in range(4, 16):
                gemm(name, 128 * n, list(early) + list(late), ys, epi(n))
            flush()
            return now["x"], now["norm"], V.last


        finish(heads)
        m = Map(nc, XT, end)
        TMP = v3(m("TMP1", 512), 2)
        X = v3(m("X1", 16 * 256), 16)
        t_x = load(X, args["x"], V.last, A.last, T.last)

        def begin1():
            finish(tail)
            every[0] = 16
            return X, t_x, Norm(X, "o_norm", TMP)
        X, nm, t = out_proj("e_w_out", list(range(16, 32)) + list(range(14)), [14, 15], lambda k: YS[:, k, :], begin1)

        stores = [0]

        def store_x(X, t):
            S.op(lambda e: e.dma_start(scratch, X).then_inc(st_sem, 16), t, inc=False, chain=False)
            stores[0] += 16
            return (st_sem, stores[0])

        t_st = store_x(X, t)
        nm.end()
        barrier(V, A)
        m = Map(nc, R0, end)
        YS = v3(m("YS2", 32 * 512, F32R), 32)
        CSX = m("CSX", 384, rows=64)
        DTR = m("DTR", 256, rows=64)
        NCST = m("NCST", 128)
        DTT = m("DTT", 128)
        ZB = v3(m("ZB2", 4 * 256), 4)
        XDT = v3(m("XDT", 1024), 2)
        CBm = m("CBm", 384)
        DB = [m(f"DB{i}", 384) for i in range(3)]
        YB = v3(m("YB", 1024), 4)
        RS3 = m("RS3", 256)
        XV1 = v3(m("XV1", 6 * 256), 6)
        assert m.at <= XT + 2048
        m = Map(nc, XT + 2048, end)
        XV = [v3(m("XV0", 6 * 256), 6), XV1]
        XP = v3(m("XP", 6 * 259), 6)
        RT = [XV[1][0:64, i, :] for i in range(4)]
        ONE64 = XV[1][0:64, 4, :]
        EA = XV[1][0:64, 5, 0:1]
        V.wait(t_st)
        A.wait(t_st)
        memset_(XP[:, :, 0:3], 0.0, E=V)

        dt_tok = []

        def dt_epi(bank, tt):
            tv = evac_rs(RT[0], bank, tt, rows=slice(0, 64))
            t_dt.append(tv)
            return (tv,)

        t_dt = []

        def dt_side():
            while not t_dt:
                yield
            t = ts_(RT[0], RT[0], cv("dt_bias", 0, rows=slice(0, 64)), None, ADD, None, t_dt[0])
            memset_(ONE64, 1.0, E=V)
            sp = softplus_steps(DTR, RT[0], RT[1], RT[2], V.last)
            yield from sp
            ta = act(EA, cv("a_log", 0, rows=slice(0, 64)), ACT.Exp)
            yield
            ts_(RT[3], DTR, EA, -1.0, MUL, MUL, ta)
            scan_(CSX[:, 0:256], ONE64, RT[3], 0.0, MUL, ADD)
            dt_tok.append(copy_(CSX[:, 256:384], CSX[:, 128:256]))
            yield
            i, bk, fr = sring.get()
            idn = ident[0:64, 0:64]
            transpose(bk[:, 0:64], CSX[:, 0:128], idn, *fr, dt_tok[0], inc=False)
            transpose(bk[:, 64:128], CSX[:, 128:256], idn, inc=False)
            transpose(bk[:, 128:192], DTR[:, 0:128], idn, inc=False)
            tt = transpose(bk[:, 192:256], DTR[:, 128:256], idn)
            yield
            ts_(NCST, bk[:, 0:128], -1.0, None, MUL, None, tt)
            t = copy_(DTT, bk[:, 128:256])
            sring.free(i, t)
            A.wait(t)
            dts_done.append(t)

        dts_done = []
        every[0] = 8
        gemm("o_w_in", 10240, 16, xn, dt_epi, width=64)
        flush()
        dts = start(dt_side())
        xv_free = [None, None]
        z_tok, v_tok, zb_free = {}, {}, [None]

        def xv_epi(g, s):
            ch = [32 + g, 40 + g, 4 * g, 4 * g + 1, 4 * g + 2, 4 * g + 3]

            def f(bank, tt):
                tv = evac_rs(XP[:, s, 3:259], bank, tt)
                k = ch[s]
                t = conv(XV[g % 2][:, s, :], XP[:, s, :], lambda t: cv("o_conv_w", 48 * t + k),
                         cv("o_conv_b", k), 4, tv, xv_free[g % 2])
                if s == 5:
                    v_tok[g] = act(XV[g % 2], XV[g % 2], ACT.Silu, t)
                return (tv,)
            return f

        def zs_epi(g, j):
            def f(bank, tt):
                tv = evac_rs(ZB[:, j, :], bank, tt)
                if j == 3:
                    z_tok[g] = act(ZB, ZB, ACT.Silu, tv)
                return (tv,)
            return f

        def ssd(g):
            B_, C_, XS_ = XV[g % 2][:, 0, :], XV[g % 2][:, 1, :], XV[g % 2][:, 2:6, :]
            tk = v_tok[g]
            ic, bc, fr = sring.get()
            mm(bc[:, 0:256], B_[:, 0:128], C_, *fr, tk, start=True, stop=True, inc=False)
            tt = mm(bc[:, 256:384], B_[:, 128:256], C_[:, 128:256], start=True, stop=True)
            tx = []
            for t in range(2):
                i, b, fr = sring.get()
                for j in range(4):
                    t2 = transpose(b[:, 128 * j:128 * j + 128], XS_[:, j, 128 * t:128 * t + 128], ident, *fr,
                                   inc=(j == 3))
                tx.append((i, b, t2))
            yield
            ta = act(CBm, bc[:, 0:384], ACT.Copy, tt, cb_last[0])
            sring.free(ic, ta)
            for t in range(2):
                i, b, t2 = tx[t]
                tv = tt_(XDT[:, t, :].rearrange("p (h d) -> p h d", h=8), b.rearrange("p (h d) -> p h d", h=8),
                         DTT[:, 64 * t + 8 * g:64 * t + 8 * g + 8].unsqueeze(2).to_broadcast([128, 8, 64]),
                         MUL, t2, y_last[0])
                sring.free(i, tv)
            t_xdt = V.last
            tg = {}
            banks = {}

            def bc_mm(e):
                h = 8 * g + e
                i, b, fr = sring.get()
                mm(b[:, 0:384], identr, maskr, *fr, start=True, stop=False, inc=False)
                banks[e] = (i, b, mm(b[:, 0:384], ident[0:64, h:h + 1].to_broadcast([64, 128]), CSX,
                                     start=False, stop=True))

            def dec(e):
                i, b, t = banks[e]
                h = 8 * g + e
                d = DB[e % 3]
                act(d[:, 0:256], b[:, 0:256], ACT.Exp, t, d_free[e % 3], bias=NCST[:, h:h + 1])
                ta = act(d[:, 256:384], b[:, 256:384], ACT.Exp, bias=NCST[:, 64 + h:65 + h])
                sring.free(i, ta)
                return lambda: mask_(e, d, ta)

            def mask_(e, d, ta):
                cb_last[0] = tg[e] = tt_(d, d, CBm, MUL, ta)

            yb = {}

            def y_mm(e):
                if e % 4 == 0:
                    i, b, fr = sring.get()
                    yb[e // 4] = [i, b, None]
                    T.wait(*fr)
                i, b, _ = yb[e // 4]
                c = 256 * ((e % 4) // 2)
                r = 64 * (e % 2)
                d = DB[e % 3]
                mm(b[r:r + 64, c:c + 256], XDT[:, 0, 64 * e:64 * e + 64], d[:, 0:256], tg[e], t_xdt,
                   start=True, stop=False, inc=False)
                t = mm(b[r:r + 64, c + 128:c + 256], XDT[:, 1, 64 * e:64 * e + 64], d[:, 256:384],
                       start=False, stop=True)
                d_free[e % 3] = t
                yb[e // 4][2] = t

            bc_mm(0)
            yield
            masks = {}
            for e in range(10):
                if e < 8:
                    masks[e] = dec(e)
                if 0 < e < 9:
                    masks[e - 1]()
                if e < 7:
                    bc_mm(e + 1)
                if e > 1:
                    y_mm(e - 2)
                if e < 9:
                    yield
            y_last[0] = T.last
            yield
            for n in range(2):
                i, b, t = yb[n]
                for j in range(2):
                    q = 2 * n + j
                    tv = stt(YB[:, q, :], XS_[:, q, :], cv("d_skip", 4 * g + q), b[:, 256 * j:256 * j + 256],
                             MUL, ADD, t, A.last)
                sring.free(i, tv)
            xv_free[g % 2] = tv
            t = tt_(YB, YB, ZB, MUL, z_tok[g])
            zb_free[0] = t
            norms.append(start(ssd_norm(g, t)))

        norms = []

        def ssd_norm(g, t):
            yield
            ts = [act(SQ[:, w, :], YB[:, 2 * w:2 * w + 2, :].rearrange("p a b -> p (a b)"), ACT.Square, t, sq_free[w])
                  for w in range(2)]
            tt_(SQ[:, 0, :], SQ[:, 0, :], SQ[:, 1, :], ADD, *ts, E=G)
            tg = tt_(SQ[:, 0, 0:256], SQ[:, 0, 0:256], SQ[:, 0, 256:512], ADD, E=G)
            yield
            i, bk, fr = sring.get()
            sq_free[0] = sq_free[1] = mm(bk[:, 0:256], ones, SQ[:, 0, 0:256], tg, *fr)
            yield
            ta = rs_from(RS3, bk[:, 0:256], 512, sq_free[1])
            sring.free(i, ta)
            yield
            for j in range(4):
                t = stt(YB[:, j, :], YB[:, j, :], cv("gnorm", 4 * g + j), RS3, MUL, MUL, ta)
            yield
            ta = act(YS[:, 4 * g:4 * g + 4, 0:256], YB, ACT.Copy, t)
            yield
            tt_(YS[:, 4 * g:4 * g + 4, 256:512], YB, YS[:, 4 * g:4 * g + 4, 0:256].bitcast(F32), SUB, ta)

        y_last, cb_last = [None], [None]
        d_free = [None] * 3
        prev = None
        every[0] = 8
        for g in range(8):
            if g == 1:
                finish(dts)
            cols = [8192 + 128 * g, 9216 + 128 * g] + [4096 + 512 * g + 128 * j for j in range(4)]
            for s in range(6):
                gemm("o_w_in", cols[s], 16, xn, xv_epi(g, s))
            flush()
            if prev is not None:
                finish(prev)
            finish(dts)
            if g == 7:
                m = Map(nc, XT, end)
                TMP = v3(m("TMP2", 512), 2)
                X = v3(m("X2", 16 * 256), 16)
                t_x = load(X, scratch, V.last, A.last, T.last, t_st)
            for j in range(4):
                gemm("o_w_in", 512 * g + 128 * j, 16, xn, zs_epi(g, j))
                if j == 0:
                    prev = start(ssd(g))
            flush()

        def begin2():
            finish(prev, *norms)
            every[0] = 16
            return X, t_x, Norm(X, "norm_mix", TMP, first="final_norm")
        X, nm, t = out_proj("o_w_out", range(28), range(28, 32), lambda k: YS[:, k, :], begin2)
        nm.end(RST)
        ta = A.last

        def norm_x(X):
            for k in range(16):
                t = stt(X[:, k, :], X[:, k, :], cv("final_norm", k), RS1, MUL, MUL, ta)
                if k % 4 == 3:
                    yield
            x_st.append(store_x(X, t))
        x_st = []
        every[0] = 8
        barrier(V, A, G)
        nx = start(norm_x(X))

        m = Map(nc, R0, end)
        GOS = v3(m("GOS", 8 * 512, F32R), 8)
        r1 = m.at
        PSM = v3(m("PSM", 16 * 256), 16)
        DOS = v3(m("DOS", 8 * 512, F32R), 8)
        r2 = m.at
        MS = v3(Map(nc, R0, end)("MS", 16 * 512, F32R), 16)
        DQ0 = v3(m("DQ0", 4 * 256), 4)
        DVT0 = v3(m("DVT0", 1024), 2)
        r3 = m.at
        DBI = m("DBI", 1024)
        P1 = [m(f"P1{i}", 32) for i in range(10)]
        PW = m("PW", 2 * 8 * 32).rearrange("p (c l a) -> p c l a", c=2, l=8)
        ZS = v3(Map(nc, m.at, end)("ZS", 8 * 512, F32R), 8)
        TB = m("TB", 2 * 2 * 2 * 256).rearrange("p (s c a b) -> p s c a b", s=2, c=2, a=2)
        BR = v3(m("BR", 8 * 128), 8)
        BI = v3(m("BI", 8 * 128), 8)
        CR = v3(m("CR", 32 * 32), 32)
        CI = v3(m("CI", 32 * 32), 32)
        US = v3(m("US", 8 * 256), 8)
        BX = [v3(m(f"BX{i}", 512), 2) for i in range(2)]
        BS = v3(m("BS", 512), 2)
        HH = v3(m("HH", 512), 2)
        PT = m("PT", 2 * 64)
        CUM = m("CUM", 256)
        RS4 = m("RS4", 256)
        mt = Map(nc, r1, r2)
        CRR, CIR = v3(mt("CRR", 1024), 32), v3(mt("CIR", 1024), 32)
        C1, C2 = v3(mt("C1", 1024), 32), v3(mt("C2", 1024), 32)
        t_b1 = load(BR, args["b_re"], T.last, V.last, A.last)
        t_b2 = load(BI, args["b_im"])
        t_c1 = load(CRR, args["c_re"])
        t_c2 = load(CIR, args["c_im"])

        def s5_consts():
            lr, dt, mag, th, r, s1, c1, den, fr_, fi_ = P1
            li = cv("a_im", 0, 32)
            ts_(lr, cv("a_re", 0, 32), -1e-4, None, MIN, None)
            ta = act(dt, cv("log_dt", 0, 32), ACT.Exp)
            tv = tt_(mag, dt, lr, MUL, ta)
            act(mag, mag, ACT.Exp, tv)
            tt_(th, dt, li, MUL)
            ts_(r, th, 1.0 / TWO_PI, 12582912.0, MUL, ADD)
            ts_(r, r, -12582912.0, None, ADD, None)
            yield
            ts_(c1, r, -6.28125, None, MUL, None)
            tt_(th, th, c1, ADD)
            stt(th, r, -0.0019350051879882812, th, MUL, ADD)
            stt(th, r, -3.0199160505063e-07, th, MUL, ADD)
            tv = ts_(th, th, 3.1415925, -3.1415925, MIN, MAX)
            yield
            ta = act(s1, th, ACT.Sin, tv)
            ta = act(c1, th, ACT.Sin, scale=0.5)
            yield
            tt_(c1, c1, c1, MUL, ta)
            ts_(c1, c1, -2.0, 1.0, MUL, ADD)
            yield
            copy_(PW[:, 0, 0, :], c1)
            copy_(PW[:, 1, 0, :], s1)
            for l in range(1, 8):
                c_, s_ = PW[:, 0, l - 1, :], PW[:, 1, l - 1, :]
                tt_(den, s_, s_, MUL)
                tt_(fr_, c_, c_, MUL)
                tt_(PW[:, 0, l, :], fr_, den, SUB)
                tv = stt(PW[:, 1, l, :], s_, 2.0, c_, MUL, MUL)
                if l % 2:
                    yield
            pw_tok.append(tv)
            yield
            tt_(fr_, mag, c1, MUL)
            ts_(fr_, fr_, -1.0, None, ADD, None)
            tt_(fi_, mag, s1, MUL)
            tt_(c1, lr, lr, MUL)
            tt_(den, li, li, MUL)
            tt_(den, den, c1, ADD)
            recip_(den, den)
            yield
            tt_(c1, fr_, lr, MUL)
            tt_(s1, fi_, li, MUL)
            tt_(r, c1, s1, ADD)
            tt_(c1, fi_, lr, MUL)
            tt_(s1, fr_, li, MUL)
            tt_(c1, c1, s1, SUB)
            tt_(fr_, r, den, MUL)
            tt_(fi_, c1, den, MUL)
            yield
            frb, fib = [x.unsqueeze(2).to_broadcast([128, 32, 32]) for x in (fr_, fi_)]
            tt_(C1, CRR, frb, MUL, t_c1, t_c2)
            tt_(C2, CIR, fib, MUL)
            tt_(CR, C1, C2, SUB)
            yield
            tt_(C1, CRR, fib, MUL)
            tt_(C2, CIR, frb, MUL)
            tv = stt(CI, C1, -1.0, C2, MUL, SUB)
            cc_tok.append(tv)

        pw_tok, cc_tok = [], []
        s5c = start(s5_consts())
        us_t = {}

        def u_epi(j):
            def f(bank, tt):
                if j == 2:
                    finish(nx)
                tv = evac_rs(US[:, j, :], bank, tt, *x_st)
                us_t[j] = tv
                return (tv,)
            return f

        for j in range(8):
            gemm("w_in_2", 128 * j, 16, xn, u_epi(j))
        flush()
        finish(s5c)

        every[0] = 8
        gring, sring, yring = ring(0, 1, 2), ring(3, 4, 5, 6), ring(7)
        mt = Map(nc, r1, r2)
        GQ = [mt(f"GQ{i}", 256) for i in range(2)]
        GK = [mt(f"GK{i}", 256) for i in range(2)]
        GR = [v3(mt(f"GR{i}", 512), 2) for i in range(2)]
        GVT = [v3(mt("GVT0", 1024), 2), v3(DBI, 2)]
        GE1s = [mt("GE10", 256), m("GE11", 256)]
        GE2 = mt("GE2", 256)
        GE3 = mt("GE3", 256)
        KTM = mt("KTM", 7 * 128).rearrange("p (a b) -> p a b", a=7)
        SC = v3(mt("SC", 256), 2)
        ST = mt("ST", 7 * 256).rearrange("p (a b) -> p a b", a=7)
        ALR = mt("ALR", 256, rows=16)
        WG = mt("WG", 512, rows=16)
        DLs = [mt(f"DL{i}", 8) for i in range(2)]
        t_wg = load(WG, args["w_gate"], V.last, A.last)
        MAG = P1[2]
        OB = v3(mt("OB", 512), 2)

        def phases(b):
            tb = TB[:, b % 2]
            a = slice(2 * b, 2 * b + 2)
            G.wait(tb_free[b % 2])
            memset_(tb[:, 0, :, 0:1], 1.0, E=G)
            memset_(tb[:, 1, :, 0:1], 0.0, E=G)
            for l in range(8):
                d = 1 << l
                q = min(d, 64)
                Cq = PW[:, 0, l, a].unsqueeze(2).to_broadcast([128, 2, q])
                Sq = PW[:, 1, l, a].unsqueeze(2).to_broadcast([128, 2, q])
                t1 = v3(PT, 2)[:, :, 0:q]
                for o in range(0, d, q):
                    x, y = slice(o, o + q), slice(d + o, d + o + q)
                    tt_(tb[:, 0, :, y], tb[:, 0, :, x], Cq, MUL, E=G)
                    tt_(t1, tb[:, 1, :, x], Sq, MUL, E=G)
                    tt_(tb[:, 0, :, y], tb[:, 0, :, y], t1, SUB, E=G)
                    tt_(tb[:, 1, :, y], tb[:, 0, :, x], Sq, MUL, E=G)
                    tt_(t1, tb[:, 1, :, x], Cq, MUL, E=G)
                    tg = tt_(tb[:, 1, :, y], tb[:, 1, :, y], t1, ADD, E=G)
                    if l > 5 or o + q == d:
                        yield
            tb_t[b] = tg

        tb_free, tb_t = [None, None], {}
        bx_free, hh_free = [None, None], [None]
        y_bank, bs_free = [], []

        def s5_tile(n):
            ft, q = n // 4, n % 4
            rows = slice(32 * q, 32 * q + 32)
            tb = TB[:, (n // 2) % 2]
            cc, ss = tb[:, 0, n % 2, :], tb[:, 1, n % 2, :]
            c2 = cc.unsqueeze(1).to_broadcast([128, 2, 256])
            s2 = ss.unsqueeze(1).to_broadcast([128, 2, 256])
            b = BX[n % 2]
            i, bk, fr = sring.get()
            mm(bk[:, 0:256], BR[rows, ft, :], US[rows, ft, :], *fr, us_t[ft], t_b1, t_b2,
               start=True, stop=True, inc=False)
            tt = mm(bk[:, 256:512], BI[rows, ft, :], US[rows, ft, :], start=True, stop=True)
            yield
            act(b, v3(bk, 2), ACT.Copy, tt, bx_free[n % 2])
            act(BS[:, 0, :], bk[:, 256:512], ACT.Copy, *bs_free)
            ta = act(BS[:, 1, :], bk[:, 0:256], ACT.Copy, scale=-1.0)
            sring.free(i, ta)
            yield
            tg = tt_(BS, BS, s2, MUL, ta, E=G)
            tt_(b, b, c2, MUL, ta, tb_t[n // 2])
            yield
            tt_(b, b, BS, ADD, tg)
            mg = MAG[:, n:n + 1].to_broadcast([128, 256])
            for c in range(2):
                tv = scan_(BS[:, c, :], mg, b[:, c, :], 0.0, MUL, ADD)
            tt_(b[:, 0, :], BS[:, 1, :], ss, MUL, tv, E=G)
            tg = tt_(b[:, 1, :], BS[:, 0, :], ss, MUL, E=G)
            tv = tt_(HH, BS, c2, MUL, hh_free[0])
            tb_free[(n // 2) % 2] = tv
            bs_free[:] = [tv, tg]
            if n % 2:
                batch_done.append(n // 2)
            yield
            yield
            tt_(HH[:, 0, :], HH[:, 0, :], b[:, 0, :], SUB, tg)
            tv = tt_(HH[:, 1, :], HH[:, 1, :], b[:, 1, :], ADD)
            bx_free[n % 2] = tv
            yield
            if q == 0:
                y_bank[:] = yring.get()
                T.wait(*y_bank[2])
            iy, by, _ = y_bank
            mm(by[rows, 0:256], CR[:, n, :], HH[:, 0, :], tv, start=True, stop=False, inc=False)
            ty = mm(by[rows, 0:256], CI[:, n, :], HH[:, 1, :], start=False, stop=True)
            hh_free[0] = ty
            if q == 3:
                yield
                tv = stt(US[:, ft, :], US[:, ft, :], cv("ssm_d", ft), by[:, 0:256], MUL, ADD, ty)
                yring.free(iy, tv)

        batch_done = []

        def s5():
            gens, ph = [], phases(0)
            nb, at, due, n = 1, 0, 0, 0
            while True:
                if ph is not None and not step(ph):
                    ph = None
                if ph is None and nb < 16 and (nb < 2 or nb - 2 in batch_done):
                    ph = phases(nb)
                    nb += 1
                gens = [g for g in gens if step(g)]
                if n < 32 and at >= due and (n // 2) in tb_t:
                    g = s5_tile(n)
                    step(g)
                    gens.append(g)
                    n += 1
                    due = at + 5
                at += 1
                if n == 32 and not gens:
                    break
                yield
            yield
            ta = act(US, US, ACT.Gelu_apprx_tanh, V.last)
            yield
            G.wait(T.last)
            V.wait(G.last, T.last)
            t_zs.append(split(ZS, US, ta, V.last, T.last, G.last))

        t_st = x_st[0]
        for e_ in (A, G, T):
            e_.wait(cc_tok[0], pw_tok[0])
        t_zs = []
        s5g = start(s5())

        g_tok = {}

        def alr_epi(bank, tt):
            tv = evac_rs(ALR, bank, tt, rows=slice(0, 16))
            g_tok["alr"] = tv
            return (tv,)

        V.wait(t_st)
        A.wait(t_st)
        gemm("w_in_2", 4096, 16, xn, alr_epi, width=16)

        def save(dst, key, act_fn=None, last=True):
            def f(bank, tt):
                tv = evac_rs(dst, bank, tt, gla_free[0])
                g_tok[key] = tv
                return (tv,)
            return f
        gla_free = [None]

        def vt_epi(dst, key):
            def f(b0, b1, tt):
                act(dst[:, 0, :], b0, ACT.Copy, tt, gla_free[0], scale=RST[:, 0:1])
                t = act(dst[:, 1, :], b1, ACT.Copy, scale=RST[:, 1:2])
                g_tok[key] = t
                return t
            return f

        def rms_tail(bk_i, bk, t_o, wcols, OS, OB, h, gate):
            ta = act(SQ[:, 0, :], bk, ACT.Square, t_o, sq_free[0], sq_free[1])
            tg = tt_(SQ[:, 0, 0:256], SQ[:, 0, 0:256], SQ[:, 0, 256:512], ADD, ta, E=G)
            yield
            ia, ba, fr = sring.get()
            tt = mm(ba[:, 0:256], ones, SQ[:, 0, 0:256], tg, *fr)
            sq_free[0] = tt
            yield
            ta = rs_from(RS4, ba[:, 0:256], 256, tt, V.last)
            sring.free(ia, ta)
            yield
            for j in range(2):
                t = stt(OB[:, j, :], bk[:, 256 * j:256 * j + 256], wcols(j), RS4, MUL, MUL, ta)
            sring.free(bk_i, t)
            if gate is not None:
                t = tt_(OB, OB, gate, MUL)
            ta = act(OS[:, 2 * h:2 * h + 2, 0:256], OB, ACT.Copy, t)
            yield
            tt_(OS[:, 2 * h:2 * h + 2, 256:512], OB, OS[:, 2 * h:2 * h + 2, 0:256].bitcast(F32), SUB, ta)

        main_done = {}

        def decays(h):
            GE1, DL = GE1s[h % 2], DLs[h % 2]
            for _ in range(3 if h else 0):
                yield
            while "alr" not in g_tok:
                yield
            i, bk, fr = sring.get()
            tt = mm(bk[:, 0:256], WG[:, 128 * h:128 * h + 128], ALR, *fr, g_tok["alr"], t_wg)
            yield
            act(GE1, bk[:, 0:256], ACT.Identity, tt, T.last, bias=cv("gla_b", h))
            sring.free(i, A.last)
            act(GE2, GE1, ACT.Abs)
            act(GE2, GE2, ACT.Exp, scale=-1.0)
            ta = act(GE2, GE2, ACT.Ln, bias=1.0)
            yield
            stt(GE1, GE1, 0.0, GE2, MIN, SUB, ta)
            tv = scan_(CUM, cs("creset"), GE1, 0.0, MUL, ADD)
            c3 = CUM.rearrange("p (a b) -> p a b", a=8)
            lastc = c3[:, :, 31:32]
            tv = tt_(GE3.rearrange("p (a b) -> p a b", a=8), lastc.to_broadcast([128, 8, 32]), c3, SUB)
            yield
            act(GE1, CUM, ACT.Exp, tv, scale=1.0 / 16)
            act(GE2, CUM, ACT.Exp, scale=-1.0 / 16)
            act(GE3, GE3, ACT.Exp, scale=1.0 / 16)
            dec_t[h] = act(DL.unsqueeze(2), lastc, ACT.Exp, scale=1.0 / 16)

        dec_t = {}

        def gla(h):
            hv = h % 2
            q_, k_, r_, v_ = GQ[h % 2], GK[h % 2], GR[h % 2], GVT[h // 2]
            t_q, t_k, t_r, t_v = [g_tok[x] for x in "qkrv"]
            GE1, DL = GE1s[h % 2], DLs[h % 2]
            act(r_, r_, ACT.Silu, t_r)
            stt(GE1, q_, 128.0 ** -0.5, GE1, MUL, MUL, dec_t[h], t_q)
            tt_(GE3, k_, GE3, MUL, t_k)
            tv = tt_(GE2, k_, GE2, MUL)
            yield
            i, bk, fr = sring.get()
            for j in range(2):
                transpose(bk[:, 128 * j:128 * j + 128], GE3[:, 128 * j:128 * j + 128], ident, tv, *fr, inc=False)
            for j in range(2):
                tt = mm(bk[:, 256 + 128 * j:384 + 128 * j], GE2[:, 128 * j:128 * j + 128],
                        GE1[:, 128 * j:128 * j + 128])
            yield
            for c in range(7):
                ta = act(KTM[:, c, :], bk[:, 128 * (c // 4):128 * (c // 4) + 128], ACT.Copy, tt,
                         scale=cs("cmask", 1, c % 4))
            tv = tt_(SC, v3(bk[:, 256:512], 2), cs("gmask").unsqueeze(1).to_broadcast([128, 2, 128]), MUL, tt, ta)
            sring.free(i, ta, tv)
            yield
            banks = []

            def kv(p):
                i, bk, fr = sring.get()
                for c in range(2 * p, min(2 * p + 2, 7)):
                    tt = mm(bk[:, 256 * (c % 2):256 * (c % 2) + 256], KTM[:, c, :],
                            v_[:, c // 4, 256 * hv:256 * hv + 256], *fr, ta, t_v)
                banks.append((i, bk, tt))

            def states(p):
                i, bk, tt = banks[p]
                for c in range(2 * p, min(2 * p + 2, 7)):
                    src = bk[:, 256 * (c % 2):256 * (c % 2) + 256]
                    if c == 0:
                        ts = copy_(ST[:, 0, :], src, tt)
                    else:
                        ts = stt(ST[:, c, :], ST[:, c - 1, :], DL[:, c:c + 1], src, MUL, ADD, tt)
                sring.free(i, ts)
                return ts

            kv(0)
            yield
            kv(1)
            states(0)
            yield
            kv(2)
            states(1)
            yield
            kv(3)
            states(2)
            yield
            ts = states(3)
            yield
            i, bk, fr = sring.get()
            for d in range(2):
                for j in range(2):
                    mm(bk[:, 256 * d + 128 * j:256 * d + 128 * j + 128],
                       v_[:, j, 256 * hv + 128 * d:256 * hv + 128 * d + 128], SC[:, j, :], *fr, tv, ts,
                       start=(j == 0), stop=False, inc=False)
                for c in range(1, 8):
                    tt = mm(bk[:, 256 * d + 32 * c:256 * d + 32 * c + 32], ST[:, c - 1, 128 * d:128 * d + 128],
                            GE1[:, 32 * c:32 * c + 32], start=False, stop=(c == 7))
            main_done[h] = tt
            V.wait(tt)
            A.wait(tt)
            yield
            yield from rms_tail(i, bk, tt, lambda j: cv("gla_norm", j), GOS, OB, h, r_)
            gla_free[0] = V.last

        def go_on(gen, done, h):
            while h not in done:
                step(gen)

        prev, cur = None, None
        for h in range(4):
            dc = start(decays(h))
            if h % 2 == 0:
                gemm_t("w_in_2", 2048 + 512 * (h // 2), 16, xn, vt_epi(GVT[h // 2], "v"))
            gemm("w_in_2", 1024 + 128 * h, 16, xn, save(GQ[h % 2], "q"))
            gemm("w_in_2", 1536 + 128 * h, 16, xn, save(GK[h % 2], "k"))
            if prev:
                finish(prev)
            for j in range(2):
                gemm("w_in_2", 3072 + 256 * h + 128 * j, 16, xn, save(GR[h % 2][:, j, :], "r"))
            flush()
            if cur:
                go_on(cur, main_done, h - 1)
            finish(dc)
            prev, cur = cur, start(gla(h))

        mt = Map(nc, r1, r2)
        DQ = [DQ0, v3(mt("DQ1", 4 * 256), 4)]
        DVT = [DVT0, v3(mt("DVT1", 1024), 2)]
        DS = [mt(f"DS{i}", 384) for i in range(2)]
        WT = mt("WT", 384)
        OBD = v3(mt("OBD", 512), 2)
        DST = mt("DST", 16)
        LQ = mt("LQ", 8)
        DNW = mt("DNW", 2)
        dq_t, dv_t = {}, {}
        dq_free, dv_free = [None, None], [None, None]
        t_db = []

        def dq_epi(h, j):
            def f(bank, tt):
                tv = evac_rs(DQ[h % 2][:, j, :], bank, tt, dq_free[h % 2])
                dq_t[h] = tv
                return (tv,)
            return f

        def dv_epi(n):
            def f(b0, b1, tt):
                act(DVT[n % 2][:, 0, :], b0, ACT.Copy, tt, dv_free[n % 2], scale=RST[:, 0:1])
                dv_t[n] = act(DVT[n % 2][:, 1, :], b1, ACT.Copy, scale=RST[:, 1:2])
                return dv_t[n]
            return f

        def lam():
            ts_(DNW, cv("diff_norm", 0, 2), 0.8, None, MUL, None)
            dl = cv("diff_lam", 0, 4).rearrange("p (a b) -> p a b", b=2)
            tv = tt_(LQ[:, 0:2], dl[:, :, 0], dl[:, :, 1], MUL)
            i, bk, fr = sring.get()
            tt = mm(bk[:, 0:2], ones, LQ[:, 0:2], tv, *fr)
            yield
            ta = act(LQ[:, 2:4], bk[:, 0:2], ACT.Exp, tt)
            sring.free(i, ta)
            yield
            tt_(LQ[:, 4:5], LQ[:, 3:4], LQ[:, 2:3], SUB, ta)
            ts_(LQ[:, 4:5], LQ[:, 4:5], -(0.8 - 0.6), None, ADD, None)

        def diff(h):
            Q = DQ[h % 2]
            VT = DVT[(h // 2) % 2]
            if h == 0:
                yield from lam()
            bks = []
            for j in range(2):
                i, bk, fr = sring.get()
                mm(bk[:, 0:256], Q[:, j, 128:256], Q[:, 2 + j, :], dq_t[h], *fr, inc=False)
                tt = mm(bk[:, 256:384], Q[:, j, 0:128], Q[:, 2 + j, 0:128])
                bks.append((i, bk))
            dq_free[h % 2] = tt
            yield
            bias = DBI[:, 256 * h:256 * h + 256]
            for j in range(2):
                i, bk = bks[j]
                stt(DS[j][:, 0:256], bk[:, 0:256], 128.0 ** -0.5, bias, MUL, ADD, tt, t_db[0])
                t = stt(DS[j][:, 256:384], bk[:, 256:384], 128.0 ** -0.5, bias[:, 128:256], MUL, ADD)
                sring.free(i, t)
                rmax_(DST[:, 2 * j:2 * j + 1], DS[j][:, 0:256])
                rmax_(DST[:, 2 * j + 1:2 * j + 2], DS[j][:, 256:384])
            tv = ts_(DST[:, 4:8], DST[:, 0:4], -1.0, None, MUL, None)
            yield
            for j in range(2):
                act(DS[j][:, 0:256], DS[j][:, 0:256], ACT.Exp, tv, bias=DST[:, 4 + 2 * j:5 + 2 * j],
                    accum=DST[:, 8 + 2 * j:9 + 2 * j])
                ta = act(DS[j][:, 256:384], DS[j][:, 256:384], ACT.Exp, bias=DST[:, 5 + 2 * j:6 + 2 * j],
                         accum=DST[:, 9 + 2 * j:10 + 2 * j])
            yield
            recip_(DST[:, 12:16], DST[:, 8:12], ta)
            ts_(DST[:, 14:16], DST[:, 14:16], LQ[:, 4:5], None, MUL, None)
            for b, c in ((0, slice(0, 256)), (1, slice(256, 384))):
                ts_(DS[0][:, c], DS[0][:, c], DST[:, 12 + b:13 + b], None, MUL, None)
                tv = stt(DS[0][:, c], DS[1][:, c], DST[:, 14 + b:15 + b], DS[0][:, c], MUL, ADD)
            yield
            i, bk, fr = sring.get()
            transpose(bk[:, 0:128], DS[0][:, 256:384], ident, tv, *fr, inc=False)
            transpose(bk[:, 128:256], DS[0][:, 0:128], ident, inc=False)
            tt = transpose(bk[:, 256:384], DS[0][:, 128:256], ident)
            V.wait(tt)
            yield
            ta = act(WT, bk[:, 0:384], ACT.Copy, tt)
            sring.free(i, ta)
            yield
            i, bk, fr = sring.get()
            for d in range(2):
                c = 256 * (h % 2) + 128 * d
                mm(bk[:, 256 * d:256 * d + 256], VT[:, 0, c:c + 128], WT[:, 0:256], ta, dv_t[h // 2], *fr,
                   start=True, stop=False, inc=False)
                tt = mm(bk[:, 256 * d + 128:256 * d + 256], VT[:, 1, c:c + 128], WT[:, 256:384],
                        start=False, stop=True)
            dv_free[(h // 2) % 2] = tt
            A.wait(tt)
            yield
            yield from rms_tail(i, bk, tt, lambda j: DNW[:, j:j + 1], DOS, OBD, h, None)

        for h in range(4):
            if h % 2 == 0:
                gemm_t("w_in_2", 6160 + 512 * (h // 2), 16, xn, dv_epi(h // 2))
            for j in range(2):
                gemm("w_in_2", 4112 + 256 * h + 128 * j, 16, xn, dq_epi(h, j))
            for j in range(2):
                gemm("w_in_2", 5136 + 256 * h + 128 * j, 16, xn, dq_epi(h, 2 + j))
            flush()
            if prev:
                finish(prev)
                prev = None
            finish(cur)
            if h == 0:
                for e_ in (V, A):
                    e_.wait(T.last, V.last, A.last)
                t_db.append(load(DBI, args["dbias"], T.last))
            cur = start(diff(h))

        SG = DQ[0]
        VB = v3(DVT[0].rearrange("p a b -> p (a b)"), 4)
        V.wait(dq_free[0], dv_free[0])
        sg_t, ms_t = {}, []

        def g12_epi(n, c):
            s = 2 * (n % 2)

            def f(bank, tt):
                tv = evac_rs(SG[:, s + c, :], bank, tt)
                if c == 1:
                    sg_t[n] = act(SG[:, s:s + 2, :], SG[:, s:s + 2, :], ACT.Sigmoid, tv)
                return (tv,)
            return f

        def y12_epi(n, c):
            s = 2 * (n % 2)

            def f(bank, tt):
                if c == 0:
                    return (tt_(PSM[:, n, :], bank[:, 0:256], SG[:, s, :], MUL, tt, sg_t[n]),)
                tv = tt_(VB[:, n % 2, :], bank[:, 0:256], SG[:, s + 1, :], MUL, tt)
                tt_(PSM[:, n, :], PSM[:, n, :], VB[:, n % 2, :], ADD)
                return (tv,)
            return f

        for n in range(16):
            for c in range(2):
                gemm("w_in_2", 7184 + 2048 * (c + 1) + 128 * n, 16, xn, g12_epi(n, c))
            if n == 0:
                flush()
                finish(cur)
                T.wait(V.last)
                V.wait(A.last, T.last)
            gemm("gla_w_br_2", 128 * n, 8, lambda k: GOS[:, k, :], y12_epi(n, 0))
            gemm("diff_w_br_2", 128 * n, 8, lambda k: DOS[:, k, :], y12_epi(n, 1))
        flush()
        t_read = T.last
        A.wait(t_read, V.last)
        V.wait(t_read, A.last)

        def g0_epi(n):
            s = 2 * (n % 2)

            def f(bank, tt):
                tv = evac_rs(SG[:, s, :], bank, tt)
                act(SG[:, s, :], SG[:, s, :], ACT.Sigmoid, tv)
                return (tv,)
            return f

        def gate_epi(n):
            s = 2 * (n % 2)

            def f(bank, tt):
                ta = act(SG[:, s + 1, :], bank[:, 0:256], ACT.Sigmoid, tt, sg_t.get(("v", n - 2)))
                sg_t["v", n] = tt_(SG[:, s, :], SG[:, s, :], SG[:, s + 1, :], MUL, ta)
                return (ta,)
            return f

        def val_epi(n):
            s = 2 * (n % 2)

            def f(bank, tt):
                tv = tt_(VB[:, n % 2, :], bank[:, 0:256], SG[:, s, :], MUL, tt)
                t = tt_(VB[:, n % 2, :], VB[:, n % 2, :], PSM[:, n, :], ADD)
                ms_t.append(split(MS[:, n, :], VB[:, n % 2, :], t))
                return (tv,)
            return f

        for n in range(16):
            gemm("w_in_2", 7184 + 128 * n, 16, xn, g0_epi(n))
            if n == 0:
                flush()
                finish(s5g)
                m = Map(nc, XT, end)
                TMP = v3(m("TMP3", 512), 2)
                X = v3(m("X3", 16 * 256), 16)
                t_x = load(X, scratch, V.last, A.last, T.last, G.last)
            gemm("ssm_w_glu_2", 2048 + 128 * n, 8, lambda k: ZS[:, k, :], gate_epi(n), t_zs[0])
            gemm("ssm_w_glu_2", 128 * n, 8, lambda k: ZS[:, k, :], val_epi(n))
        flush()

        def begin3():
            every[0] = 16
            return X, t_x, Norm(X, "norm_ffn", TMP)

        def ms(k):
            T.wait(ms_t[k])
            return MS[:, k, :]
        gring, sring = ring(0, 1, 2, 3), ring(4, 5, 6, 7)
        X, nm, t = out_proj("w_out_2", range(14), [14, 15], ms, begin3)

        nm.end()
        barrier(V, A)
        m = Map(nc, R0, XT)
        HS = v3(m("HS", 43 * 512, F32R), 43)
        UP = v3(m("UP", 2 * 258), 2)
        VG = [v3(m(f"VG{i}", 512), 2) for i in range(2)]
        memset_(UP[:, :, 0:2], 0.0, E=V)
        hs_t, vg_free = {}, [None, None]

        def up_epi(i, s):
            vg = VG[i % 2]

            def f(bank, tt):
                tv = evac_rs(UP[:, s, 2:258], bank, tt)
                k = 43 * s + i
                t = conv(vg[:, s, :], UP[:, s, :], lambda t: cv("ffn_w", 86 * t + k), cv("ffn_b", k), 3, tv,
                         vg_free[i % 2])
                if s == 1:
                    ta = act(vg[:, 1, :], vg[:, 1, :], ACT.Silu, t)
                    deferred.append(lambda: product(ta))
                return (tv,)

            def product(ta):
                t = tt_(vg[:, 0, :], vg[:, 0, :], vg[:, 1, :], MUL, ta)
                ta = act(HS[:, i, 0:256], vg[:, 0, :], ACT.Copy, t)
                deferred.append(lambda: rest(ta))

            def rest(ta):
                hs_t[i] = tt_(HS[:, i, 256:512], vg[:, 0, :], HS[:, i, 0:256].bitcast(F32), SUB, ta)
                vg_free[i % 2] = hs_t[i]
            return f
        for i in range(43):
            gemm("ffn_w_up_2", 128 * i, 16, xn, up_epi(i, 0))
            gemm("ffn_w_up_2", 5504 + 128 * i, 16, xn, up_epi(i, 1))
        flush()
        SUMB = sring.get()
        T.wait(*SUMB[2])
        def down_epi(n):
            def f(bank, tt):
                t = tt_(X[:, n, :], X[:, n, :], bank[:, 0:256], ADD, tt)
                square(n, RSB, 0, X[:, n, :], t)
                return (t,)
            return f

        def hs(k):
            T.wait(hs_t[k])
            return HS[:, k, :]
        for n in range(16):
            gemm("ffn_w_down_2", 128 * n, 43, hs, down_epi(n))
        flush()
        mm(SUMB[1][:, 0:256], ones, RSB, G.last)
        ta = rs_from(RSB, SUMB[1][:, 0:256], 2048, T.last, V.last)
        for k in range(16):
            t = stt(X[:, k, :], X[:, k, :], cv("norm_final", k), RSB, MUL, MUL, ta)
            if k % 4 == 3:
                S.op(lambda e, k=k: e.dma_start(out[:, k - 3:k + 1, :], X[:, k - 3:k + 1, :]).then_inc(out_sem, 16),
                     t, inc=False, chain=False)
        S.wait((out_sem, 64))
        S.wait((st_sem, stores[0]))
        assert blk[0] == NBLOCKS, (blk[0], NBLOCKS)

        block = ctx.enter_context(nc.Block())

        @block.sync
        def _(e):
            S.run(e)

        @block.scalar
        def _(e):
            A.run(e)

        @block.vector
        def _(e):
            V.run(e)

        @block.gpsimd
        def _(e):
            G.run(e)

        @block.tensor
        def _(e):
            T.run(e)
    return order



def cols(a, n):
    return np.ascontiguousarray(np.asarray(a, np.float32).reshape(-1, 128).T)


def vectors(I):
    v = np.zeros((128, NVEC), np.float32)

    def put(name, a):
        v[:a.shape[0], VOFF[name]:VOFF[name] + a.shape[1]] = a

    for name, key in [("e_norm", "e_norm"), ("conv_l_w", "e_conv_l_w"), ("conv_l_b", "e_conv_l_b"),
                      ("lru_ba", "e_lru_ba"), ("lru_bx", "e_lru_bx"), ("lru_lam", "e_lru_lam"),
                      ("conv_m_w", "e_conv_m_w"), ("conv_m_b", "e_conv_m_b"), ("m_norm", "e_m_norm"),
                      ("o_norm", "o_norm"), ("o_conv_w", "o_conv_w"), ("o_conv_b", "o_conv_b"),
                      ("gnorm", "o_gnorm"), ("final_norm", "final_norm"), ("norm_mix", "norm_mix_w_2"),
                      ("ssm_d", "ssm_d_2"), ("gla_b", "gla_b_gate_2"), ("gla_norm", "gla_norm_w_2"),
                      ("diff_norm", "diff_norm_w_2"), ("norm_ffn", "norm_ffn_w_2"),
                      ("ffn_w", "ffn_conv_w_2"), ("ffn_b", "ffn_conv_b_2"), ("norm_final", "norm_final_w_2")]:
        put(name, cols(I[key], 0))
    b = I["e_b_if"][0]
    v[0:4, VOFF["b_if"]] = b[0:4]
    v[32:36, VOFF["b_if"]] = b[4:8]
    put("dt_bias", I["o_dt_bias"][0].reshape(64, 1))
    put("a_log", I["o_a_log"][0].reshape(64, 1))
    put("d_skip", np.repeat(I["o_d_skip"][0].reshape(32, 2), 64, axis=1).T)
    put("a_re", I["ssm_a_re_2"][0].reshape(32, 128).T)
    put("a_im", I["ssm_a_im_2"][0].reshape(32, 128).T)
    put("log_dt", np.repeat(I["ssm_log_dt_2"][0].reshape(32, 2), 64, axis=1).T)
    put("diff_lam", np.stack([I[f"diff_lam_{n}_2"][0] for n in ("q1", "k1", "q2", "k2")], axis=1))
    return v


def shapes():
    c = np.zeros((128, NSHP), np.float32)
    p = np.arange(128)[:, None]
    j = np.arange(256)[None, :]

    def put(name, a):
        c[:, SOFF[name]:SOFF[name] + a.shape[1]] = a

    put("ident", np.eye(128, dtype=np.float32))
    put("ones", np.ones((128, 128), np.float32))
    m = np.where(p <= j, 0.0, NEG).astype(np.float32)
    put("mask", np.concatenate([m, m[:, 0:128]], axis=1))
    q = np.arange(128)[None, :]
    put("gmask", ((p <= q) & (p // 32 == q // 32)).astype(np.float32))
    put("creset", np.broadcast_to((j % 32 != 0).astype(np.float32), (128, 256)))
    put("cmask", (p // 32 == np.arange(8)[None, :] % 4).astype(np.float32))
    rel = (128 + p - j).astype(np.float32)
    d = [np.where(rel >= 0, -(2.0 ** (-8.0 * (h + 1) / 4)) * rel, NEG) for h in range(4)]
    return c, np.concatenate(d, axis=1).astype(np.float32)


def pack_weights(I, order):
    w = np.zeros((NUNITS, 128, UB, 128), np.float32)
    for n, (name, k, c, width) in enumerate(order):
        a = I[name][0]
        if isinstance(c, tuple):
            a, c = a[c[0]], c[1]
        w[n // UB, :, n % UB, :width] = a[128 * k:128 * k + 128, c:c + width]
    return w.reshape(NUNITS, 128, UB * 128)


def host_arrays(I, order):
    I = {k: np.asarray(v) for k, v in I.items()}
    x = np.ascontiguousarray(I["x"][0].T.reshape(16, 128, 256).transpose(1, 0, 2))
    wif = I["e_w_if"][0].reshape(32, 128, 8).transpose(1, 0, 2)
    w_if = np.zeros((128, 32, 36), np.float32)
    w_if[:, :, 0:4] = wif[:, :, 0:4]
    w_if[:, :, 32:36] = wif[:, :, 4:8]
    b = {}
    for n in ("re", "im"):
        s = I[f"ssm_b_{n}_2"][0].reshape(8, 4, 2, 64, 16)
        t = np.zeros((4, 2, 16, 8, 2, 64), np.float32)
        c = np.zeros((2, 64, 32, 2, 16), np.float32)
        g = I[f"ssm_c_{n}_2"][0].reshape(32, 2, 16, 64)
        for i in range(2):
            t[:, i, :, :, i, :] = s[:, :, i].transpose(1, 3, 0, 2)
            c[i, :, :, i, :] = g[:, i].transpose(2, 0, 1)
        b["b_" + n] = t.reshape(128, 8, 128)
        b["c_" + n] = c.reshape(128, 32, 32)
    shp, dbias = shapes()
    return {"x": x, "vec": vectors(I), "shp": shp, "dbias": dbias, "w_if": w_if, "w_gate": I["gla_w_gate_2"][0],
            "w": pack_weights(I, order), **b}


_SHAPES = {"x": (128, 16, 256), "vec": (128, NVEC), "shp": (128, NSHP), "dbias": (128, 1024),
           "w_if": (128, 32, 36), "w_gate": (16, 512), "w": (NUNITS, 128, UB * 128),
           "b_re": (128, 8, 128), "b_im": (128, 8, 128), "c_re": (128, 32, 32), "c_im": (128, 32, 32)}


def program(nc):
    args = {n: nc.dram_tensor(f"in_{n}", s, F32, kind="ExternalInput").ap() for n, s in _SHAPES.items()}
    out = nc.dram_tensor("out_0", (128, 16, 256), F32, kind="ExternalOutput").ap()
    scratch = nc.dram_tensor("scratch_0", (128, 16, 256), F32).ap()
    return build(nc, args, out, scratch)


def kernel(**inputs):
    import concourse.bacc as _bacc
    from concourse.bass_utils import run_bass_kernel_spmd as _run

    nc = _bacc.Bacc("TRN2", target_bir_lowering=False, num_devices=1)
    order = program(nc)
    arrays = {f"in_{n}": np.ascontiguousarray(a) for n, a in host_arrays(inputs, order).items()}
    r = _run(nc, [arrays], core_ids=[0])
    o = r.results[0]["out_0"]
    return np.ascontiguousarray(o.transpose(1, 0, 2).reshape(2048, 256).T)[None]
```
